# Optimizing a Trainium2 kernel written in Bass

```python
import math
import jax, jax.numpy as jnp
from jax import lax
import numpy as np

D_MODEL = 2048
BATCH = 1
SEQ = 256
DEPTH = 1

CHUNK = 64
D_MIX = D_MODEL
NORM_EPS = 1e-6
DSA_WIDTH = D_MIX // 2
DSA_HEAD_DIM = 128
DSA_HEADS = DSA_WIDTH // DSA_HEAD_DIM
IDX_HEADS = 16
IDX_DIM = 64
TOPK_MAX = 256
ROPE_THETA = 10000.0
RWKV_WIDTH = D_MIX - DSA_WIDTH
RWKV_HEAD_DIM = 64
RWKV_HEADS = RWKV_WIDTH // RWKV_HEAD_DIM
DECAY_LORA = 64
AICL_LORA = 64
GATE_LORA = 160
GN_EPS = 64e-5
N_GROUPS = 4
EXPERTS_PER_GROUP = 4
N_EXPERTS = N_GROUPS * EXPERTS_PER_GROUP
TOP_K_IN_GROUP = 2
D_EXPERT = 512
DSA_SPLITS = (DSA_WIDTH, DSA_WIDTH, DSA_WIDTH, IDX_HEADS * IDX_DIM, IDX_DIM, IDX_HEADS)
RWKV_SPLITS = (RWKV_WIDTH, DECAY_LORA, RWKV_WIDTH, RWKV_WIDTH, AICL_LORA, GATE_LORA)
DSA_COLS = sum(DSA_SPLITS)
RWKV_COLS = sum(RWKV_SPLITS)
IN_COLS = DSA_COLS + RWKV_COLS


def split_cols(p, sizes):
    cuts = np.cumsum(sizes)[:-1].tolist()
    return jnp.split(p, cuts, axis=-1)

def rms_norm(x, g, eps=NORM_EPS):
    xf = x.astype(jnp.float32)
    y = xf * lax.rsqrt(jnp.mean(xf * xf, axis=-1, keepdims=True) + eps)
    return (y * g.astype(jnp.float32)).astype(x.dtype)

def rope(x, pos):
    d = x.shape[-1]
    half = d // 2
    inv = ROPE_THETA ** (-jnp.arange(half, dtype=jnp.float32) * (2.0 / d))
    ang = pos.astype(jnp.float32)[:, None] * inv[None, :]
    cos = jnp.cos(ang)[None, :, None, :]
    sin = jnp.sin(ang)[None, :, None, :]
    xf = x.astype(jnp.float32)
    x1, x2 = xf[..., :half], xf[..., half:]
    out = jnp.concatenate([x1 * cos - x2 * sin, x2 * cos + x1 * sin], axis=-1)
    return out.astype(x.dtype)

def token_shift_mix(p, mu):
    prev = jnp.pad(p, ((0, 0), (1, 0), (0, 0)))[:, :-1]
    return p + (prev - p) * mu

def dsa_mixer(q, k, v, q_idx, k_idx, w_idx, q_gain, k_gain):
    B, S = q.shape[0], q.shape[1]
    f32 = jnp.float32
    pos = jnp.arange(S)
    q = rope(rms_norm(q.reshape(B, S, DSA_HEADS, DSA_HEAD_DIM), q_gain), pos)
    k = rope(rms_norm(k.reshape(B, S, DSA_HEADS, DSA_HEAD_DIM), k_gain), pos)
    v = v.reshape(B, S, DSA_HEADS, DSA_HEAD_DIM)
    q_idx = rope(q_idx.reshape(B, S, IDX_HEADS, IDX_DIM), pos)
    k_idx = rope(k_idx[:, :, None, :], pos)[:, :, 0]
    w_idx = w_idx.astype(f32) * (IDX_HEADS ** -0.5 * IDX_DIM ** -0.5)
    top_k = min(TOPK_MAX, S // 4)
    n_blocks = S // CHUNK
    key_pos = jnp.arange(S)
    scale = DSA_HEAD_DIM ** -0.5

    def block(i):
        start = i * CHUNK
        qi_idx = lax.dynamic_slice_in_dim(q_idx, start, CHUNK, axis=1)
        wi = lax.dynamic_slice_in_dim(w_idx, start, CHUNK, axis=1)
        qi = lax.dynamic_slice_in_dim(q, start, CHUNK, axis=1)
        iscore = jnp.einsum('bqhd,bsd->bqhs', qi_idx, k_idx, preferred_element_type=f32)
        iscore = jnp.einsum('bqhs,bqh->bqs', jax.nn.relu(iscore), wi)
        admissible = key_pos < start + CHUNK
        iscore = jnp.where(admissible[None, None, :], iscore, -jnp.inf)
        sel_score, sel = lax.top_k(iscore, top_k)
        valid = jnp.isfinite(sel_score)
        k_sel = jax.vmap(lambda kb, ib: kb[ib])(k, sel)
        v_sel = jax.vmap(lambda vb, ib: vb[ib])(v, sel)
        logits = jnp.einsum('bqhd,bqkhd->bhqk', qi, k_sel, preferred_element_type=f32) * scale
        logits = jnp.where(valid[:, None, :, :], logits, -jnp.inf)
        probs = jax.nn.softmax(logits, axis=-1)
        return jnp.einsum('bhqk,bqkhd->bqhd', probs.astype(v.dtype), v_sel)

    out = lax.map(block, jnp.arange(n_blocks))
    return out.transpose(1, 0, 2, 3, 4).reshape(B, S, DSA_WIDTH)

def rwkv7_mixer(r, d_w, k, v, d_a, d_g, w0, w_decay_up, a0, w_aicl_up, w_gate_lora_up,
                k_k, k_a, r_k, ln_x_w, ln_x_b, out_dtype):
    B, S = r.shape[0], r.shape[1]
    H, N = RWKV_HEADS, RWKV_HEAD_DIM
    f32 = jnp.float32
    w = -jax.nn.softplus(-(w0 + jnp.tanh(d_w) @ w_decay_up)) - 0.5
    decay = jnp.exp(-jnp.exp(w.astype(f32)))
    a = jax.nn.sigmoid((a0 + d_a @ w_aicl_up).astype(f32))
    g = (jax.nn.sigmoid(d_g) @ w_gate_lora_up).astype(f32)
    heads = lambda t: t.astype(f32).reshape(B, S, H, N)
    kk = heads(k * k_k)
    kk = kk / jnp.maximum(jnp.sqrt(jnp.sum(kk * kk, axis=-1, keepdims=True)), 1e-12)
    k = k.astype(f32) * (1.0 + (a - 1.0) * k_a.astype(f32))
    r_h, k_h, v_h, w_h, a_h = heads(r), heads(k), heads(v), heads(decay), heads(a)
    b_h = kk * a_h

    def step(state, inp):
        r_t, w_t, k_t, v_t, kk_t, b_t = inp
        sa = jnp.einsum('bhvk,bhk->bhv', state, -kk_t)
        state = (state * w_t[:, :, None, :] + sa[..., None] * b_t[:, :, None, :]
                 + v_t[..., None] * k_t[:, :, None, :])
        return state, jnp.einsum('bhvk,bhk->bhv', state, r_t)

    xs = tuple(t.transpose(1, 0, 2, 3) for t in (r_h, w_h, k_h, v_h, kk, b_h))
    _, ys = lax.scan(step, jnp.zeros((B, H, N, N), f32), xs)
    y = ys.transpose(1, 0, 2, 3)
    mu = jnp.mean(y, axis=-1, keepdims=True)
    var = jnp.mean(jnp.square(y - mu), axis=-1, keepdims=True)
    y = ((y - mu) * lax.rsqrt(var + GN_EPS)).reshape(B, S, RWKV_WIDTH)
    y = y * ln_x_w.astype(f32) + ln_x_b.astype(f32)
    bonus = jnp.sum(r_h * k_h * r_k.astype(f32), axis=-1, keepdims=True) * v_h
    y = (y + bonus.reshape(B, S, RWKV_WIDTH)) * g
    return y.astype(out_dtype)

def hier_moe(h, w_route_group, b_route_group, w_route_expert, b_route_expert,
             w_e_gate, w_e_up, w_e_down):
    B, S, D = h.shape
    f32 = jnp.float32
    t = h.reshape(B * S, D)
    grp_prob = jax.nn.softmax((t @ w_route_group).astype(f32) + b_route_group.astype(f32), axis=-1)
    p_grp, g_sel = lax.top_k(grp_prob, 1)
    exp_logits = ((t @ w_route_expert).astype(f32) + b_route_expert.astype(f32))
    exp_logits = exp_logits.reshape(-1, N_GROUPS, EXPERTS_PER_GROUP)
    exp_logits = jnp.take_along_axis(exp_logits, g_sel[:, :, None], axis=1)[:, 0]
    p_exp, e_sel = lax.top_k(jax.nn.softmax(exp_logits, axis=-1), TOP_K_IN_GROUP)
    p_exp = p_exp / jnp.sum(p_exp, axis=-1, keepdims=True)
    gate_w = p_grp * p_exp
    expert_id = g_sel * EXPERTS_PER_GROUP + e_sel
    combine = jnp.sum(jax.nn.one_hot(expert_id, N_EXPERTS, dtype=f32) * gate_w[..., None], axis=1)
    y = jnp.zeros((B * S, D), f32)
    for e in range(N_EXPERTS):
        he = jax.nn.silu(t @ w_e_gate[e]) * (t @ w_e_up[e])
        y = y + combine[:, e:e + 1] * (he @ w_e_down[e]).astype(f32)
    return y.reshape(B, S, D).astype(h.dtype)

def first_inputs(seed: int = 0) -> dict:
    key = jax.random.key(seed)
    ks = jax.random.split(key, 32)
    f32 = jnp.float32
    nrm = lambda k, shape, s: jax.random.normal(k, shape, f32) * s
    L, D = DEPTH, D_MODEL
    return {
        'x': jax.random.normal(ks[0], (BATCH, SEQ, D), f32),
        'g_mix': 1.0 + nrm(ks[1], (L, D), 0.02),
        'w_in': nrm(ks[2], (L, D, IN_COLS), D ** -0.5),
        'rwkv_shift_mix': jax.random.uniform(ks[3], (L, RWKV_COLS), f32),
        'q_gain': 1.0 + nrm(ks[4], (L, DSA_HEAD_DIM), 0.02),
        'k_gain': 1.0 + nrm(ks[5], (L, DSA_HEAD_DIM), 0.02),
        'w0': jax.random.uniform(ks[6], (L, RWKV_WIDTH), f32, -6.0, -1.0),
        'w_decay_up': nrm(ks[7], (L, DECAY_LORA, RWKV_WIDTH), 0.1),
        'a0': nrm(ks[8], (L, RWKV_WIDTH), 0.1),
        'w_aicl_up': nrm(ks[9], (L, AICL_LORA, RWKV_WIDTH), 0.5 * AICL_LORA ** -0.5),
        'w_gate_lora_up': nrm(ks[10], (L, GATE_LORA, RWKV_WIDTH), GATE_LORA ** -0.5),
        'k_k': 0.85 + nrm(ks[11], (L, RWKV_WIDTH), 0.02),
        'k_a': 1.0 + nrm(ks[12], (L, RWKV_WIDTH), 0.02),
        'r_k': nrm(ks[13], (L, RWKV_HEADS, RWKV_HEAD_DIM), 0.1),
        'ln_x_w': 1.0 + nrm(ks[14], (L, RWKV_WIDTH), 0.02),
        'ln_x_b': nrm(ks[15], (L, RWKV_WIDTH), 0.01),
        'w_out': nrm(ks[16], (L, D_MIX, D), D_MIX ** -0.5),
        'g_ffn': 1.0 + nrm(ks[17], (L, D), 0.02),
        'w_route_group': nrm(ks[18], (L, D, N_GROUPS), D ** -0.5),
        'b_route_group': nrm(ks[19], (L, N_GROUPS), 0.01),
        'w_route_expert': nrm(ks[20], (L, D, N_EXPERTS), D ** -0.5),
        'b_route_expert': nrm(ks[21], (L, N_EXPERTS), 0.01),
        'w_e_gate': nrm(ks[22], (L, N_EXPERTS, D, D_EXPERT), D ** -0.5),
        'w_e_up': nrm(ks[23], (L, N_EXPERTS, D, D_EXPERT), D ** -0.5),
        'w_e_down': nrm(ks[24], (L, N_EXPERTS, D_EXPERT, D), D_EXPERT ** -0.5),
    }

def first_block(x, g_mix, w_in, rwkv_shift_mix, q_gain, k_gain, w0, w_decay_up, a0, w_aicl_up,
              w_gate_lora_up, k_k, k_a, r_k, ln_x_w, ln_x_b, w_out, g_ffn, w_route_group,
              b_route_group, w_route_expert, b_route_expert, w_e_gate, w_e_up, w_e_down):
    for l in range(DEPTH):
        h = rms_norm(x, g_mix[l])
        proj = h @ w_in[l]
        p_dsa, p_rwkv = proj[..., :DSA_COLS], proj[..., DSA_COLS:]
        q, k, v, q_idx, k_idx, w_idx = split_cols(p_dsa, DSA_SPLITS)
        y_dsa = dsa_mixer(q, k, v, q_idx, k_idx, w_idx, q_gain[l], k_gain[l])
        p_rwkv = token_shift_mix(p_rwkv, rwkv_shift_mix[l])
        r, d_w, kr, vr, d_a, d_g = split_cols(p_rwkv, RWKV_SPLITS)
        y_rwkv = rwkv7_mixer(r, d_w, kr, vr, d_a, d_g, w0[l], w_decay_up[l], a0[l], w_aicl_up[l],
                             w_gate_lora_up[l], k_k[l], k_a[l], r_k[l], ln_x_w[l], ln_x_b[l],
                             x.dtype)
        x = x + jnp.concatenate([y_dsa.astype(x.dtype), y_rwkv], axis=-1) @ w_out[l]
        x = x + hier_moe(rms_norm(x, g_ffn[l]), w_route_group[l], b_route_group[l],
                         w_route_expert[l], b_route_expert[l], w_e_gate[l], w_e_up[l],
                         w_e_down[l])
    return x


DEPTH_2 = 2

HEAD_DIM = 128
EPS = 1e-6
DN_QK_HEADS = 8
DN_V_HEADS = 16
DN_DK = 128
DN_DV = 128
DN_CONV = 4
DN_CHUNK = 64
SW_HEADS = 8
SW_PATTERNS = ((128, 1), (512, 4), (2048, 16))
SW_GROUPS = 3
SW_BLOCK = 128
ROPE_THETA_2 = 500000.0
ROPE_DIM = HEAD_DIM // 4
SC_WIDTH = 3072
SC_CONV = 3

A_Q = DN_QK_HEADS * DN_DK
A_K = DN_QK_HEADS * DN_DK
A_V = DN_V_HEADS * DN_DV
A_Z = A_V
B_Q = SW_GROUPS * SW_HEADS * HEAD_DIM
B_K = SW_HEADS * HEAD_DIM
B_V = SW_HEADS * HEAD_DIM
B_Z = B_V
HYB_IN = A_Q + A_K + A_V + A_Z + 2 * DN_V_HEADS + B_Q + B_K + B_V + B_Z
HYB_MIX = A_V + B_V
N_EVEN = (DEPTH_2 + 1) // 2
N_ODD = DEPTH_2 // 2


def rmsnorm(x, w):
    xf = x.astype(jnp.float32)
    y = xf * lax.rsqrt(jnp.mean(xf * xf, axis=-1, keepdims=True) + EPS)
    return (y * w.astype(jnp.float32)).astype(x.dtype)

def causal_depthwise_conv(x, w):
    k = w.shape[1]
    rhs = jnp.transpose(w)[:, None, :].astype(x.dtype)
    return lax.conv_general_dilated(x, rhs, window_strides=(1,), padding=[(k - 1, 0)],
                                    dimension_numbers=('NWC', 'WIO', 'NWC'),
                                    feature_group_count=x.shape[-1])

def partial_rope(x, pos):
    half = ROPE_DIM // 2
    inv = jnp.power(jnp.float32(ROPE_THETA_2), -jnp.arange(half, dtype=jnp.float32) * 2.0 / ROPE_DIM)
    ang = pos.astype(jnp.float32)[:, None] * inv[None, :]
    cos = jnp.cos(ang)[None, :, None, :]
    sin = jnp.sin(ang)[None, :, None, :]
    x1 = x[..., :half]
    x2 = x[..., half:ROPE_DIM]
    return jnp.concatenate([x1 * cos - x2 * sin, x2 * cos + x1 * sin, x[..., ROPE_DIM:]], axis=-1)

def l2norm(x):
    return x * lax.rsqrt(jnp.sum(x * x, axis=-1, keepdims=True) + EPS)

def gated_delta_chunked(q, k, v, beta, g):
    b, s, h, dk = q.shape
    dv = v.shape[-1]
    n = s // DN_CHUNK
    c = DN_CHUNK

    def chunks(t):
        return t.reshape(b, n, c, h, t.shape[-1]).transpose(0, 1, 3, 2, 4)

    q, k, v = chunks(q), chunks(k), chunks(v)
    beta = beta.reshape(b, n, c, h).transpose(0, 1, 3, 2)
    g = jnp.cumsum(g.reshape(b, n, c, h).transpose(0, 1, 3, 2), axis=-1)
    idx = jnp.arange(c)
    causal = idx[:, None] >= idx[None, :]
    strict = idx[:, None] > idx[None, :]
    diff = g[..., :, None] - g[..., None, :]
    decay = jnp.exp(jnp.where(causal, diff, -jnp.inf))
    kk = jnp.einsum('bnhik,bnhjk->bnhij', k, k)
    a_strict = jnp.where(strict, beta[..., :, None] * kk * decay, 0.0)
    rhs = jnp.concatenate([v * beta[..., None], k * (beta * jnp.exp(g))[..., None]], axis=-1)
    sol = lax.linalg.triangular_solve(a_strict, rhs, left_side=True, lower=True, unit_diagonal=True)
    u = sol[..., :dv]
    w = sol[..., dv:]
    qk = jnp.einsum('bnhik,bnhjk->bnhij', q, k) * decay

    def step(state, inp):
        q_c, k_c, u_c, w_c, g_c, qk_c = inp
        v_new = u_c - jnp.einsum('bhck,bhkv->bhcv', w_c, state)
        o = jnp.einsum('bhck,bhkv->bhcv', q_c * jnp.exp(g_c)[..., None], state) + \
            jnp.einsum('bhij,bhjv->bhiv', qk_c, v_new)
        g_last = g_c[..., -1]
        state = state * jnp.exp(g_last)[..., None, None] + jnp.einsum(
            'bhck,bhcv->bhkv', k_c * jnp.exp(g_last[..., None] - g_c)[..., None], v_new)
        return state, o

    xs = tuple(jnp.moveaxis(t, 1, 0) for t in (q, k, u, w, g, qk))
    state0 = jnp.zeros((b, h, dk, dv), jnp.float32)
    _, o = lax.scan(step, state0, xs)
    return o.transpose(1, 0, 3, 2, 4).reshape(b, s, h, dv)

def dilated_window_group(q, k, v, dil):
    b, s, h, dh = q.shape
    wb = SW_BLOCK
    ln = s // dil
    nb = -(-ln // wb)
    lp = nb * wb

    def strided(t):
        t = t.reshape(b, ln, dil, h, dh).transpose(0, 2, 3, 1, 4)
        t = jnp.pad(t, ((0, 0), (0, 0), (0, 0), (0, lp - ln), (0, 0)))
        return t.reshape(b, dil, h, nb, wb, dh)

    def with_prev(t):
        prev = jnp.concatenate([jnp.zeros_like(t[:, :, :, :1]), t[:, :, :, :-1]], axis=3)
        return jnp.concatenate([prev, t], axis=4)

    qs = strided(q)
    kb = with_prev(strided(k))
    vb = with_prev(strided(v))
    sc = jnp.einsum('brhnqc,brhnkc->brhnqk', qs, kb) * (dh ** -0.5)
    i = jnp.arange(wb)[:, None]
    j = jnp.arange(2 * wb)[None, :]
    dist = i + wb - j
    blk = jnp.arange(nb)[:, None, None]
    valid = (dist >= 0) & (dist <= wb) & (blk * wb - wb + j >= 0)
    sc = jnp.where(valid, sc, -jnp.inf)
    m = jnp.max(sc, axis=-1, keepdims=True)
    p = jnp.exp(sc - m)
    den = jnp.sum(p, axis=-1)
    num = jnp.einsum('brhnqk,brhnkc->brhnqc', p, vb)

    def unstride(t):
        rest = t.shape[5:]
        t = t.reshape((b, dil, h, lp) + rest)[:, :, :, :ln]
        return jnp.moveaxis(t, 3, 1).reshape((b, s, h) + rest)

    return unstride(num), unstride(den), unstride(m[..., 0])

def dilated_attention(q, k, v):
    nums, dens, maxs = [], [], []
    for gi, (window, dil) in enumerate(SW_PATTERNS):
        n_, d_, m_ = dilated_window_group(q[:, :, gi], k, v, dil)
        nums.append(n_)
        dens.append(d_)
        maxs.append(m_)
    mx = jnp.max(jnp.stack(maxs), axis=0)
    wts = [jnp.exp(m_ - mx) for m_ in maxs]
    num = sum(w_[..., None] * n_ for w_, n_ in zip(wts, nums))
    den = sum(w_ * d_ for w_, d_ in zip(wts, dens))
    return num / den[..., None]

def hybrid_layer(h, w_in, conv_w, a_log, dt_bias, dn_norm_w, w_out, pos):
    b, s, _ = h.shape
    f32 = jnp.float32
    proj = h @ w_in
    sizes = [A_Q, A_K, A_V, A_Z, DN_V_HEADS, DN_V_HEADS, B_Q, B_K, B_V, B_Z]
    offs = []
    acc = 0
    for sz in sizes[:-1]:
        acc += sz
        offs.append(acc)
    aq, ak, av, az, ab, aa, bq, bk, bv, bz = jnp.split(proj, offs, axis=-1)

    qkv = jax.nn.silu(causal_depthwise_conv(jnp.concatenate([aq, ak, av], axis=-1), conv_w)).astype(f32)
    q_a = l2norm(qkv[..., :A_Q].reshape(b, s, DN_QK_HEADS, DN_DK)) * (DN_DK ** -0.5)
    k_a = l2norm(qkv[..., A_Q:A_Q + A_K].reshape(b, s, DN_QK_HEADS, DN_DK))
    v_a = qkv[..., A_Q + A_K:].reshape(b, s, DN_V_HEADS, DN_DV)
    rep = DN_V_HEADS // DN_QK_HEADS
    q_a = jnp.repeat(q_a, rep, axis=2)
    k_a = jnp.repeat(k_a, rep, axis=2)
    beta = jax.nn.sigmoid(ab.astype(f32))
    g = -jnp.exp(a_log.astype(f32)) * jax.nn.softplus(aa.astype(f32) + dt_bias.astype(f32))
    o_a = gated_delta_chunked(q_a, k_a, v_a, beta, g)
    o_a = o_a * lax.rsqrt(jnp.mean(o_a * o_a, axis=-1, keepdims=True) + EPS) * dn_norm_w.astype(f32)
    y_a = (o_a.reshape(b, s, A_V) * jax.nn.silu(az.astype(f32))).astype(h.dtype)

    q_b = partial_rope(bq.astype(f32).reshape(b, s, SW_GROUPS * SW_HEADS, HEAD_DIM), pos)
    q_b = q_b.reshape(b, s, SW_GROUPS, SW_HEADS, HEAD_DIM)
    k_b = partial_rope(bk.astype(f32).reshape(b, s, SW_HEADS, HEAD_DIM), pos)
    v_b = bv.astype(f32).reshape(b, s, SW_HEADS, HEAD_DIM)
    o_b = dilated_attention(q_b, k_b, v_b)
    y_b = (o_b.reshape(b, s, B_V) * jax.nn.silu(bz.astype(f32))).astype(h.dtype)

    return jnp.concatenate([y_a, y_b], axis=-1) @ w_out

def shortconv_layer(h, w_in, conv_w, w_out):
    gate_b, gate_c, u, z = jnp.split(h @ w_in, 4, axis=-1)
    y = gate_b * causal_depthwise_conv(gate_c * u, conv_w)
    return (y * jax.nn.silu(z)) @ w_out

def second_inputs(seed: int = 0) -> dict:
    key = jax.random.key(seed)
    ks = jax.random.split(key, 14)
    f32 = jnp.float32

    def nrm(k, shape, scale):
        return jax.random.normal(k, shape, f32) * scale

    x = nrm(ks[0], (BATCH, SEQ, D_MODEL), 1.0)
    norm_w = 1.0 + nrm(ks[1], (DEPTH_2, D_MODEL), 0.05)
    hyb_w_in = nrm(ks[2], (N_EVEN, D_MODEL, HYB_IN), D_MODEL ** -0.5)
    dn_conv_w = nrm(ks[3], (N_EVEN, A_Q + A_K + A_V, DN_CONV), DN_CONV ** -0.5)
    dn_a_log = jnp.log(jax.random.uniform(ks[4], (N_EVEN, DN_V_HEADS), f32, 1.0, 16.0))
    dt = jnp.exp(jax.random.uniform(ks[5], (N_EVEN, DN_V_HEADS), f32, jnp.log(1e-3), jnp.log(1e-1)))
    dn_dt_bias = dt + jnp.log(-jnp.expm1(-dt))
    dn_norm_w = 1.0 + nrm(ks[6], (N_EVEN, DN_DV), 0.05)
    hyb_w_out = nrm(ks[7], (N_EVEN, HYB_MIX, D_MODEL), HYB_MIX ** -0.5)
    sc_w_in = nrm(ks[8], (N_ODD, D_MODEL, 4 * SC_WIDTH), D_MODEL ** -0.5)
    sc_conv_w = nrm(ks[9], (N_ODD, SC_WIDTH, SC_CONV), SC_CONV ** -0.5)
    sc_w_out = nrm(ks[10], (N_ODD, SC_WIDTH, D_MODEL), SC_WIDTH ** -0.5)
    final_norm_w = 1.0 + nrm(ks[11], (D_MODEL,), 0.05)
    return {"x": x, "norm_w": norm_w, "hyb_w_in": hyb_w_in, "dn_conv_w": dn_conv_w,
            "dn_a_log": dn_a_log, "dn_dt_bias": dn_dt_bias, "dn_norm_w": dn_norm_w,
            "hyb_w_out": hyb_w_out, "sc_w_in": sc_w_in, "sc_conv_w": sc_conv_w,
            "sc_w_out": sc_w_out, "final_norm_w": final_norm_w}

def second_block(x, norm_w, hyb_w_in, dn_conv_w, dn_a_log, dn_dt_bias, dn_norm_w, hyb_w_out,
              sc_w_in, sc_conv_w, sc_w_out, final_norm_w):
    pos = jnp.arange(x.shape[1], dtype=jnp.int32)
    h = x
    for layer in range(DEPTH_2):
        hn = rmsnorm(h, norm_w[layer])
        li = layer // 2
        if layer % 2 == 0:
            h = h + hybrid_layer(hn, hyb_w_in[li], dn_conv_w[li], dn_a_log[li], dn_dt_bias[li],
                                 dn_norm_w[li], hyb_w_out[li], pos)
        else:
            h = h + shortconv_layer(hn, sc_w_in[li], sc_conv_w[li], sc_w_out[li])
    return rmsnorm(h, final_norm_w)


def setup_inputs(seed=0):
    out = dict(first_inputs(seed))
    for name, value in second_inputs(seed + 1).items():
        if name != "x":
            out[name + "_2"] = value
    return out


def reference(
    x, g_mix, w_in, rwkv_shift_mix, q_gain, k_gain, w0, w_decay_up, a0, w_aicl_up,
    w_gate_lora_up, k_k, k_a, r_k, ln_x_w, ln_x_b, w_out, g_ffn, w_route_group, b_route_group,
    w_route_expert, b_route_expert, w_e_gate, w_e_up, w_e_down, norm_w_2, hyb_w_in_2,
    dn_conv_w_2, dn_a_log_2, dn_dt_bias_2, dn_norm_w_2, hyb_w_out_2, sc_w_in_2, sc_conv_w_2,
    sc_w_out_2, final_norm_w_2,
):
    x = first_block(
        x, g_mix, w_in, rwkv_shift_mix, q_gain, k_gain, w0, w_decay_up, a0, w_aicl_up,
        w_gate_lora_up, k_k, k_a, r_k, ln_x_w, ln_x_b, w_out, g_ffn, w_route_group,
        b_route_group, w_route_expert, b_route_expert, w_e_gate, w_e_up, w_e_down,
    )
    return second_block(
        x, norm_w_2, hyb_w_in_2, dn_conv_w_2, dn_a_log_2, dn_dt_bias_2, dn_norm_w_2,
        hyb_w_out_2, sc_w_in_2, sc_conv_w_2, sc_w_out_2, final_norm_w_2,
    )


_drawn_inputs = setup_inputs


def setup_inputs(seed=0):
    import zlib

    import numpy as np

    out = dict(_drawn_inputs(seed))
    spreads = {}
    factors = {'q_gain': 4.986,
     'k_gain': 6.255,
     'k_k': 21.787,
     'ln_x_w': 12.994,
     'ln_x_b': 27.634,
     'b_route_group': 8.0,
     'b_route_expert': 23.059,
     'g_ffn': 4.313,
     'dn_norm_w_2': 23.272,
     'norm_w_2': 2.985}
    for name, (base, spread) in spreads.items():
        noise = np.random.default_rng([zlib.crc32(name.encode()), seed]).standard_normal(out[name].shape)
        drawn = base * np.exp(spread * noise) if base else spread * noise
        out[name] = __import__('jax').numpy.asarray(drawn.astype(out[name].dtype))
    for name, factor in factors.items():
        out[name] = (out[name] * factor).astype(out[name].dtype)
    return out
```

```python
import numpy as np
import concourse.bass as bass
from concourse import mybir
from concourse.alu_op_type import AluOpType as ALU
from contextlib import ExitStack

F32 = mybir.dt.float32
F32R = mybir.dt.float32r
ACT = mybir.ActivationFunctionType
AX = mybir.AxisListType.X

P = 128
S = 256
D = 2048
KT = D // P
NT = S // P
UNIT = 16
SUB = 8
RING = 3
NEXP, NGRP, EPG, DEXP = 16, 4, 4, 512
DSA_H, IDX_H, RWKV_P, DN_H, SW_H = 8, 16, 8, 8, 8
TOPK = 64
EPS = 1e-6
GN_EPS = 64e-5
NEG, MARK, BIG = -3.0e38, -3.3e38, 1.0e30

U_PRO = 0
U_DSA = U_PRO + 4 + IDX_H // 2
U_RWKV = U_DSA + 3 * DSA_H
U_WOUT = U_RWKV + 3 * RWKV_P
U_MOE = U_WOUT + KT
U_AB = U_MOE + 12 * NEXP
U_DN = U_AB + 1
U_SW = U_DN + 6 * DN_H
U_HOUT = U_SW + 6 * SW_H
U_SC = U_HOUT + 24
U_SOUT = U_SC + 96
N_UNITS = U_SOUT + 24
N_SUBS = 2 * N_UNITS

_VEC = [("g_mix", 16), ("g_ffn", 16), ("norm2", 32), ("final", 16), ("mu", 24), ("mu_dwda", 1), ("mu_dg1", 1),
        ("mu_dg2", 1), ("w0", 8), ("a0", 8), ("k_k", 8), ("k_a", 8), ("r_k", 8), ("lnw", 8), ("lnb", 8),
        ("q_gain", 1), ("k_gain", 1), ("dn_norm", 1), ("dn_conv", 128), ("sc_conv", 72), ("a_log", 1), ("dt_bias", 1)]
VEC = {}
NVEC = 0
for _n, _w in _VEC:
    VEC[_n] = NVEC
    NVEC += _w

_C0 = [("ident", P), ("levels", 7 * P), ("incl", P), ("strict", P)]
_C1 = [("heads", P), ("perm_q", P), ("perm_i", P), ("cos_q", S), ("sin_q", S), ("cos_i", S), ("sin_i", S)]
_C2 = [("perm_w", P), ("cos_w", S), ("sin_w", S), ("bias0", 3 * P), ("bias1", 3 * S)]


def _columns(parts):
    at, out = 0, {}
    for name, width in parts:
        out[name] = (at, width)
        at += width
    return out, at


C0, N0 = _columns(_C0)
C1, N1 = _columns(_C1)
C2, N2 = _columns(_C2)


def program(nc, stream, x_in, vecs_in, c0_in, c1_in, c2_in, lora_in, route_in, rbias_in, out, dbg=None):
    ctx = ExitStack()
    with ctx:
        def sb(name, shape, dt=F32):
            return ctx.enter_context(nc.sbuf_tensor(name, shape, dt))

        sems = {}

        def sem(name):
            if name not in sems:
                sems[name] = ctx.enter_context(nc.semaphore(name))
            return sems[name]

        stage = sb("stage", [P, RING, UNIT * P])
        w_hi = sb("w_hi", [P, RING, SUB * P], F32R)
        w_lo = sb("w_lo", [P, RING, SUB * P], F32R)
        x = sb("x", [P, KT, S])
        h_hi = sb("h_hi", [P, KT, S], F32R)
        h_lo = sb("h_lo", [P, KT, S], F32R)
        y_hi = sb("y_hi", [P, 24, S], F32R)
        y_lo = sb("y_lo", [P, 24, S], F32R)
        vecs = sb("vecs", [P, NVEC])
        c0 = sb("c0", [P, N0])
        c12 = sb("c12", [P, max(N1, N2)])
        ones = sb("ones", [P, P])
        route = sb("route", [P, KT, 20])
        rbias = sb("rbias", [P, 20])
        arena = sb("arena", [P, 11900])

        gp = ctx.enter_context(nc.psum_tensor("gp", [P, 3, 512], F32))
        pm = ctx.enter_context(nc.psum_tensor("pm", [P, 5, 512], F32))

        def con(name):
            for table, t in ((C0, c0), (C1, c12), (C2, c12)):
                if name in table:
                    at, width = table[name]
                    return t[:, at:at + width]

        def vec(name, k=0, n=1):
            return vecs[:, bass.ds(VEC[name] + k, n)] if not isinstance(k, int) else \
                vecs[:, VEC[name] + k:VEC[name] + k + n]

        ident = con("ident")
        levels = con("levels").rearrange("p (l c) -> p l c", l=7)

        def areas(start, parts):
            at, got = start, []
            for shape in parts:
                n = 1
                for d in shape:
                    n *= d
                v = arena[:, at:at + n]
                if len(shape) == 2:
                    v = v.rearrange("p (a b) -> p a b", a=shape[0])
                elif len(shape) == 3:
                    v = v.rearrange("p (a b c) -> p a b c", a=shape[0], b=shape[1])
                got.append(v)
                at += n
            assert at <= 11900, at
            return got, at

        s_load, s_c2 = sem("s_load"), sem("s_c2")
        s_stage = [sem(f"s_stage{k}") for k in range(RING)]
        s_hi, s_lo = sem("s_hi"), sem("s_lo")
        s_sub = sem("s_sub")
        s_evac = [sem(f"s_evac{k}") for k in range(3)]
        s_dv, s_ac = sem("s_dv_chain"), sem("s_ac_chain")
        s_zero = sem("s_zero")
        s_yhi, s_y = sem("s_yhi"), sem("s_y")

        def plus(ev, *more):
            return [a + b for a, b in zip(ev, more)]

        EV_PRO = [0, 0, 0]
        EV_DSA = plus(EV_PRO, 4, 4, 4)
        EV_RWKV = plus(EV_DSA, DSA_H, DSA_H, DSA_H)
        EV_WOUT = plus(EV_RWKV, RWKV_P, RWKV_P, RWKV_P)
        EV_AB = plus(EV_WOUT, 6, 5, 5)
        EV_DN = plus(EV_AB, 1, 0, 0)
        EV_SW = plus(EV_DN, 2 * DN_H, 2 * DN_H, 2 * DN_H)
        EV_HOUT = plus(EV_SW, 2 * SW_H, 2 * SW_H, 2 * SW_H)
        EV_SC = plus(EV_HOUT, 8, 8, 0)
        EV_SOUT = plus(EV_SC, 32, 32, 32)
        EV_END = plus(EV_SOUT, 8, 8, 0)
        Y_DSA, Y_RWKV, Y_DN, Y_SW, Y_SC = 1, 9, 17, 25, 33
        LOADS = 6

        def loop(eng, n, body):
            with eng.Fori(0, n) as i:
                body(i)

        class Chain:

            def __init__(self, eng, s):
                self.eng, self.s, self.base, self.k, self.at = eng, s, 0, 0, None

            def link(self, ins):
                self.k += 1
                ins.then_inc(self.s, 1)
                self.eng.wait_ge(self.s, self.base + self.k if self.at is None else self.at + self.k)

            def loop(self, n, links, body):
                start = self.base + self.k
                with self.eng.Fori(0, n) as i:
                    self.at, self.k = start + links * i, 0
                    body(i)
                    assert self.k == links, self.k
                self.at, self.k, self.base = None, 0, start + links * n

            def turn(self, links, body, i):
                k = self.k
                body(i)
                assert self.k - k == links, self.k - k

        (notsel, tanh_a, sig1, sig2), L1 = areas(0, [(NT, S), (S,), (S,), (S,)])
        (kraw, misc, dwda, dg1, mixd, qraw, t_1, t_2, krope, qrope, relu, isc, wtok, top8), _ = areas(
            L1, [(S,), (S + 1,), (S + 1,), (S + 1,), (S,), (2, S), (S,), (S,), (S,), (2, S), (2, 512), (NT, S), (NT, 16),
                 (NT, 8)])
        (d_raw, d_sq, d_rs, d_qn, d_t1, d_t2, d_qk, d_lg, d_pr, d_pT, d_v, d_nm, d_sum), _ = areas(
            L1, [(3, S), (512,), (512,), (2, S), (2, S), (2, S), (2, S), (NT, S), (NT, S), (NT, S), (NT, P), (NT,), (NT,)])
        (r_raw, r_mix, r_D, r_lw, r_cum, r_P, r_Pi, r_a, r_g, r_sq, r_tmp, r_at, r_bt, r_kt, r_rt, r_tok, r_Aak, r_R,
         r_rhs, r_U, r_S, r_lora, r_negm, r_em, r_sc, r_A, r_X), r_end = areas(
            L1, [(3, S + 1), (3, S), (3, S), (S,), (S,), (S,), (S,), (S,), (S,), (S,), (S,), (S,), (S,), (S,), (S,),
                 (4, P), (4, P), (2, 4, P), (NT, P), (NT, P), (P,), (3 * P,), (NT,), (NT,), (1,), (4, P), (4, P)])
        (r_Y,), r_end = areas(r_end, [(4, P)])
        lw0 = L1 + 3 * (S + 1) + 6 * S
        (r_T, r_al0), _ = areas(lw0, [(4, P), (4, P)])
        (r_al1,), _ = areas(lw0 + 6 * S, [(4, P)])
        r_Al = [r_al0, r_al1]
        (hf, n_rs), _ = areas(0, [(KT, S), (S,)])
        (rl, g1v, g4, gs, gr, w16, w16b, m8, m8b, pg, oneh, es, es2, e4, w4, comb, combT, csel, bce, sg, hef, he2), _ = areas(
            KT * S + S, [(NT, 20), (NT,), (NT, 4), (NT,), (NT,), (NT, 16), (NT, 16), (NT, 8), (NT, 8), (NT,), (NT, 4),
                         (NT, 4), (NT, 4), (NT, 4), (NT, 4), (NT, P), (S,), (S,), (S,), (2, S), (2, S), (2, S)])
        (ab, g_x, g_e, g_s, gb, gtok, nbeta, egt, neg_eg, ea), L2 = areas(
            0, [(S,), (S,), (S,), (S,), (S,), (NT, P), (NT, 16), (NT, 16), (NT, 16), (1,)])
        (n_raw, n_qkv, n_z, n_sq, n_rn, n_v, n_kd, n_gs, n_E1, n_E2, n_A, n_QK, n_X, n_Y, n_r0, n_r1, n_vn, n_S, n_o,
         n_ss, n_or), _ = areas(
            L2, [(4, S + 3), (4, S), (2, S), (512,), (512,), (4, P), (2, P), (2, S), (4, P), (4, P), (4, P), (4, P), (4, P),
                 (4, P), (2, P), (2, P), (4, P), (2, P), (4, P), (4,), (4,)])
        n_at = L2 + 4 * (S + 3) + 6 * S
        (n_al0, n_al1), _ = areas(n_at, [(4, P), (4, P)])
        n_Al = [n_al0, n_al1]
        n_T = n_E1
        n_yf = n_E2[:, :, :].rearrange("p (h c) t -> p h (c t)", h=2)
        (w_raw, w_t1, w_t2, w_qk, w_z, w_v0, w_v, w_l0, w_l1, w_p0, w_p1, w_pT, w_nm, w_sum, w_yf), _ = areas(
            0, [(4, S), (4, S), (4, S), (4, S), (S,), (S,), (NT, P), (3 * P,), (3 * S,), (P,), (S,), (3, P), (NT,), (NT,),
                (S,)])
        (q_b, q_c, q_cu, q_z, q_a), _ = areas(0, [(3, S), (3, S), (3, S + 2), (3, S), (3, S)])

        solve = [sem(f"s_solve_{n}") for n in ("level", "t1", "t1_out", "dy", "dx", "xy")]
        s_al, s_t1, s_t1o, s_dy, s_dx, s_xy = solve

        block = ctx.enter_context(nc.Block())

        @block.sync
        def _(sp):
            for u in range(RING):
                sp.dma_start(stage[:, u, :], stream[u]).then_inc(s_stage[u], 16)
            turns = (N_UNITS - RING) // RING
            with sp.Fori(0, turns) as t:
                for k in range(RING):
                    sp.wait_ge(s_lo, 2 * RING * t + 2 * k + 2)
                    sp.dma_start(stage[:, k, :], stream[RING * t + (RING + k)]).then_inc(s_stage[k], 16)
            for u in range(RING + turns * RING, N_UNITS):
                sp.wait_ge(s_lo, 2 * (u - RING) + 2)
                sp.dma_start(stage[:, u % RING, :], stream[u]).then_inc(s_stage[u % RING], 16)
            sp.wait_ge(sem("s_hf"), 4 * 5)
            sp.dma_start(out, hf[:, :, :]).then_inc(sem("s_out"), 16)
            sp.wait_ge(sem("s_out"), 16)

        @block.gpsimd
        def _(pool):
            G = nc.gpsimd
            G.memset(ones[:, :], 1.0).then_inc(s_zero, 1)
            pool.wait_ge(sem("s_hlo"), 4)
            for v in (misc, dwda, dg1):
                G.memset(v[:, 0:1], 0.0).then_inc(s_zero, 1)

            pool.wait_ge(s_y, Y_RWKV)
            G.memset(r_raw[:, :, 0:1], 0.0).then_inc(s_zero, 1)
            G.memset(r_S[:, :], 0.0).then_inc(s_zero, 1)

            def level_masks(A, Al, it):
                for lv in range(7):
                    if lv == 2:
                        pool.wait_ge(s_xy, 7 * it + 1)
                    if lv >= 2:
                        pool.wait_ge(s_t1, 7 * it + lv - 1)
                    G.tensor_tensor(Al[lv % 2], A, levels[:, lv, :].unsqueeze(1).broadcast_to([P, 4, P]),
                                    ALU.mult).then_inc(s_al, 1)

            def rwkv(p):
                pool.wait_ge(sem("s_lora_in"), 4 + p)
                pool.dma_start(r_lora, lora_in[p]).then_inc(sem("s_rw_lw"), 16)
                pool.wait_ge(sem("s_rw_A"), p + 1)
                level_masks(r_A, r_Al, p)

            loop(pool, RWKV_P, rwkv)

            pool.wait_ge(s_y, Y_DN)
            pool.dma_start(c12[:, 0:N2], c2_in).then_inc(s_c2, 16)

            pool.wait_ge(sem("s_hlo"), 12)
            G.memset(gb, 0.0).then_inc(s_zero, 1)
            G.memset(n_raw[:, :, 0:3], 0.0).then_inc(s_zero, 1)

            def delta(i):
                pool.wait_ge(sem("s_dn_E"), i + 1)
                G.tensor_tensor(n_E2, n_E2, con("incl").unsqueeze(1).broadcast_to([P, 4, P]),
                                ALU.mult).then_inc(sem("s_dn_E2"), 1)
                pool.wait_ge(sem("s_dn_A"), i + 1)
                level_masks(n_A, n_Al, i + RWKV_P)

            loop(pool, DN_H, delta)
            pool.wait_ge(s_evac[0], EV_SC[0])
            pool.wait_ge(s_evac[1], EV_SC[1])
            pool.wait_ge(sem("s_hlo"), 4 * 4)
            G.memset(q_cu[:, :, 0:2], 0.0).then_inc(s_zero, 1)

        @block.tensor
        def _(pe):
            T = nc.tensor

            def half(out_ap, sub, i, step, hi, lo, kts, first, last):
                slot = sub % RING
                pe.wait_ge(s_lo, sub + 1 + step * i)
                for t in range(SUB):
                    w = slice(t * P, (t + 1) * P)
                    o, k = out_ap[t] if isinstance(out_ap, list) else out_ap, kts[t]
                    T.matmul(o, w_hi[:, slot, w], hi[:, k, :], start=first[t], stop=False)
                    T.matmul(o, w_hi[:, slot, w], lo[:, k, :], start=False, stop=False)
                    ins = T.matmul(o, w_lo[:, slot, w], hi[:, k, :], start=False, stop=last[t])
                ins.then_inc(s_sub, 1)

            def unit(k, u, i, step, hi, lo):
                for hf_ in range(2):
                    half(gp[:, k, 0:S], 2 * u + hf_, i, 2 * step, hi, lo, [SUB * hf_ + t for t in range(SUB)],
                         [hf_ == 0 and t == 0 for t in range(SUB)], [hf_ == 1 and t == SUB - 1 for t in range(SUB)])

            def norm_sum(n):
                for kt in range(KT):
                    if kt % 4 == 0:
                        pe.wait_ge(sem("s_sq"), 4 * n + kt // 4 + 1)
                    ins = T.matmul(pm[:, 0, 0:S], ones[:, :], hf[:, kt, :], start=kt == 0, stop=kt == KT - 1)
                ins.then_inc(sem("s_nsum"), 1)

            def transposes(pairs, s):
                for o, i_ in pairs:
                    ins = T.transpose(o, i_, ident)
                ins.then_inc(s, 1)

            def inverse(Al, X, Y, Tt, it):
                for lv in range(7):
                    pe.wait_ge(s_al, 7 * it + lv + 1)
                    if lv:
                        pe.wait_ge(s_xy, 7 * it + lv)
                    for s_ in range(4):
                        ins = T.matmul(pm[:, 0, s_ * P:(s_ + 1) * P], Al[lv % 2][:, s_, :], ident if lv == 0 else Y[:, s_, :],
                                       start=True, stop=True)
                    ins.then_inc(s_t1, 1)
                    if lv == 0:
                        continue
                    pe.wait_ge(s_t1o, 6 * it + lv)
                    for s_ in range(4):
                        ins = T.matmul(pm[:, 1, s_ * P:(s_ + 1) * P], X[:, s_, :], Tt[:, s_, :], start=True, stop=True)
                    ins.then_inc(s_dy, 1)
                    if lv < 6:
                        for s_ in range(4):
                            ins = T.matmul(pm[:, 2, s_ * P:(s_ + 1) * P], Tt[:, s_, :], X[:, s_, :], start=True, stop=True)
                        ins.then_inc(s_dx, 1)

            pe.wait_ge(s_zero, 1)
            pe.wait_ge(s_load, 16 * LOADS)

            norm_sum(0)
            pe.wait_ge(sem("s_hlo"), 4)
            for j in range(4):
                pe.wait_ge(s_evac[j % 3], EV_PRO[j % 3] + j // 3)
                unit(j % 3, U_PRO + j, 0, 0, h_hi, h_lo)
                if j == 0:
                    pe.wait_ge(s_evac[0], 1)
                    T.matmul(pm[:, 0, 0:S], con("perm_i"), kraw, start=True, stop=True).then_inc(sem("s_ix_rot"), 1)
                if j == 1:
                    pe.wait_ge(s_evac[1], 1)
                    transposes([(pm[:, 4, c * P:(c + 1) * P], misc[:, 1 + c * P:1 + (c + 1) * P]) for c in range(NT)],
                               sem("s_ix_wT"))
            for b in range(IDX_H // 2):
                u = 4 + b
                pe.wait_ge(s_evac[u % 3], u // 3)
                unit(u % 3, U_PRO + u, 0, 0, h_hi, h_lo)
                pe.wait_ge(s_evac[u % 3], u // 3 + 1)
                pe.wait_ge(sem("s_ix_rope"), 1 + b)
                T.matmul(pm[:, 0, 0:S], con("perm_i"), qraw[:, b % 2, :], start=True, stop=True).then_inc(sem("s_ix_rot"), 1)
                pe.wait_ge(sem("s_ix_rope"), 2 + b)
                pe.wait_ge(sem("s_ix_relu"), 2 * b)
                for hd in range(2):
                    rows = slice(64 * hd, 64 * hd + 64)
                    for qt in range(NT):
                        ins = T.matmul(pm[:, 2 + hd, qt * S:(qt + 1) * S], qrope[rows, b % 2, qt * P:(qt + 1) * P],
                                       krope[rows, :], start=True, stop=True)
                    ins.then_inc(sem("s_ix_sc"), 1)

            def dsa(i):
                for j in range(3):
                    pe.wait_ge(s_evac[j], EV_DSA[j] + i)
                    unit(j, U_DSA + j, i, 3, h_hi, h_lo)
                pe.wait_ge(sem("s_qk_sq"), i + 1)
                T.matmul(pm[:, 0, :], ones[:, :], d_sq, start=True, stop=True).then_inc(sem("s_qk_ss"), 1)
                transposes([(pm[:, 4, c * P:(c + 1) * P], d_raw[:, 2, c * P:(c + 1) * P]) for c in range(NT)],
                           sem("s_at_vT"))
                pe.wait_ge(sem("s_ds_qn"), i + 1)
                T.matmul(pm[:, 1, :], con("perm_q"), d_qn.rearrange("p a b -> p (a b)"), start=True,
                         stop=True).then_inc(sem("s_at_rot"), 1)
                pe.wait_ge(sem("s_at_qk"), i + 1)
                for qt in range(NT):
                    ins = T.matmul(pm[:, 2, qt * S:(qt + 1) * S], d_qk[:, 0, qt * P:(qt + 1) * P], d_qk[:, 1, :],
                                   start=True, stop=True)
                ins.then_inc(sem("s_ds_sc"), 1)
                pe.wait_ge(sem("s_at_pr"), i + 1)
                transposes([(pm[:, 3, kt * S + qt * P:kt * S + (qt + 1) * P], d_pr[:, qt, kt * P:(kt + 1) * P])
                            for kt in range(NT) for qt in range(NT)], sem("s_at_pT"))
                pe.wait_ge(sem("s_at_v"), i + 1)
                pe.wait_ge(sem("s_at_pTo"), i + 1)
                for kt in range(NT):
                    ins = T.matmul(pm[:, 0, 0:S], d_v[:, kt, :], d_pT[:, kt, :], start=kt == 0, stop=kt == NT - 1)
                ins.then_inc(sem("s_at_o"), 1)

            pe.wait_ge(s_y, Y_DSA)
            loop(pe, DSA_H, dsa)

            def rwkv(p):
                for j in range(3):
                    pe.wait_ge(s_evac[j], EV_RWKV[j] + p)
                    unit(j, U_RWKV + j, p, 3, h_hi, h_lo)
                pe.wait_ge(s_y, Y_RWKV + p)
                pe.wait_ge(sem("s_rw_lw"), 16 * p + 16)
                T.matmul(pm[:, 0, 0:S], r_lora[0:64, 0:P], tanh_a[0:64, :], start=True, stop=True)
                T.matmul(pm[:, 1, 0:S], r_lora[64:P, 0:P], tanh_a[64:P, :], start=True, stop=True)
                T.matmul(pm[:, 2, 0:S], r_lora[:, P:2 * P], sig1, start=True, stop=False)
                T.matmul(pm[:, 2, 0:S], r_lora[0:32, 2 * P:3 * P], sig2[0:32, :], start=False,
                         stop=True).then_inc(sem("s_lora_in"), 1)
                pe.wait_ge(sem("s_rw_kk2"), p + 1)
                T.matmul(pm[:, 3, 0:S], con("heads"), r_sq, start=True, stop=True).then_inc(sem("s_rw_kkn"), 1)
                pe.wait_ge(sem("s_rw_ops"), p + 1)
                transposes([(pm[:, 3, 0:P], r_mix[:, 2, 0:P]), (pm[:, 3, P:2 * P], r_mix[:, 2, P:S]),
                            (pm[:, 3, 2 * P:3 * P], r_bt[:, 0:P]), (pm[:, 3, 3 * P:4 * P], r_kt[:, 0:P])], sem("s_rw_tT"))
                pe.wait_ge(sem("s_rw_g"), p + 1)
                for hd in range(2):
                    rows = slice(64 * hd, 64 * hd + 64)
                    for c in range(NT):
                        cols = slice(c * P, (c + 1) * P)
                        T.matmul(pm[:, hd, c * P:(c + 1) * P], r_at[rows, cols], r_bt[rows, cols], start=True, stop=True)
                        ins = T.matmul(pm[:, hd, (2 + c) * P:(3 + c) * P], r_kt[rows, cols], r_at[rows, cols], start=True,
                                       stop=True)
                    ins.then_inc(sem("s_rw_mA"), 1)
                for hd in range(2):
                    rows = slice(64 * hd, 64 * hd + 64)
                    bank = (2, 4)[hd]
                    for c in range(NT):
                        cols = slice(c * P, (c + 1) * P)
                        T.matmul(pm[:, bank, c * P:(c + 1) * P], r_bt[rows, cols], r_rt[rows, cols], start=True, stop=True)
                        ins = T.matmul(pm[:, bank, (2 + c) * P:(3 + c) * P], r_kt[rows, cols], r_rt[rows, cols], start=True,
                                       stop=True)
                    ins.then_inc(sem("s_rw_mR"), 1)
                pe.wait_ge(sem("s_rw_R"), p + 1)
                inverse(r_Al, r_X, r_Y, r_T, p)
                pe.wait_ge(sem("s_rw_tok"), p + 1)
                pe.wait_ge(s_xy, 7 * p + 7)
                for c in range(NT):
                    if c:
                        pe.wait_ge(sem("s_rw_S"), p + 1)
                    for hd in range(2):
                        o = slice(c * P + 64 * hd, c * P + 64 * hd + 64)
                        if c:
                            T.matmul(pm[:, 3, o], r_at[:, P:S], r_S[:, 64 * hd:64 * hd + 64], start=True, stop=False)
                        ins = T.matmul(pm[:, 3, o], r_Aak[:, 2 * hd + c, :], r_tok[:, c, 64 * hd:64 * hd + 64],
                                       start=c == 0, stop=True)
                    ins.then_inc(sem("s_rw_mrhs"), 1)
                    pe.wait_ge(sem("s_rw_rhs"), NT * p + c + 1)
                    for hd in range(2):
                        o = slice(c * P + 64 * hd, c * P + 64 * hd + 64)
                        ins = T.matmul(pm[:, 4, o], r_Y[:, 2 * hd + c, :], r_rhs[:, c, 64 * hd:64 * hd + 64], start=True,
                                       stop=True)
                    ins.then_inc(sem("s_rw_mU"), 1)
                    pe.wait_ge(sem("s_rw_U"), NT * p + c + 1)
                    if c == 0:
                        T.matmul(pm[:, 0, 0:P], r_tok[:, 2, :], r_U[:, 0, :], start=True, stop=False)
                        T.matmul(pm[:, 0, 0:P], r_tok[:, 3, :], r_tok[:, 0, :], start=False,
                                 stop=True).then_inc(sem("s_rw_mS"), 1)
                    for hd in range(2):
                        o = slice(c * P + 64 * hd, c * P + 64 * hd + 64)
                        v = slice(64 * hd, 64 * hd + 64)
                        if c:
                            T.matmul(pm[:, 1, o], r_rt[:, P:S], r_S[:, v], start=True, stop=False)
                        T.matmul(pm[:, 1, o], r_R[:, hd, c, :], r_U[:, c, v], start=c == 0, stop=False)
                        ins = T.matmul(pm[:, 1, o], r_R[:, hd, 2 + c, :], r_tok[:, c, v], start=False, stop=True)
                ins.then_inc(sem("s_rw_my"), 1)
                pe.wait_ge(sem("s_rw_yt"), p + 1)
                transposes([(pm[:, 2, c * P:(c + 1) * P], r_X[:, c, :]) for c in range(NT)], sem("s_rw_yT"))
                pe.wait_ge(sem("s_rw_yTo"), p + 1)
                T.matmul(pm[:, 3, 0:S], con("heads"), r_X[:, 2:4, :].rearrange("p a b -> p (a b)"), start=True, stop=True)
                T.matmul(pm[:, 3, S:2 * S], con("heads"), r_D[:, 2, :], start=True, stop=True).then_inc(sem("s_rw_mean"), 1)
                pe.wait_ge(sem("s_rw_yc2"), p + 1)
                T.matmul(pm[:, 4, 0:S], con("heads"), r_Y[:, 2:4, :].rearrange("p a b -> p (a b)"), start=True,
                         stop=True).then_inc(sem("s_rw_var"), 1)

            pe.wait_ge(s_y, Y_RWKV)
            pe.wait_ge(sem("s_lora_in"), 4)
            loop(pe, RWKV_P, rwkv)

            pe.wait_ge(s_y, Y_DN)

            def wout(i):
                for j in range(3):
                    pe.wait_ge(s_evac[j], EV_WOUT[j] + i)
                    unit(j, U_WOUT + j, i, 3, y_hi, y_lo)

            loop(pe, 5, wout)
            pe.wait_ge(s_evac[0], EV_WOUT[0] + 5)
            unit(0, U_WOUT + 15, 0, 0, y_hi, y_lo)

            norm_sum(1)
            pe.wait_ge(sem("s_hf"), 8)
            for tt in range(NT):
                for kt in range(KT):
                    ins = T.matmul(pm[:, 1, tt * 32:tt * 32 + 20], hf[:, kt, tt * P:(tt + 1) * P], route[:, kt, :],
                                   start=kt == 0, stop=kt == KT - 1)
            ins.then_inc(sem("s_rt_lg"), 1)
            pe.wait_ge(sem("s_rt_comb"), 1)
            transposes([(pm[:, 2, tt * P:(tt + 1) * P], comb[:, tt, :]) for tt in range(NT)], sem("s_rt_cT"))
            pe.wait_ge(sem("s_hlo"), 8)
            pe.wait_ge(sem("s_rt_cTo"), 1)

            def token_weights(e):
                pe.wait_ge(sem("s_me_sel"), e + 1)
                T.matmul(gp[:, 0, 0:S], ones[0:16, :], csel[0:16, :], start=True, stop=True).then_inc(sem("s_me_bcm"), 1)

            def moe(e):
                pe.wait_ge(sem("s_me_bc"), e + 1)
                for b in range(4):
                    pe.wait_ge(sem(f"s_me_pair{b % 2}"), 2 * e + b // 2 + 1)
                    for j in range(2):
                        u = U_MOE + 2 * b + j
                        o = (gp[:, 0, 0:S], gp[:, 1, 0:S], gp[:, 2, 0:S], pm[:, 4, 0:S])[2 * (b % 2) + j]
                        for hf_ in range(2):
                            half(o, 2 * u + hf_, e, 24, h_hi, h_lo, [SUB * hf_ + t for t in range(SUB)],
                                 [hf_ == 0 and t == 0 for t in range(SUB)], [hf_ == 1 and t == SUB - 1 for t in range(SUB)])
                pe.wait_ge(sem("s_me_he"), 4 * e + 4)
                token_weights(e + 1)
                for d in range(4):
                    u = U_MOE + 8 + d
                    pe.wait_ge(sem(f"s_me_down{d % 2}"), 2 * e + d // 2 + 1)
                    for hf_ in range(2):
                        nb = [2 * hf_ + t // 4 for t in range(SUB)]
                        o = [pm[:, 2 * (d % 2) + n // 2, (n % 2) * S:(n % 2) * S + S] for n in nb]
                        half(o, 2 * u + hf_, e, 24, y_hi, y_lo, [t % 4 for t in range(SUB)],
                             [t % 4 == 0 for t in range(SUB)], [t % 4 == 3 for t in range(SUB)])

            token_weights(0)
            loop(pe, NEXP, moe)

            norm_sum(2)
            pe.wait_ge(sem("s_hlo"), 12)
            unit(0, U_AB, 0, 0, h_hi, h_lo)
            pe.wait_ge(sem("s_ab_kd"), 1)
            transposes([(pm[:, 0, c * P:(c + 1) * P], gb[:, c * P:(c + 1) * P]) for c in range(NT)], sem("s_ab_T"))

            def delta(i):
                for j in range(6):
                    pe.wait_ge(s_evac[j % 3], EV_DN[j % 3] + 2 * i + j // 3)
                    unit(j % 3, U_DN + j, i, 6, h_hi, h_lo)
                pe.wait_ge(s_y, Y_DN + i)
                pe.wait_ge(sem("s_qk_sq"), DSA_H + i + 1)
                T.matmul(pm[:, 0, :], ones[:, :], n_sq, start=True, stop=True).then_inc(sem("s_qk_ss"), 1)
                transposes([(pm[:, 1, (2 * v + c) * P:(2 * v + c + 1) * P], n_qkv[:, 2 + v, c * P:(c + 1) * P])
                            for v in range(2) for c in range(NT)], sem("s_dn_vT"))
                pe.wait_ge(sem("s_dn_gs"), i + 1)
                T.matmul(pm[:, 4, :], ones[0:16, :], n_gs[0:16, :, :].rearrange("p a b -> p (a b)"), start=True,
                         stop=True).then_inc(sem("s_dn_gb"), 1)
                pe.wait_ge(sem("s_dn_qk"), i + 1)
                for c in range(NT):
                    cols = slice(c * P, (c + 1) * P)
                    T.matmul(pm[:, 3, c * P:(c + 1) * P], n_qkv[:, 1, cols], n_qkv[:, 1, cols], start=True, stop=True)
                    ins = T.matmul(pm[:, 3, (2 + c) * P:(3 + c) * P], n_qkv[:, 1, cols], n_qkv[:, 0, cols], start=True,
                                   stop=True)
                ins.then_inc(sem("s_dn_kk"), 1)
                transposes([(pm[:, 2, 0:P], n_qkv[:, 1, 0:P])], sem("s_dn_kT"))
                pe.wait_ge(sem("s_dn_kd"), i + 1)
                pe.wait_ge(sem("s_dn_QK"), i + 1)
                pe.wait_ge(sem("s_dn_v"), i + 1)
                inverse(n_Al, n_X, n_Y, n_T, i + RWKV_P)
                pe.wait_ge(s_xy, 7 * (i + RWKV_P) + 7)
                for v in range(2):
                    ins = T.matmul(pm[:, 0, v * P:(v + 1) * P], n_Y[:, 2 * v, :], n_r0[:, v, :], start=True, stop=True)
                ins.then_inc(sem("s_dn_m0"), 1)
                pe.wait_ge(sem("s_dn_vn"), 2 * i + 1)
                for v in range(2):
                    ins = T.matmul(pm[:, 1, v * P:(v + 1) * P], n_kd[:, v, :], n_vn[:, v, :], start=True, stop=True)
                ins.then_inc(sem("s_dn_mS"), 1)
                for v in range(2):
                    T.matmul(pm[:, 2, v * P:(v + 1) * P], n_QK[:, 2 * v, :], n_vn[:, v, :], start=True, stop=True)
                pe.wait_ge(sem("s_dn_S"), i + 1)
                state = n_S.rearrange("p a b -> p (a b)")
                T.matmul(pm[:, 3, 0:S], n_qkv[:, 1, P:S], state, start=True, stop=True)
                T.matmul(pm[:, 3, S:2 * S], n_qkv[:, 0, P:S], state, start=True, stop=True).then_inc(sem("s_dn_mks"), 1)
                pe.wait_ge(sem("s_dn_r1"), i + 1)
                for v in range(2):
                    ins = T.matmul(pm[:, 0, S + v * P:S + (v + 1) * P], n_Y[:, 2 * v + 1, :], n_r1[:, v, :], start=True,
                                   stop=True)
                ins.then_inc(sem("s_dn_m0"), 1)
                pe.wait_ge(sem("s_dn_vn"), 2 * i + 2)
                for v in range(2):
                    ins = T.matmul(pm[:, 2, S + v * P:S + (v + 1) * P], n_QK[:, 2 * v + 1, :], n_vn[:, 2 + v, :], start=True,
                                   stop=True)
                ins.then_inc(sem("s_dn_mo"), 1)
                pe.wait_ge(sem("s_dn_on"), i + 1)
                transposes([(pm[:, 4, v * S + c * P:v * S + (c + 1) * P], n_o[:, 2 * c + v, :]) for v in range(2)
                            for c in range(NT)], sem("s_dn_oT"))

            pe.wait_ge(sem("s_ab_tok"), 1)
            loop(pe, DN_H, delta)

            def swa(i):
                for j in range(6):
                    pe.wait_ge(s_evac[j % 3], EV_SW[j % 3] + 2 * i + j // 3)
                    unit(j % 3, U_SW + j, i, 6, h_hi, h_lo)
                pe.wait_ge(s_y, Y_SW + i)
                pe.wait_ge(s_evac[0], EV_SW[0] + 2 * i + 2)
                for n in range(2):
                    ins = T.matmul(pm[:, n, :], con("perm_w"), w_raw[:, 2 * n:2 * n + 2, :].rearrange("p a b -> p (a b)"),
                                   start=True, stop=True)
                ins.then_inc(sem("s_at_rot"), 1)
                pe.wait_ge(s_evac[1], EV_SW[1] + 2 * i + 2)
                transposes([(pm[:, 4, c * P:(c + 1) * P], w_v0[:, c * P:(c + 1) * P]) for c in range(NT)], sem("s_at_vT"))
                pe.wait_ge(sem("s_at_qk"), DSA_H + i + 1)
                for g in range(3):
                    ins = T.matmul(pm[:, 0, g * P:(g + 1) * P], w_qk[:, g, 0:P], w_qk[:, 3, 0:P], start=True, stop=True)
                ins.then_inc(sem("s_sw_sc"), 1)
                for g in range(3):
                    ins = T.matmul(pm[:, 1 + g // 2, (g % 2) * S:(g % 2) * S + S], w_qk[:, g, P:S], w_qk[:, 3, :], start=True,
                                   stop=True)
                ins.then_inc(sem("s_sw_sc"), 1)
                pe.wait_ge(sem("s_at_pr"), DSA_H + i + 1)
                transposes([(pm[:, 3, 0:P], w_p0), (pm[:, 3, P:2 * P], w_p1[:, 0:P]), (pm[:, 3, 2 * P:3 * P], w_p1[:, P:S])],
                           sem("s_at_pT"))
                pe.wait_ge(sem("s_at_v"), DSA_H + i + 1)
                pe.wait_ge(sem("s_at_pTo"), DSA_H + i + 1)
                T.matmul(pm[:, 0, 0:P], w_v[:, 0, :], w_pT[:, 0, :], start=True, stop=True)
                T.matmul(pm[:, 0, P:S], w_v[:, 0, :], w_pT[:, 1, :], start=True, stop=False)
                T.matmul(pm[:, 0, P:S], w_v[:, 1, :], w_pT[:, 2, :], start=False, stop=True).then_inc(sem("s_at_o"), 1)

            pe.wait_ge(s_y, Y_SW)
            pe.wait_ge(s_c2, 16)
            loop(pe, SW_H, swa)

            def project(u0, ev):
                def turn(i):
                    for b in range(2):
                        pe.wait_ge(s_evac[b], ev[b] + i)
                        for s_ in range(3):
                            half(gp[:, b, 0:S], 2 * u0 + 3 * b + s_, i, 6, y_hi, y_lo, [SUB * s_ + t for t in range(SUB)],
                                 [s_ == 0 and t == 0 for t in range(SUB)], [s_ == 2 and t == SUB - 1 for t in range(SUB)])
                return turn

            pe.wait_ge(s_y, Y_SC)
            loop(pe, 8, project(U_HOUT, EV_HOUT))

            norm_sum(3)
            pe.wait_ge(sem("s_hlo"), 16)

            def shortconv(i):
                for n in range(12):
                    pe.wait_ge(s_evac[n % 3], EV_SC[n % 3] + 4 * i + n // 3)
                    unit(n % 3, U_SC + n, i, 12, h_hi, h_lo)

            loop(pe, 8, shortconv)
            pe.wait_ge(s_y, Y_SC + 24)
            out_turn = project(U_SOUT, EV_SOUT)
            loop(pe, 7, out_turn)
            out_turn(7)
            norm_sum(4)

        @block.scalar
        def _(act):
            A = nc.scalar
            chain = Chain(act, s_ac)

            def split(sub, i=0, step=0):
                if isinstance(i, int) and sub + step * i >= N_SUBS:
                    return
                u, slot = sub // 2, sub % RING
                act.wait_ge(s_stage[u % RING], 16 * (u // RING + 1) + 16 * (step // (2 * RING)) * i)
                if sub >= RING:
                    act.wait_ge(s_sub, sub - RING + 1 + step * i)
                A.activation(w_hi[:, slot, :], stage[:, u % RING, (sub % 2) * SUB * P:(sub % 2 + 1) * SUB * P],
                             ACT.Copy).then_inc(s_hi, 1)

            def ahead(u, i=0, step=0):
                split(2 * u + RING, i, 2 * step)
                split(2 * u + RING + 1, i, 2 * step)

            def done(u, i=0, step=0):
                act.wait_ge(s_sub, 2 * u + 2 + 2 * step * i)

            for o, src in ((x[:, :, :], x_in), (vecs[:, :], vecs_in), (c0[:, :], c0_in), (c12[:, 0:N1], c1_in),
                           (route[:, :, :], route_in), (rbias[:, :], rbias_in)):
                act.dma_start(o, src).then_inc(s_load, 16)

            def norm(n, last=False):
                for q in range(4):
                    A.activation(hf[:, 4 * q:4 * q + 4, :], x[:, 4 * q:4 * q + 4, :], ACT.Square).then_inc(sem("s_sq"), 1)
                act.wait_ge(sem("s_nrv"), n + 1)
                A.activation(n_rs, n_rs, ACT.Sqrt).then_inc(sem("s_nrs"), 1)
                if last:
                    return
                for q in range(4):
                    act.wait_ge(sem("s_hf"), 4 * n + q + 1)
                    A.activation(h_hi[:, 4 * q:4 * q + 4, :], hf[:, 4 * q:4 * q + 4, :], ACT.Copy).then_inc(sem("s_hhi"), 1)

            act.wait_ge(s_load, 16 * LOADS)
            norm(0)
            for sub in range(RING):
                split(sub)
            act.wait_ge(sem("s_hlo"), 4)
            act.wait_ge(s_zero, 4)
            for j in range(4):
                ahead(U_PRO + j)
                done(U_PRO + j)
                o = (kraw, misc[:, 1:S + 1], dwda[:, 1:S + 1], dg1[:, 1:S + 1])[j]
                A.activation(o, gp[:, j % 3, 0:S], ACT.Copy).then_inc(s_evac[j % 3], 1)
            act.wait_ge(sem("s_lora_mix"), 1)
            A.activation(tanh_a[0:64, :], t_2[0:64, :], ACT.Tanh).then_inc(sem("s_lora_in"), 1)
            A.activation(tanh_a[64:P, :], t_2[64:P, :], ACT.Copy).then_inc(sem("s_lora_in"), 1)
            act.wait_ge(sem("s_lora_mix"), 2)
            A.activation(sig1, mixd, ACT.Sigmoid).then_inc(sem("s_lora_in"), 1)
            act.wait_ge(sem("s_lora_mix"), 3)
            A.activation(sig2, sig2, ACT.Sigmoid).then_inc(sem("s_lora_in"), 1)
            for b in range(IDX_H // 2):
                u = 4 + b
                ahead(U_PRO + u)
                done(U_PRO + u)
                if b >= 2:
                    act.wait_ge(sem("s_ix_rope"), b)
                A.activation(qraw[:, b % 2, :], gp[:, u % 3, 0:S], ACT.Copy).then_inc(s_evac[u % 3], 1)
                for hd in range(2):
                    act.wait_ge(sem("s_ix_sc"), 2 * b + hd + 1)
                    if b:
                        act.wait_ge(sem("s_ix_acc"), 2 * b - 1 + hd)
                    A.activation(relu[:, hd, :], pm[:, 2 + hd, :], ACT.Relu).then_inc(sem("s_ix_relu"), 1)

            def dsa(i):
                for j in range(3):
                    ahead(U_DSA + j, i, 3)
                    if j == 0:
                        act.wait_ge(s_y, Y_DSA + i)
                    done(U_DSA + j, i, 3)
                    A.activation(d_raw[:, j, :], gp[:, j, 0:S], ACT.Copy).then_inc(s_evac[j], 1)
                act.wait_ge(s_evac[2], EV_DSA[2] + 1 + i)
                A.activation(d_sq, d_raw[:, 0:2, :].rearrange("p a b -> p (a b)"), ACT.Square).then_inc(sem("s_qk_sq"), 1)
                act.wait_ge(sem("s_qk_rv"), i + 1)
                A.activation(d_rs, d_rs, ACT.Sqrt).then_inc(sem("s_qk_rs"), 1)
                act.wait_ge(sem("s_at_nm"), i + 1)
                for qt in range(NT):
                    A.activation(d_pr[:, qt, :], d_lg[:, qt, :], ACT.Exp, bias=d_nm[:, qt:qt + 1],
                                 accum_out=d_sum[:, qt:qt + 1]).then_inc(sem("s_ds_ex"), 1)
                act.wait_ge(sem("s_at_pT"), i + 1)
                A.activation(d_pT.rearrange("p a b -> p (a b)"), pm[:, 3, :], ACT.Copy).then_inc(sem("s_at_pTo"), 1)
                act.wait_ge(sem("s_at_o"), i + 1)
                A.activation(y_hi[:, i, :], pm[:, 0, 0:S], ACT.Copy).then_inc(s_yhi, 1)

            act.wait_ge(s_y, Y_DSA)
            loop(act, DSA_H, dsa)

            def solver(Tt, it):
                for lv in range(1, 7):
                    act.wait_ge(s_t1, 7 * it + lv + 1)
                    A.activation(Tt.rearrange("p a b -> p (a b)"), pm[:, 0, :], ACT.Copy).then_inc(s_t1o, 1)

            def rwkv(p):
                for j in range(3):
                    ahead(U_RWKV + j, p, 3)
                    if j == 0:
                        act.wait_ge(s_y, Y_RWKV + p)
                    done(U_RWKV + j, p, 3)
                    A.activation(r_raw[:, j, 1:S + 1], gp[:, j, 0:S], ACT.Copy).then_inc(s_evac[j], 1)
                act.wait_ge(sem("s_lora_in"), 5 + p)
                A.activation(r_lw, pm[:, 0, 0:S], ACT.Sigmoid, bias=vec("w0", p))
                A.activation(r_a, pm[:, 1, 0:S], ACT.Sigmoid, bias=vec("a0", p)).then_inc(sem("s_rw_sig"), 1)
                A.activation(r_g, pm[:, 2, 0:S], ACT.Copy).then_inc(sem("s_rw_g"), 1)
                act.wait_ge(sem("s_rw_kkn"), p + 1)
                A.activation(r_tmp, pm[:, 3, 0:S], ACT.Sqrt).then_inc(sem("s_rw_nrm"), 1)
                act.wait_ge(sem("s_rw_cc"), p + 1)
                A.activation(r_P, r_cum, ACT.Exp)
                A.activation(r_Pi, r_cum, ACT.Exp, scale=-1.0)
                A.activation(r_em, r_negm, ACT.Exp, scale=-1.0)
                A.activation(r_lw, r_lw, ACT.Exp).then_inc(sem("s_rw_exp"), 1)
                act.wait_ge(sem("s_rw_tT"), p + 1)
                A.activation(r_tok.rearrange("p a b -> p (a b)"), pm[:, 3, :], ACT.Copy).then_inc(sem("s_rw_tok"), 1)
                for hd in range(2):
                    act.wait_ge(sem("s_rw_mA"), 2 * p + hd + 1)
                    ins = A.activation(r_A[:, 2 * hd:2 * hd + 2, :].rearrange("p a b -> p (a b)"), pm[:, hd, 0:S], ACT.Copy)
                ins.then_inc(sem("s_rw_A"), 1)
                solver(r_T, p)
                for c in range(NT):
                    act.wait_ge(sem("s_rw_mrhs"), NT * p + c + 1)
                    A.activation(r_rhs[:, c, :], pm[:, 3, c * P:(c + 1) * P], ACT.Copy).then_inc(sem("s_rw_rhs"), 1)
                    act.wait_ge(sem("s_rw_mU"), NT * p + c + 1)
                    A.activation(r_U[:, c, :], pm[:, 4, c * P:(c + 1) * P], ACT.Copy).then_inc(sem("s_rw_U"), 1)
                act.wait_ge(sem("s_rw_my"), p + 1)
                A.activation(r_X[:, 0:2, :].rearrange("p a b -> p (a b)"), pm[:, 1, 0:S], ACT.Copy).then_inc(sem("s_rw_yt"), 1)
                act.wait_ge(sem("s_rw_yT"), p + 1)
                A.activation(r_X[:, 2:4, :].rearrange("p a b -> p (a b)"), pm[:, 2, 0:S], ACT.Copy).then_inc(sem("s_rw_yTo"), 1)
                act.wait_ge(sem("s_rw_yc"), p + 1)
                A.activation(r_Y[:, 2:4, :], r_Y[:, 0:2, :], ACT.Square).then_inc(sem("s_rw_yc2"), 1)
                act.wait_ge(sem("s_ho_rv"), p + 1)
                A.activation(r_tmp, r_tmp, ACT.Sqrt).then_inc(sem("s_ho_rs"), 1)
                act.wait_ge(sem("s_yf"), p + 1)
                A.activation(y_hi[:, p + DSA_H, :], r_sq, ACT.Copy).then_inc(s_yhi, 1)

            act.wait_ge(s_zero, 6)
            loop(act, RWKV_P, rwkv)

            loop(act, 5, lambda i: [ahead(U_WOUT + j, i, 3) for j in range(3)])
            ahead(U_WOUT + 15)
            for k in range(3):
                act.wait_ge(s_evac[k], EV_AB[k])
            norm(1)
            for n in range(2):
                act.wait_ge(sem("s_rt_d"), n + 1)
                A.activation(e4, g4, ACT.Exp).then_inc(sem("s_rt_e"), 1)
            act.wait_ge(sem("s_rt_cT"), 1)
            A.activation(combT, pm[:, 2, 0:S], ACT.Copy).then_inc(sem("s_rt_cTo"), 1)

            def moe(e):
                for b in range(4):
                    ahead(U_MOE + 2 * b, e, 12)
                    ahead(U_MOE + 2 * b + 1, e, 12)
                    done(U_MOE + 2 * b + 1, e, 12)
                    A.activation(sg[:, b % 2, :], gp[:, 2 * (b % 2), 0:S], ACT.Silu).then_inc(sem("s_me_sg"), 1)
                    act.wait_ge(sem("s_me_he2"), 4 * e + b + 1)
                    A.activation(y_hi[:, b, :], he2[:, b % 2, :], ACT.Copy).then_inc(sem("s_me_hhi"), 1)
                token_weights(e + 1)
                for d in range(4):
                    ahead(U_MOE + 8 + d, e, 12)

            def token_weights(e):
                act.wait_ge(sem("s_me_bcm"), e + 1)
                A.activation(bce, gp[:, 0, 0:S], ACT.Copy).then_inc(sem("s_me_bc"), 1)

            token_weights(0)
            loop(act, NEXP, moe)

            for k in range(2):
                act.wait_ge(sem(f"s_me_down{k}"), 2 * NEXP + 1)
            norm(2)
            ahead(U_AB)
            act.wait_ge(sem("s_hlo"), 12)
            done(U_AB)
            A.activation(ab, gp[:, 0, 0:S], ACT.Copy).then_inc(s_evac[0], 1)
            act.wait_ge(s_evac[0], EV_DN[0])
            act.wait_ge(s_zero, 7)
            A.activation(gb[32:48, :], ab[32:48, :], ACT.Sigmoid)
            act.wait_ge(sem("s_ab_x"), 1)
            chain.link(A.activation(g_e[0:16, :], g_e[0:16, :], ACT.Exp))
            A.activation(ea[0:16, :], vecs[0:16, VEC["a_log"]:VEC["a_log"] + 1], ACT.Exp)
            A.activation(g_s[0:16, :], g_e[0:16, :], ACT.Ln, bias=1.0).then_inc(sem("s_ab_ln"), 1)
            act.wait_ge(sem("s_ab_cum"), 1)
            A.activation(gb[64:80, 0:P], g_x[0:16, 0:P], ACT.Exp).then_inc(sem("s_ab_kd"), 1)
            act.wait_ge(sem("s_ab_tokg"), 1)
            A.activation(egt, gtok[:, :, 0:16], ACT.Exp).then_inc(sem("s_ab_eg"), 1)

            def delta(i):
                for j in range(6):
                    ahead(U_DN + j, i, 6)
                    if j == 0:
                        act.wait_ge(s_y, Y_DN + i)
                    done(U_DN + j, i, 6)
                    if j < 4:
                        A.activation(n_raw[:, j, 3:S + 3], gp[:, j % 3, 0:S], ACT.Copy).then_inc(s_evac[j % 3], 1)
                    else:
                        A.activation(n_z[:, j - 4, :], gp[:, j % 3, 0:S], ACT.Silu).then_inc(s_evac[j % 3], 1)
                act.wait_ge(sem("s_dn_cv"), i + 1)
                chain.link(A.activation(n_qkv, n_qkv, ACT.Silu))
                A.activation(n_sq, n_qkv[:, 0:2, :].rearrange("p a b -> p (a b)"), ACT.Square).then_inc(sem("s_qk_sq"), 1)
                act.wait_ge(sem("s_dn_vT"), i + 1)
                A.activation(n_v.rearrange("p a b -> p (a b)"), pm[:, 1, :], ACT.Copy).then_inc(sem("s_dn_v"), 1)
                act.wait_ge(sem("s_qk_rv"), DSA_H + i + 1)
                A.activation(n_rn, n_rn, ACT.Sqrt).then_inc(sem("s_qk_rs"), 1)
                act.wait_ge(sem("s_dn_D"), i + 1)
                A.activation(n_E2, n_E2, ACT.Exp).then_inc(sem("s_dn_E"), 1)
                A.activation(n_E1, n_E1, ACT.Exp, scale=-1.0).then_inc(sem("s_dn_E1"), 1)
                solver(n_T, i + RWKV_P)
                act.wait_ge(sem("s_dn_m0"), 2 * i + 1)
                A.activation(n_vn[:, 0:2, :].rearrange("p a b -> p (a b)"), pm[:, 0, 0:S], ACT.Copy).then_inc(sem("s_dn_vn"), 1)
                act.wait_ge(sem("s_dn_mS"), i + 1)
                A.activation(n_S.rearrange("p a b -> p (a b)"), pm[:, 1, 0:S], ACT.Copy).then_inc(sem("s_dn_S"), 1)
                act.wait_ge(sem("s_dn_m0"), 2 * i + 2)
                A.activation(n_vn[:, 2:4, :].rearrange("p a b -> p (a b)"), pm[:, 0, S:2 * S], ACT.Copy).then_inc(sem("s_dn_vn"), 1)
                act.wait_ge(sem("s_dn_mo"), i + 1)
                A.activation(n_o.rearrange("p a b -> p (a b)"), pm[:, 2, :], ACT.Copy).then_inc(sem("s_dn_o"), 1)
                act.wait_ge(sem("s_dn_ot"), i + 1)
                for k in range(4):
                    ins = A.activation(n_A[:, k, :], n_o[:, k, :], ACT.Square, accum_out=n_ss[:, k:k + 1])
                ins.then_inc(sem("s_dn_os"), 1)
                act.wait_ge(sem("s_ho_rv"), RWKV_P + i + 1)
                A.activation(n_or, n_or, ACT.Sqrt).then_inc(sem("s_ho_rs"), 1)
                act.wait_ge(sem("s_yf"), RWKV_P + i + 1)
                A.activation(y_hi[:, bass.ds(2 * i, 2), :], n_yf, ACT.Copy).then_inc(s_yhi, 1)

            act.wait_ge(s_zero, 8)
            chain.loop(DN_H, 1, delta)

            def swa(i):
                for j in range(6):
                    ahead(U_SW + j, i, 6)
                    if j == 0:
                        act.wait_ge(s_y, Y_SW + i)
                    done(U_SW + j, i, 6)
                    o = w_raw[:, j, :] if j < 4 else w_v0 if j == 4 else w_z
                    A.activation(o, gp[:, j % 3, 0:S], ACT.Silu if j == 5 else ACT.Copy).then_inc(s_evac[j % 3], 1)
                act.wait_ge(sem("s_at_nm"), DSA_H + i + 1)
                A.activation(w_l0, w_l0, ACT.Exp, bias=w_nm[:, 0:1], accum_out=w_sum[:, 0:1])
                A.activation(w_l1, w_l1, ACT.Exp, bias=w_nm[:, 1:2], accum_out=w_sum[:, 1:2]).then_inc(sem("s_sw_ex"), 1)
                act.wait_ge(sem("s_at_pT"), DSA_H + i + 1)
                A.activation(w_pT.rearrange("p a b -> p (a b)"), pm[:, 3, 0:3 * P], ACT.Copy).then_inc(sem("s_at_pTo"), 1)
                act.wait_ge(sem("s_yf"), RWKV_P + DN_H + i + 1)
                A.activation(y_hi[:, i + 16, :], w_yf, ACT.Copy).then_inc(s_yhi, 1)

            loop(act, SW_H, swa)

            def project(u0):
                def turn(i):
                    for j in range(3):
                        ahead(u0 + j, i, 3)
                return turn

            loop(act, 8, project(U_HOUT))

            for k in range(3):
                act.wait_ge(s_evac[k], EV_SC[k])
            norm(3)
            act.wait_ge(sem("s_hlo"), 16)

            def shortconv(i):
                for n in range(12):
                    bb, j, k = n // 4, n % 4, n % 3
                    ahead(U_SC + n, i, 12)
                    if j == 2:
                        continue
                    if j == 0:
                        act.wait_ge(s_y, Y_SC - 2 + bb + 3 * i)
                    done(U_SC + n, i, 12)
                    o = (q_b, q_c, None, q_z)[j][:, bb, :]
                    A.activation(o, gp[:, k, 0:S], ACT.Silu if j == 3 else ACT.Copy).then_inc(s_evac[k], 1)
                    if j == 3:
                        act.wait_ge(sem("s_sc_y"), 3 * i + bb + 1)
                        A.activation(y_hi[:, 3 * i + bb, :], q_a[:, bb, :], ACT.Copy).then_inc(s_yhi, 1)

            loop(act, 8, shortconv)
            loop(act, 7, project(U_SOUT))
            project(U_SOUT)(7)
            for k in range(3):
                act.wait_ge(s_evac[k], EV_END[k])
            norm(4, last=True)

        @block.vector
        def _(dve):
            V = nc.vector
            chain = Chain(dve, s_dv)
            link = chain.link

            def split(sub, i=0, step=0):
                if isinstance(i, int) and sub + step * i >= N_SUBS:
                    return
                u, slot = sub // 2, sub % RING
                dve.wait_ge(s_hi, sub + 1 + step * i)
                V.tensor_tensor(w_lo[:, slot, :], stage[:, u % RING, (sub % 2) * SUB * P:(sub % 2 + 1) * SUB * P],
                                w_hi[:, slot, :].bitcast(F32), ALU.subtract).then_inc(s_lo, 1)

            def ahead(u, i=0, step=0):
                split(2 * u + RING, i, 2 * step)
                split(2 * u + RING + 1, i, 2 * step)

            def lower(lo, hi, full, s):
                V.tensor_tensor(lo, full, hi.bitcast(F32), ALU.subtract).then_inc(s, 1)

            def norm(n, gain, last=False):
                dve.wait_ge(sem("s_nsum"), n + 1)
                link(V.tensor_scalar(n_rs, pm[:, 0, 0:S], 1.0 / D, EPS, ALU.mult, ALU.add))
                V.reciprocal(n_rs, n_rs).then_inc(sem("s_nrv"), 1)
                dve.wait_ge(sem("s_nrs"), n + 1)
                for kt in range(KT):
                    ins = V.scalar_tensor_tensor(hf[:, kt, :], x[:, kt, :], vecs[:, gain + kt:gain + kt + 1], n_rs, ALU.mult,
                                                 ALU.mult)
                    if kt % 4 == 3:
                        ins.then_inc(sem("s_hf"), 1)
                if last:
                    return
                for q in range(4):
                    dve.wait_ge(sem("s_hhi"), 4 * n + q + 1)
                    lower(h_lo[:, 4 * q:4 * q + 4, :], h_hi[:, 4 * q:4 * q + 4, :], hf[:, 4 * q:4 * q + 4, :], sem("s_hlo"))

            def bc(ap, n):
                return ap.unsqueeze(1).broadcast_to([P, n, ap.shape[-1]])

            dve.wait_ge(s_load, 16 * LOADS)
            norm(0, VEC["g_mix"])
            for sub in range(RING):
                split(sub)
            dve.wait_ge(sem("s_hlo"), 4)
            for j in range(4):
                ahead(U_PRO + j)
            dve.wait_ge(sem("s_ix_rot"), 1)
            V.tensor_tensor(t_1, kraw, con("cos_i"), ALU.mult)
            link(V.tensor_tensor(t_2, pm[:, 0, 0:S], con("sin_i"), ALU.mult))
            link(V.tensor_tensor(krope, t_1, t_2, ALU.add))
            dve.wait_ge(sem("s_ix_wT"), 1)
            V.tensor_scalar(wtok, pm[:, 4, 0:S].rearrange("p (a b) -> p a b", a=NT)[:, :, 32:48],
                            float(IDX_H ** -0.5 * 64 ** -0.5), None, ALU.mult).then_inc(sem("s_ix_rope"), 1)
            dve.wait_ge(s_evac[2], 1)
            link(V.tensor_tensor(t_1, dwda[:, 0:S], dwda[:, 1:S + 1], ALU.subtract))
            V.scalar_tensor_tensor(t_2, t_1, vec("mu_dwda"), dwda[:, 1:S + 1], ALU.mult,
                                   ALU.add).then_inc(sem("s_lora_mix"), 1)
            dve.wait_ge(s_evac[0], 2)
            dve.wait_ge(sem("s_lora_mix"), 1)
            link(V.tensor_tensor(t_1, dg1[:, 0:S], dg1[:, 1:S + 1], ALU.subtract))
            V.scalar_tensor_tensor(mixd, t_1, vec("mu_dg1"), dg1[:, 1:S + 1], ALU.mult,
                                   ALU.add).then_inc(sem("s_lora_mix"), 1)
            dve.wait_ge(sem("s_lora_mix"), 2)
            link(V.tensor_tensor(t_1, misc[:, 0:S], misc[:, 1:S + 1], ALU.subtract))
            V.scalar_tensor_tensor(sig2, t_1, vec("mu_dg2"), misc[:, 1:S + 1], ALU.mult,
                                   ALU.add).then_inc(sem("s_lora_mix"), 1)
            dve.wait_ge(sem("s_lora_mix"), 3)
            dve.wait_ge(sem("s_lora_in"), 2)
            for b in range(IDX_H // 2):
                ahead(U_PRO + 4 + b)
                dve.wait_ge(sem("s_ix_rot"), b + 2)
                V.tensor_tensor(t_1, qraw[:, b % 2, :], con("cos_i"), ALU.mult)
                link(V.tensor_tensor(t_2, pm[:, 0, 0:S], con("sin_i"), ALU.mult))
                V.tensor_tensor(qrope[:, b % 2, :], t_1, t_2, ALU.add).then_inc(sem("s_ix_rope"), 1)
                dve.wait_ge(sem("s_ix_rope"), b + 2)
                for hd in range(2):
                    dve.wait_ge(sem("s_ix_relu"), 2 * b + hd + 1)
                    if b or hd:
                        dve.wait_ge(sem("s_ix_acc"), 2 * b + hd)
                    for qt in range(NT):
                        r = relu[:, hd, qt * S:(qt + 1) * S]
                        w = wtok[:, qt, 2 * b + hd:2 * b + hd + 1]
                        if b == 0 and hd == 0:
                            ins = V.tensor_scalar(isc[:, qt, :], r, w, None, ALU.mult)
                        else:
                            ins = V.scalar_tensor_tensor(isc[:, qt, :], r, w, isc[:, qt, :], ALU.mult, ALU.add)
                    ins.then_inc(sem("s_ix_acc"), 1)
            dve.wait_ge(sem("s_ix_acc"), IDX_H)
            V.memset(isc[0:64, 0, 64:S], NEG)
            V.memset(isc[64:P, 0, P:S], NEG)
            link(V.memset(isc[0:64, 1, 192:S], NEG))
            for r in range(TOPK // 8):
                V.max(top8[:, 0, :], isc[:, 0, :])
                link(V.max(top8[:, 1, :], isc[:, 1, :]))
                V.match_replace(isc[:, 0, :], top8[:, 0, :], isc[:, 0, :], MARK)
                link(V.match_replace(isc[:, 1, :], top8[:, 1, :], isc[:, 1, :], MARK))
            V.tensor_scalar(notsel, isc, MARK, BIG, ALU.not_equal, ALU.mult).then_inc(s_y, 1)
            dve.wait_ge(s_y, Y_DSA)

            def dsa(i):
                for j in range(3):
                    ahead(U_DSA + j, i, 3)
                dve.wait_ge(sem("s_qk_ss"), i + 1)
                link(V.tensor_scalar(d_rs, pm[:, 0, :], 1.0 / P, EPS, ALU.mult, ALU.add))
                V.reciprocal(d_rs, d_rs).then_inc(sem("s_qk_rv"), 1)
                dve.wait_ge(sem("s_at_vT"), i + 1)
                V.tensor_copy(d_v.rearrange("p a b -> p (a b)"), pm[:, 4, 0:S]).then_inc(sem("s_at_v"), 1)
                dve.wait_ge(sem("s_qk_rs"), i + 1)
                V.scalar_tensor_tensor(d_qn[:, 0, :], d_raw[:, 0, :], vec("q_gain"), d_rs[:, 0:S], ALU.mult, ALU.mult)
                V.scalar_tensor_tensor(d_qn[:, 1, :], d_raw[:, 1, :], vec("k_gain"), d_rs[:, S:2 * S], ALU.mult,
                                       ALU.mult).then_inc(sem("s_ds_qn"), 1)
                dve.wait_ge(sem("s_at_rot"), i + 1)
                V.tensor_tensor(d_t1, d_qn, bc(con("cos_q"), 2), ALU.mult)
                link(V.tensor_tensor(d_t2, pm[:, 1, :].rearrange("p (a b) -> p a b", a=2), bc(con("sin_q"), 2), ALU.mult))
                V.tensor_tensor(d_qk, d_t1, d_t2, ALU.add).then_inc(sem("s_at_qk"), 1)
                dve.wait_ge(sem("s_ds_sc"), i + 1)
                link(V.scalar_tensor_tensor(d_lg.rearrange("p a b -> p (a b)"), pm[:, 2, :], float(P ** -0.5),
                                            notsel.rearrange("p a b -> p (a b)"), ALU.mult, ALU.subtract))
                V.reduce_max(d_nm, d_lg, AX, negate=True).then_inc(sem("s_at_nm"), 1)
                dve.wait_ge(sem("s_ds_ex"), NT * i + NT)
                link(V.reciprocal(d_sum, d_sum))
                for qt in range(NT):
                    ins = V.tensor_scalar(d_pr[:, qt, :], d_pr[:, qt, :], d_sum[:, qt:qt + 1], None, ALU.mult)
                ins.then_inc(sem("s_at_pr"), 1)
                dve.wait_ge(s_yhi, Y_DSA + i)
                lower(y_lo[:, i, :], y_hi[:, i, :], pm[:, 0, 0:S], s_y)

            chain.loop(DSA_H, 4, dsa)

            def solver(Al, X, Y, it):
                dve.wait_ge(s_t1, 7 * it + 1)
                V.tensor_tensor(X, Al[0], bc(ident, 4), ALU.add)
                V.tensor_tensor(Y, pm[:, 0, :].rearrange("p (a b) -> p a b", a=4), bc(ident, 4), ALU.add).then_inc(s_xy, 1)
                for lv in range(1, 7):
                    dve.wait_ge(s_xy, 7 * it + lv)
                    if lv < 6:
                        dve.wait_ge(s_dx, 5 * it + lv)
                        V.tensor_tensor(X, X, pm[:, 2, :].rearrange("p (a b) -> p a b", a=4), ALU.add)
                    dve.wait_ge(s_dy, 6 * it + lv)
                    V.tensor_tensor(Y, Y, pm[:, 1, :].rearrange("p (a b) -> p a b", a=4), ALU.add).then_inc(s_xy, 1)

            def rwkv(p):
                for j in range(3):
                    ahead(U_RWKV + j, p, 3)
                for j in range(3):
                    dve.wait_ge(s_evac[j], EV_RWKV[j] + 1 + p)
                link(V.tensor_tensor(r_D, r_raw[:, :, 0:S], r_raw[:, :, 1:S + 1], ALU.subtract))
                for j in range(3):
                    ins = V.scalar_tensor_tensor(r_mix[:, j, :], r_D[:, j, :], vec("mu", p + 8 * j), r_raw[:, j, 1:S + 1],
                                                 ALU.mult, ALU.add)
                link(ins)
                kk, kp, rk = r_D[:, 0, :], r_D[:, 1, :], r_D[:, 2, :]
                link(V.tensor_scalar(kk, r_mix[:, 1, :], vec("k_k", p), None, ALU.mult))
                V.tensor_tensor(r_sq, kk, kk, ALU.mult).then_inc(sem("s_rw_kk2"), 1)
                dve.wait_ge(sem("s_rw_sig"), p + 1)
                link(V.tensor_scalar(r_lw, r_lw, -float(np.exp(-0.5)), None, ALU.mult))
                for c in range(NT):
                    ins = V.tensor_tensor_scan(r_cum[:, c * P:(c + 1) * P], ones[:, :], r_lw[:, c * P:(c + 1) * P], 0.0,
                                               ALU.mult, ALU.add)
                link(ins)
                mid = r_cum.rearrange("p (c t) -> p c t", c=NT)[:, :, P // 2 - 1:P // 2]
                link(V.tensor_scalar(r_negm.unsqueeze(2), mid, -1.0, None, ALU.mult))
                for c in range(NT):
                    ins = V.tensor_scalar(r_cum[:, c * P:(c + 1) * P], r_cum[:, c * P:(c + 1) * P], r_negm[:, c:c + 1], None,
                                          ALU.add)
                link(ins)
                V.tensor_tensor(r_lw, r_cum, r_lw, ALU.subtract).then_inc(sem("s_rw_cc"), 1)
                link(V.tensor_scalar(kp, r_a, -1.0, vec("k_a", p), ALU.add, ALU.mult))
                link(V.scalar_tensor_tensor(kp, kp, 1.0, r_mix[:, 1, :], ALU.add, ALU.mult))
                V.scalar_tensor_tensor(rk, r_mix[:, 0, :], vec("r_k", p), kp, ALU.mult, ALU.mult)
                dve.wait_ge(sem("s_rw_nrm"), p + 1)
                link(V.tensor_scalar(r_tmp, r_tmp, 1e-12, None, ALU.max))
                link(V.reciprocal(r_tmp, r_tmp))
                link(V.tensor_tensor(kk, kk, r_tmp, ALU.mult))
                dve.wait_ge(sem("s_rw_exp"), p + 1)
                V.scalar_tensor_tensor(r_at, kk, -1.0, r_lw, ALU.mult, ALU.mult)
                link(V.tensor_tensor(r_tmp, kk, r_a, ALU.mult))
                V.tensor_tensor(r_bt, r_tmp, r_Pi, ALU.mult)
                V.tensor_tensor(r_kt, kp, r_Pi, ALU.mult)
                V.tensor_tensor(r_sc, r_P[:, P - 1:P], r_em[:, 1:2], ALU.mult)
                V.tensor_tensor(r_rt, r_mix[:, 0, :], r_P, ALU.mult).then_inc(sem("s_rw_ops"), 1)
                dve.wait_ge(sem("s_rw_A"), p + 1)
                for hd in range(2):
                    V.tensor_tensor(r_Aak[:, 2 * hd:2 * hd + 2, :], pm[:, hd, S:2 * S].rearrange("p (a b) -> p a b", a=2),
                                    bc(con("strict"), 2), ALU.mult)
                for hd in range(2):
                    dve.wait_ge(sem("s_rw_mR"), 2 * p + hd + 1)
                    ins = V.tensor_tensor(r_R[:, hd, :, :], pm[:, (2, 4)[hd], :].rearrange("p (a b) -> p a b", a=4),
                                          bc(con("incl"), 4), ALU.mult)
                ins.then_inc(sem("s_rw_R"), 1)
                solver(r_Al, r_X, r_Y, p)
                dve.wait_ge(sem("s_rw_mS"), p + 1)
                for hd in range(2):
                    rows = slice(64 * hd, 64 * hd + 64)
                    ins = V.tensor_scalar(r_S[rows, rows], pm[rows, 0, rows], r_sc[rows, :], None, ALU.mult)
                ins.then_inc(sem("s_rw_S"), 1)
                y_, yc = r_X[:, 2:4, :].rearrange("p a b -> p (a b)"), r_Y[:, 0:2, :].rearrange("p a b -> p (a b)")
                dve.wait_ge(sem("s_rw_yTo"), p + 1)
                dve.wait_ge(sem("s_rw_mean"), p + 1)
                V.scalar_tensor_tensor(yc, pm[:, 3, 0:S], -1.0 / 64, y_, ALU.mult, ALU.add).then_inc(sem("s_rw_yc"), 1)
                V.tensor_tensor(rk, pm[:, 3, S:2 * S], r_mix[:, 2, :], ALU.mult)
                dve.wait_ge(sem("s_rw_var"), p + 1)
                link(V.tensor_scalar(r_tmp, pm[:, 4, 0:S], 1.0 / 64, GN_EPS, ALU.mult, ALU.add))
                V.reciprocal(r_tmp, r_tmp).then_inc(sem("s_ho_rv"), 1)
                dve.wait_ge(sem("s_ho_rs"), p + 1)
                link(V.scalar_tensor_tensor(r_sq, yc, vec("lnw", p), r_tmp, ALU.mult, ALU.mult))
                link(V.scalar_tensor_tensor(r_sq, r_sq, vec("lnb", p), rk, ALU.add, ALU.add))
                V.tensor_tensor(r_sq, r_sq, r_g, ALU.mult).then_inc(sem("s_yf"), 1)
                dve.wait_ge(s_yhi, Y_RWKV + p)
                lower(y_lo[:, p + DSA_H, :], y_hi[:, p + DSA_H, :], r_sq, s_y)

            dve.wait_ge(s_zero, 6)
            chain.loop(RWKV_P, 16, rwkv)

            def wout(i):
                for j in range(3):
                    ahead(U_WOUT + j, i, 3)
                    dve.wait_ge(s_sub, 2 * (U_WOUT + j) + 2 + 6 * i)
                    V.tensor_tensor(x[:, 3 * i + j, :], x[:, 3 * i + j, :], gp[:, j, 0:S], ALU.add).then_inc(s_evac[j], 1)

            loop(dve, 5, wout)
            ahead(U_WOUT + 15)
            dve.wait_ge(s_sub, 2 * (U_WOUT + 15) + 2)
            V.tensor_tensor(x[:, 15, :], x[:, 15, :], gp[:, 0, 0:S], ALU.add).then_inc(s_evac[0], 1)

            norm(1, VEC["g_ffn"])

            def top(w, m, keep, list_out):
                for tt in range(NT):
                    ins = V.max(m[:, tt, :], w[:, tt, :])
                link(ins)
                if list_out is not None:
                    V.tensor_copy(list_out, m[:, :, 0])
                link(V.memset(m8b, -1.0))
                link(V.tensor_copy(m8b[:, :, 0:keep], m[:, :, 0:keep]))
                for tt in range(NT):
                    ins = V.match_replace(w16b[:, tt, :], m8b[:, tt, :], w[:, tt, :], -2.0)
                link(ins)

            def softmax4(src, n):
                link(V.reduce_max(g1v, src, AX))
                V.tensor_tensor(g4, src, g1v.unsqueeze(2).broadcast_to([P, NT, 4]), ALU.subtract).then_inc(sem("s_rt_d"), 1)
                dve.wait_ge(sem("s_rt_e"), n + 1)
                link(V.reduce_sum(gs, e4, AX))
                link(V.reciprocal(gr, gs))
                link(V.tensor_tensor(w16[:, :, 0:4], e4, gr.unsqueeze(2).broadcast_to([P, NT, 4]), ALU.mult))

            dve.wait_ge(sem("s_rt_lg"), 1)
            V.memset(comb, 0.0)
            V.memset(w16, -1.0)
            link(V.tensor_tensor(rl, pm[:, 1, 0:64].rearrange("p (a b) -> p a b", a=NT)[:, :, 0:20], bc(rbias[:, :], NT),
                                 ALU.add))
            softmax4(rl[:, :, 0:4], 0)
            top(w16, m8, 1, pg)
            link(V.tensor_scalar(oneh, w16b[:, :, 0:4], -2.0, None, ALU.is_equal))
            for g in range(NGRP):
                o = es if g == 0 else es2
                link(V.tensor_tensor(o, rl[:, :, 4 + EPG * g:4 + EPG * (g + 1)], oneh[:, :, g:g + 1].broadcast_to([P, NT, EPG]),
                                     ALU.mult))
                if g:
                    link(V.tensor_tensor(es, es, es2, ALU.add))
            softmax4(es, 1)
            top(w16, m8, 2, None)
            link(V.tensor_scalar(w4, w16b[:, :, 0:4], -2.0, None, ALU.is_equal))
            link(V.tensor_tensor(w4, w4, w16[:, :, 0:4], ALU.mult))
            link(V.tensor_tensor(gs, m8[:, :, 0], m8[:, :, 1], ALU.add))
            link(V.reciprocal(gr, gs))
            link(V.tensor_tensor(w4, w4, gr.unsqueeze(2).broadcast_to([P, NT, 4]), ALU.mult))
            link(V.tensor_tensor(w4, w4, pg.unsqueeze(2).broadcast_to([P, NT, 4]), ALU.mult))
            for g in range(NGRP):
                ins = V.tensor_tensor(comb[:, :, EPG * g:EPG * (g + 1)], w4, oneh[:, :, g:g + 1].broadcast_to([P, NT, EPG]),
                                      ALU.mult)
            ins.then_inc(sem("s_rt_comb"), 1)

            def select(e):
                V.tensor_scalar(csel[0:16, :], combT[0:16, :], c0[0:16, bass.ds(C0["ident"][0] + e, 1)], None,
                                ALU.mult).then_inc(sem("s_me_sel"), 1)

            def moe(e):
                for b in range(4):
                    ahead(U_MOE + 2 * b, e, 12)
                    ahead(U_MOE + 2 * b + 1, e, 12)
                    dve.wait_ge(sem("s_me_sg"), 4 * e + b + 1)
                    up = gp[:, 1, 0:S] if b % 2 == 0 else pm[:, 4, 0:S]
                    V.tensor_tensor(hef[:, b % 2, :], sg[:, b % 2, :], up, ALU.mult).then_inc(sem(f"s_me_pair{b % 2}"), 1)
                    dve.wait_ge(sem(f"s_me_pair{b % 2}"), 2 * e + b // 2 + 2)
                    if b == 0:
                        dve.wait_ge(sem("s_me_bc"), e + 1)
                    V.tensor_tensor(he2[:, b % 2, :], hef[:, b % 2, :], bce, ALU.mult).then_inc(sem("s_me_he2"), 1)
                    dve.wait_ge(sem("s_me_hhi"), 4 * e + b + 1)
                    lower(y_lo[:, b, :], y_hi[:, b, :], he2[:, b % 2, :], sem("s_me_he"))
                select(e + 1)
                for d in range(4):
                    ahead(U_MOE + 8 + d, e, 12)
                    dve.wait_ge(s_sub, 2 * (U_MOE + 8 + d) + 2 + 24 * e)
                    xs = x[:, 4 * d:4 * d + 4, :]
                    V.tensor_tensor(xs, xs, pm[:, 2 * (d % 2):2 * (d % 2) + 2, :].rearrange("p a (b c) -> p (a b) c", b=2),
                                    ALU.add).then_inc(sem(f"s_me_down{d % 2}"), 1)

            dve.wait_ge(sem("s_rt_cTo"), 1)
            for k in range(2):
                dve.sem_inc(sem(f"s_me_pair{k}"), 1)
                dve.sem_inc(sem(f"s_me_down{k}"), 1)
            select(0)
            loop(dve, NEXP, moe)

            norm(2, VEC["norm2"])
            dve.wait_ge(sem("s_hlo"), 12)
            ahead(U_AB)
            dve.wait_ge(s_evac[0], EV_DN[0])
            link(V.tensor_scalar(g_x[0:16, :], ab[0:16, :], vecs[0:16, VEC["dt_bias"]:VEC["dt_bias"] + 1], None, ALU.add))
            V.scalar_tensor_tensor(g_e[0:16, :], g_x[0:16, :], -1.0, g_x[0:16, :], ALU.mult, ALU.min).then_inc(sem("s_ab_x"), 1)
            dve.wait_ge(sem("s_ab_ln"), 1)
            link(V.scalar_tensor_tensor(g_s[0:16, :], g_x[0:16, :], 0.0, g_s[0:16, :], ALU.max, ALU.add))
            link(V.tensor_scalar(g_s[0:16, :], g_s[0:16, :], ea[0:16, :], -1.0, ALU.mult, ALU.mult))
            dve.wait_ge(s_zero, 7)
            for c in range(NT):
                ins = V.tensor_tensor_scan(gb[0:16, c * P:(c + 1) * P], ones[0:16, :], g_s[0:16, c * P:(c + 1) * P], 0.0,
                                           ALU.mult, ALU.add)
            link(ins)
            V.tensor_scalar(g_x[0:16, 0:P], gb[0:16, 0:P], -1.0, gb[0:16, P - 1:P], ALU.mult,
                            ALU.add).then_inc(sem("s_ab_cum"), 1)
            dve.wait_ge(sem("s_ab_T"), 1)
            V.tensor_copy(gtok, pm[:, 0, 0:S].rearrange("p (a b) -> p a b", a=NT)).then_inc(sem("s_ab_tokg"), 1)
            dve.wait_ge(sem("s_ab_tokg"), 1)
            V.tensor_scalar(nbeta, gtok[:, :, 32:48], -1.0, None, ALU.mult)
            dve.wait_ge(sem("s_ab_eg"), 1)
            V.tensor_scalar(neg_eg, egt, -1.0, None, ALU.mult).then_inc(sem("s_ab_tok"), 1)
            dve.wait_ge(sem("s_ab_tok"), 1)

            def delta(i):
                for j in range(6):
                    ahead(U_DN + j, i, 6)
                for v in range(2):
                    ins = V.tensor_scalar(n_gs[0:16, v, :], gb[0:16, :], c0[0:16, bass.ds(C0["ident"][0] + v + 2 * i, 1)], None,
                                          ALU.mult)
                ins.then_inc(sem("s_dn_gs"), 1)
                for k in range(3):
                    dve.wait_ge(s_evac[k], EV_DN[k] + 2 * i + 2)
                for tap in range(4):
                    for j in range(4):
                        w = vec("dn_conv", 16 * i + 4 * j + tap)
                        src = n_raw[:, j, tap:tap + S]
                        if tap == 0:
                            ins = V.tensor_scalar(n_qkv[:, j, :], src, w, None, ALU.mult)
                        else:
                            ins = V.scalar_tensor_tensor(n_qkv[:, j, :], src, w, n_qkv[:, j, :], ALU.mult, ALU.add)
                    if tap < 3:
                        link(ins)
                ins.then_inc(sem("s_dn_cv"), 1)
                dve.wait_ge(sem("s_dn_gb"), i + 1)
                for v in range(2):
                    for c in range(NT):
                        k = 2 * v + c
                        g = gtok[:, c, bass.ds(v + 2 * i, 1)]
                        V.tensor_scalar(n_E1[:, k, :], pm[:, 4, v * S + c * P:v * S + (c + 1) * P], g, 0.0, ALU.subtract, ALU.max)
                        ins = V.tensor_scalar(n_E2[:, k, :], pm[:, 4, v * S + c * P:v * S + (c + 1) * P], g, 0.0, ALU.subtract,
                                              ALU.min)
                ins.then_inc(sem("s_dn_D"), 1)
                dve.wait_ge(sem("s_qk_ss"), DSA_H + i + 1)
                link(V.tensor_scalar(n_rn, pm[:, 0, :], EPS, None, ALU.add))
                V.reciprocal(n_rn, n_rn).then_inc(sem("s_qk_rv"), 1)
                dve.wait_ge(sem("s_qk_rs"), DSA_H + i + 1)
                V.scalar_tensor_tensor(n_qkv[:, 0, :], n_qkv[:, 0, :], float(P ** -0.5), n_rn[:, 0:S], ALU.mult, ALU.mult)
                V.tensor_tensor(n_qkv[:, 1, :], n_qkv[:, 1, :], n_rn[:, S:2 * S], ALU.mult).then_inc(sem("s_dn_qk"), 1)
                dve.wait_ge(sem("s_dn_kk"), i + 1)
                dve.wait_ge(sem("s_dn_E1"), i + 1)
                for v in range(2):
                    for c in range(NT):
                        ins = V.scalar_tensor_tensor(n_A[:, 2 * v + c, :], pm[:, 3, c * P:(c + 1) * P],
                                                     nbeta[:, c, bass.ds(v + 2 * i, 1)], n_E1[:, 2 * v + c, :], ALU.mult, ALU.mult)
                ins.then_inc(sem("s_dn_A"), 1)
                dve.wait_ge(sem("s_dn_E2"), i + 1)
                for v in range(2):
                    ins = V.tensor_tensor(n_QK[:, 2 * v:2 * v + 2, :], pm[:, 3, S:2 * S].rearrange("p (a b) -> p a b", a=2),
                                          n_E2[:, 2 * v:2 * v + 2, :], ALU.mult)
                ins.then_inc(sem("s_dn_QK"), 1)
                dve.wait_ge(sem("s_dn_kT"), i + 1)
                dve.wait_ge(sem("s_dn_v"), i + 1)
                for v in range(2):
                    V.tensor_scalar(n_r0[:, v, :], n_v[:, 2 * v, :], gtok[:, 0, bass.ds(32 + v + 2 * i, 1)], None, ALU.mult)
                    ins = V.tensor_scalar(n_kd[:, v, :], pm[:, 2, 0:P], gtok[:, 0, bass.ds(64 + v + 2 * i, 1)], None, ALU.mult)
                ins.then_inc(sem("s_dn_kd"), 1)
                solver(n_Al, n_X, n_Y, i + RWKV_P)
                dve.wait_ge(sem("s_dn_mks"), i + 1)
                for v in range(2):
                    ins = V.scalar_tensor_tensor(n_r1[:, v, :], pm[:, 3, v * P:(v + 1) * P], neg_eg[:, 1, bass.ds(v + 2 * i, 1)],
                                                 n_v[:, 2 * v + 1, :], ALU.mult, ALU.add)
                link(ins)
                for v in range(2):
                    ins = V.tensor_scalar(n_r1[:, v, :], n_r1[:, v, :], gtok[:, 1, bass.ds(32 + v + 2 * i, 1)], None, ALU.mult)
                ins.then_inc(sem("s_dn_r1"), 1)
                dve.wait_ge(sem("s_dn_o"), i + 1)
                for v in range(2):
                    ins = V.scalar_tensor_tensor(n_o[:, 2 + v, :], pm[:, 3, S + v * P:S + (v + 1) * P],
                                                 egt[:, 1, bass.ds(v + 2 * i, 1)], n_o[:, 2 + v, :], ALU.mult, ALU.add)
                ins.then_inc(sem("s_dn_ot"), 1)
                dve.wait_ge(sem("s_dn_os"), i + 1)
                link(V.tensor_scalar(n_or, n_ss, 1.0 / P, EPS, ALU.mult, ALU.add))
                V.reciprocal(n_or, n_or).then_inc(sem("s_ho_rv"), 1)
                dve.wait_ge(sem("s_ho_rs"), RWKV_P + i + 1)
                for k in range(4):
                    ins = V.tensor_scalar(n_o[:, k, :], n_o[:, k, :], n_or[:, k:k + 1], None, ALU.mult)
                ins.then_inc(sem("s_dn_on"), 1)
                dve.wait_ge(sem("s_dn_oT"), i + 1)
                V.scalar_tensor_tensor(n_yf, pm[:, 4, :].rearrange("p (a b) -> p a b", a=2), vec("dn_norm"), n_z, ALU.mult,
                                       ALU.mult).then_inc(sem("s_yf"), 1)
                dve.wait_ge(s_yhi, Y_DN + i)
                lower(y_lo[:, bass.ds(2 * i, 2), :], y_hi[:, bass.ds(2 * i, 2), :], n_yf, s_y)

            dve.wait_ge(s_zero, 8)
            chain.loop(DN_H, 6, delta)

            def swa(i):
                for j in range(6):
                    ahead(U_SW + j, i, 6)
                for k in range(3):
                    dve.wait_ge(s_evac[k], EV_SW[k] + 2 * i + 2)
                dve.wait_ge(sem("s_at_rot"), DSA_H + i + 1)
                V.tensor_tensor(w_t1, w_raw, bc(con("cos_w"), 4), ALU.mult)
                link(V.tensor_tensor(w_t2, pm[:, 0:2, :].rearrange("p n (a b) -> p (n a) b", a=2), bc(con("sin_w"), 4), ALU.mult))
                V.tensor_tensor(w_qk, w_t1, w_t2, ALU.add).then_inc(sem("s_at_qk"), 1)
                dve.wait_ge(sem("s_at_vT"), DSA_H + i + 1)
                V.tensor_copy(w_v.rearrange("p a b -> p (a b)"), pm[:, 4, 0:S]).then_inc(sem("s_at_v"), 1)
                dve.wait_ge(sem("s_sw_sc"), 2 * i + 1)
                V.scalar_tensor_tensor(w_l0, pm[:, 0, 0:3 * P], float(P ** -0.5), con("bias0"), ALU.mult, ALU.add)
                dve.wait_ge(sem("s_sw_sc"), 2 * i + 2)
                link(V.scalar_tensor_tensor(w_l1, pm[:, 1:3, :].rearrange("p a b -> p (a b)")[:, 0:3 * S], float(P ** -0.5),
                                            con("bias1"), ALU.mult, ALU.add))
                V.reduce_max(w_nm[:, 0:1], w_l0, AX, negate=True)
                V.reduce_max(w_nm[:, 1:2], w_l1, AX, negate=True).then_inc(sem("s_at_nm"), 1)
                dve.wait_ge(sem("s_sw_ex"), i + 1)
                V.tensor_tensor(w_p0, w_l0[:, 0:P], w_l0[:, P:2 * P], ALU.add)
                V.tensor_tensor(w_p1, w_l1[:, 0:S], w_l1[:, S:2 * S], ALU.add)
                link(V.reciprocal(w_sum, w_sum))
                V.tensor_tensor(w_p0, w_p0, w_l0[:, 2 * P:3 * P], ALU.add)
                link(V.tensor_tensor(w_p1, w_p1, w_l1[:, 2 * S:3 * S], ALU.add))
                V.tensor_scalar(w_p0, w_p0, w_sum[:, 0:1], None, ALU.mult)
                V.tensor_scalar(w_p1, w_p1, w_sum[:, 1:2], None, ALU.mult).then_inc(sem("s_at_pr"), 1)
                dve.wait_ge(sem("s_at_o"), DSA_H + i + 1)
                V.tensor_tensor(w_yf, w_z, pm[:, 0, 0:S], ALU.mult).then_inc(sem("s_yf"), 1)
                dve.wait_ge(s_yhi, Y_SW + i)
                lower(y_lo[:, i + 16, :], y_hi[:, i + 16, :], w_yf, s_y)

            chain.loop(SW_H, 4, swa)

            def project(u0):
                def turn(i):
                    for s_ in range(6):
                        split(2 * u0 + RING + s_, i, 6)
                        if s_ % 3 == 2:
                            b = s_ // 3
                            dve.wait_ge(s_sub, 2 * u0 + s_ + 1 + 6 * i)
                            V.tensor_tensor(x[:, 2 * i + b, :], x[:, 2 * i + b, :], gp[:, b, 0:S], ALU.add).then_inc(s_evac[b], 1)
                return turn

            loop(dve, 8, project(U_HOUT))

            norm(3, VEC["norm2"] + KT)
            dve.wait_ge(s_zero, 9)

            def shortconv(i):
                for n in range(12):
                    bb, j, k = n // 4, n % 4, n % 3
                    ahead(U_SC + n, i, 12)
                    if j == 2:
                        kc = (n - 1) % 3
                        dve.wait_ge(s_evac[kc], EV_SC[kc] + (n - 1) // 3 + 1 + 4 * i)
                        dve.wait_ge(s_sub, 2 * (U_SC + n) + 2 + 24 * i)
                        V.tensor_tensor(q_cu[:, bb, 2:S + 2], q_c[:, bb, :], gp[:, k, 0:S], ALU.mult).then_inc(s_evac[k], 1)
                    if j == 3:
                        ku = (n - 1) % 3
                        dve.wait_ge(s_evac[ku], EV_SC[ku] + (n - 1) // 3 + 1 + 4 * i)
                        w = 9 * i + 3 * bb
                        link(V.tensor_scalar(q_a[:, bb, :], q_cu[:, bb, 0:S], vec("sc_conv", w), None, ALU.mult))
                        for tap in (1, 2):
                            link(V.scalar_tensor_tensor(q_a[:, bb, :], q_cu[:, bb, tap:tap + S], vec("sc_conv", w + tap),
                                                        q_a[:, bb, :], ALU.mult, ALU.add))
                        link(V.tensor_tensor(q_a[:, bb, :], q_a[:, bb, :], q_b[:, bb, :], ALU.mult))
                        dve.wait_ge(s_evac[k], EV_SC[k] + n // 3 + 1 + 4 * i)
                        V.tensor_tensor(q_a[:, bb, :], q_a[:, bb, :], q_z[:, bb, :], ALU.mult).then_inc(sem("s_sc_y"), 1)
                        dve.wait_ge(s_yhi, Y_SC + bb + 3 * i)
                        lower(y_lo[:, 3 * i + bb, :], y_hi[:, 3 * i + bb, :], q_a[:, bb, :], s_y)

            chain.loop(8, 12, shortconv)
            out_turn = project(U_SOUT)
            loop(dve, 7, out_turn)
            out_turn(7)
            norm(4, VEC["final"], last=True)


def _constants():
    idx = np.arange(P)
    t, s = idx[:, None], idx[None, :]
    levels = [((t // (2 * b) == s // (2 * b)) & ((t // b) % 2 == 1) & ((s // b) % 2 == 0)) for b in (1, 2, 4, 8, 16, 32, 64)]
    c0 = {"ident": np.eye(P), "levels": np.concatenate(levels, 1), "incl": t <= s, "strict": t < s}

    def swap(size, half):
        m = np.zeros((P, P))
        for b in range(0, P, size):
            for k in range(half):
                m[b + half + k, b + k] = -1
                m[b + k, b + half + k] = 1
        return m

    def angles(theta, dim, half):
        inv = np.float32(theta) ** (-np.arange(half, dtype=np.float32) * np.float32(2.0 / dim))
        a = np.arange(S, dtype=np.float32)[None, :] * inv.astype(np.float32)[:, None]
        return np.cos(a), np.sin(a)

    cq, sq = angles(10000.0, 128, 64)
    ci, si = angles(10000.0, 64, 32)
    cw, sw = angles(500000.0, 32, 16)
    c1 = {"heads": (t // 64) == (s // 64), "perm_q": swap(128, 64), "perm_i": swap(64, 32), "cos_q": np.tile(cq, (2, 1)),
          "sin_q": np.tile(sq, (2, 1)), "cos_i": np.tile(ci, (4, 1)), "sin_i": np.tile(si, (4, 1))}
    cos_w, sin_w = np.ones((P, S)), np.zeros((P, S))
    cos_w[0:32], sin_w[0:32] = np.tile(cw, (2, 1)), np.tile(sw, (2, 1))

    def window(q0, keys):
        d = (q0 + idx)[:, None] - np.arange(keys)[None, :]
        ok = [(d >= 0) & (d <= 128), (d >= 0) & (d % 4 == 0), (d >= 0) & (d % 16 == 0)]
        return np.concatenate([np.where(o, 0.0, -BIG) for o in ok], 1)

    c2 = {"perm_w": swap(128, 16), "cos_w": cos_w, "sin_w": sin_w, "bias0": window(0, P), "bias1": window(P, S)}

    def pack(values, order):
        return np.concatenate([np.asarray(values[n], np.float32) for n, _ in order], 1)

    return pack(c0, _C0), pack(c1, _C1), pack(c2, _C2)


def _blocks(w):
    k, n = w.shape
    return w.reshape(k // P, P, n // P, P).transpose(2, 1, 0, 3)


def _wide(*cols):
    w = np.concatenate(cols, 1)
    return np.concatenate([w, np.zeros((w.shape[0], P - w.shape[1]), w.dtype)], 1)


def _stream(a):
    out = np.empty((N_UNITS, P, UNIT * P), np.float32)
    w = a["w_in"][0]
    q, k, v, qi, ki, wi = np.split(w[:, :4176], np.cumsum([1024, 1024, 1024, 1024, 64]), 1)
    r, dw, kr, vr, da, dg = np.split(w[:, 4176:], np.cumsum([1024, 64, 1024, 1024, 64]), 1)

    def put(u, blocks, step=1):
        n = blocks.shape[0]
        out[u:u + step * (n - 1) + 1:step] = blocks.reshape(n, P, UNIT * P)

    put(U_PRO, _blocks(np.concatenate([_wide(ki, ki), _wide(dg[:, 128:], wi), _wide(dw, da), dg[:, :128], qi], 1)))
    for j, m in enumerate((q, k, v)):
        put(U_DSA + j, _blocks(m), 3)
    for j, m in enumerate((r, kr, vr)):
        put(U_RWKV + j, _blocks(m), 3)
    put(U_WOUT, _blocks(a["w_out"][0]))
    for e in range(NEXP):
        u = U_MOE + 12 * e
        put(u, _blocks(a["w_e_gate"][0, e]), 2)
        put(u + 1, _blocks(a["w_e_up"][0, e]), 2)
        d = _blocks(a["w_e_down"][0, e])
        out[u + 8:u + 12] = d.reshape(4, 4, P, 4 * P).transpose(0, 2, 1, 3).reshape(4, P, UNIT * P)
    w = a["hyb_w_in_2"][0]
    aq, ak, av, az, ab, aa, bq, bk, bv, bz = np.split(
        w, np.cumsum([1024, 1024, 2048, 2048, 16, 16, 3072, 1024, 1024]), 1)
    gap = np.zeros((D, 16), np.float32)
    put(U_AB, _blocks(_wide(aa, gap, ab)))
    put(U_DN, _blocks(aq), 6)
    put(U_DN + 1, _blocks(ak), 6)
    for h in range(2):
        put(U_DN + 2 + h, _blocks(av)[h::2], 6)
        put(U_DN + 4 + h, _blocks(az)[h::2], 6)
    for g in range(3):
        put(U_SW + g, _blocks(bq)[8 * g:8 * g + 8], 6)
    for j, m in enumerate((bk, bv, bz)):
        put(U_SW + 3 + j, _blocks(m), 6)

    def tall(u, w):
        b = _blocks(w).transpose(0, 2, 1, 3).reshape(-1, UNIT, P, P)
        out[u:u + b.shape[0]] = b.transpose(0, 2, 1, 3).reshape(-1, P, UNIT * P)

    tall(U_HOUT, a["hyb_w_out_2"][0])
    for j, m in enumerate(np.split(a["sc_w_in_2"][0], 4, 1)):
        put(U_SC + j, _blocks(m), 4)
    tall(U_SOUT, a["sc_w_out_2"][0])
    return out


def _vectors(a):
    def cols(v):
        return np.reshape(v, (-1, P)).T

    def padded(v):
        return np.concatenate([v, np.zeros(P - v.size, np.float32)])[:, None]

    mu = a["rwkv_shift_mix"][0]
    dc = a["dn_conv_w_2"][0].reshape(32, P, 4)
    dn = np.concatenate([dc[b] for i in range(8) for b in (i, 8 + i, 16 + 2 * i, 17 + 2 * i)], 1)
    sc = a["sc_conv_w_2"][0].reshape(24, P, 3).transpose(1, 0, 2).reshape(P, 72)
    got = {
        "g_mix": cols(a["g_mix"][0]), "g_ffn": cols(a["g_ffn"][0]), "norm2": cols(a["norm_w_2"]), "final": cols(a["final_norm_w_2"]),
        "mu": np.concatenate([cols(mu[0:1024]), cols(mu[1088:2112]), cols(mu[2112:3136])], 1),
        "mu_dwda": np.concatenate([mu[1024:1088], mu[3136:3200]])[:, None], "mu_dg1": mu[3200:3328][:, None],
        "mu_dg2": padded(mu[3328:3360]), "w0": cols(a["w0"][0]), "a0": cols(a["a0"][0]), "k_k": cols(a["k_k"][0]),
        "k_a": cols(a["k_a"][0]), "r_k": cols(a["r_k"][0]), "lnw": cols(a["ln_x_w"][0]), "lnb": cols(a["ln_x_b"][0]),
        "q_gain": cols(a["q_gain"][0]), "k_gain": cols(a["k_gain"][0]), "dn_norm": cols(a["dn_norm_w_2"][0]),
        "dn_conv": dn, "sc_conv": sc, "a_log": padded(a["dn_a_log_2"][0]), "dt_bias": padded(a["dn_dt_bias_2"][0]),
    }
    return np.ascontiguousarray(np.concatenate([got[n] for n, _ in _VEC], 1))


def _lora(a):
    g = a["w_gate_lora_up"][0]
    wa = np.concatenate([a["w_decay_up"][0], a["w_aicl_up"][0]], 0)
    g2 = np.concatenate([g[128:], np.zeros((96, g.shape[1]), np.float32)], 0)
    return np.ascontiguousarray(np.stack([np.concatenate([m[:, P * p:P * (p + 1)] for m in (wa, g[:128], g2)], 1)
                                          for p in range(RWKV_P)]))


def _arrays(a):
    c0, c1, c2 = _constants()
    route = np.concatenate([a["w_route_group"][0], a["w_route_expert"][0]], 1).reshape(KT, P, 20).transpose(1, 0, 2)
    rb = np.concatenate([a["b_route_group"][0], a["b_route_expert"][0]])
    return {
        "stream": _stream(a), "x": np.ascontiguousarray(a["x"][0].T.reshape(KT, P, S).transpose(1, 0, 2)),
        "vecs": _vectors(a), "c0": c0, "c1": c1, "c2": c2, "lora": _lora(a), "route": np.ascontiguousarray(route),
        "rbias": np.ascontiguousarray(np.broadcast_to(rb, (P, 20))),
    }


def kernel(**inputs):
    import concourse.bacc as bacc
    from concourse.bass_utils import run_bass_kernel_spmd

    nc = bacc.Bacc("TRN2", target_bir_lowering=False, num_devices=1)
    arrays, args = {}, []
    for name, v in _arrays({k: np.asarray(v) for k, v in inputs.items()}).items():
        arrays[f"in_{name}"] = v
        args.append(nc.dram_tensor(f"in_{name}", v.shape, mybir.dt.from_np(v.dtype), kind="ExternalInput").ap())
    out = nc.dram_tensor("out_0", (P, KT, S), F32, kind="ExternalOutput").ap()
    program(nc, *args, out)
    got = run_bass_kernel_spmd(nc, [arrays], core_ids=[0]).results[0]["out_0"]
    return np.ascontiguousarray(got.transpose(1, 0, 2).reshape(D, S).T)[None]
```

```python
import numpy as np
import concourse.bass as bass
from concourse import mybir
from concourse.alu_op_type import AluOpType as ALU
from contextlib import ExitStack

F32 = mybir.dt.float32
F32R = mybir.dt.float32r
ACT = mybir.ActivationFunctionType
AX = mybir.AxisListType.X

P = 128
S = 256
D = 2048
KT = D // P
NT = S // P
UNIT = 16
SUB = 8
RING = 3
NEXP, NGRP, EPG, DEXP = 16, 4, 4, 512
DSA_H, IDX_H, RWKV_P, DN_H, SW_H = 8, 16, 8, 8, 8
TOPK = 64
EPS = 1e-6
GN_EPS = 64e-5
ARENA = 11900
NEG, MARK, BIG = -3.0e38, -3.3e38, 1.0e30

U_PRO = 0
U_RW0 = U_PRO + 4 + IDX_H // 2
U_T1 = U_RW0 + 6
U_WOUT = U_T1 + 6 * RWKV_P - 6
U_MOE = U_WOUT + KT
U_TM = U_MOE + 2
U_AB = U_MOE + 12 * NEXP
U_DN0 = U_AB + 1
U_T2 = U_DN0 + 6
U_HOUT = U_T2 + 12 * DN_H - 6
U_SC = U_HOUT + 24
U_SOUT = U_SC + 96
N_UNITS = U_SOUT + 24
N_SUBS = 2 * N_UNITS

_VEC = [("g_mix", 16), ("g_ffn", 16), ("norm2", 32), ("final", 16), ("mu", 24), ("mu_dwda", 1), ("mu_dg1", 1),
        ("mu_dg2", 1), ("w0", 8), ("a0", 8), ("k_k", 8), ("k_a", 8), ("r_k", 8), ("lnw", 8), ("lnb", 8),
        ("q_gain", 1), ("k_gain", 1), ("dn_norm", 1), ("dn_conv", 128), ("sc_conv", 72), ("a_log", 1), ("dt_bias", 1)]
VEC = {}
NVEC = 0
for _n, _w in _VEC:
    VEC[_n] = NVEC
    NVEC += _w

_C0 = [("ident", P), ("levels", 7 * P), ("incl", P), ("strict", P)]
_C1 = [("heads", P), ("perm_q", P), ("perm_i", P), ("cos_q", S), ("sin_q", S), ("cos_i", S), ("sin_i", S)]
_C2 = [("perm_w", P), ("cos_w", S), ("sin_w", S), ("bias0", 3 * P), ("bias1", 3 * S)]


def _columns(parts):
    at, out = 0, {}
    for name, width in parts:
        out[name] = (at, width)
        at += width
    return out, at


C0, N0 = _columns(_C0)
C1, N1 = _columns(_C1)
C2, N2 = _columns(_C2)


def program(nc, stream, x_in, vecs_in, c0_in, c1_in, c2_in, lora_in, route_in, rbias_in, out):
    ctx = ExitStack()
    with ctx:
        def sb(name, shape, dt=F32):
            return ctx.enter_context(nc.sbuf_tensor(name, shape, dt))

        sems = {}

        def sem(name):
            if name not in sems:
                sems[name] = ctx.enter_context(nc.semaphore(name))
            return sems[name]

        stage = sb("stage", [P, RING, UNIT * P])
        w_hi = sb("w_hi", [P, RING, SUB * P], F32R)
        w_lo = sb("w_lo", [P, RING, SUB * P], F32R)
        x = sb("x", [P, KT, S])
        h_hi = sb("h_hi", [P, KT, S], F32R)
        h_lo = sb("h_lo", [P, KT, S], F32R)
        y_hi = sb("y_hi", [P, 24, S], F32R)
        y_lo = sb("y_lo", [P, 24, S], F32R)
        vecs = sb("vecs", [P, NVEC])
        c0 = sb("c0", [P, N0])
        c12 = sb("c12", [P, max(N1, N2)])
        ones = sb("ones", [P, P])
        route = sb("route", [P, KT, 20])
        rbias = sb("rbias", [P, 20])
        arena = sb("arena", [P, ARENA])

        gp = ctx.enter_context(nc.psum_tensor("gp", [P, 3, 512], F32))
        pm = ctx.enter_context(nc.psum_tensor("pm", [P, 5, 512], F32))

        def con(name):
            for table, t in ((C0, c0), (C1, c12), (C2, c12)):
                if name in table:
                    at, width = table[name]
                    return t[:, at:at + width]

        def vec(name, k=0, n=1):
            return vecs[:, bass.ds(VEC[name] + k, n)] if not isinstance(k, int) else \
                vecs[:, VEC[name] + k:VEC[name] + k + n]

        ident = con("ident")
        levels = con("levels").rearrange("p (l c) -> p l c", l=7)

        def areas(start, parts):
            at, got = start, []
            for shape in parts:
                n = 1
                for d in shape:
                    n *= d
                v = arena[:, at:at + n]
                if len(shape) == 2:
                    v = v.rearrange("p (a b) -> p a b", a=shape[0])
                elif len(shape) == 3:
                    v = v.rearrange("p (a b c) -> p a b c", a=shape[0], b=shape[1])
                got.append(v)
                at += n
            assert at <= ARENA, at
            return got, at

        s_load, s_c2 = sem("s_load"), sem("s_c2")
        s_x = [sem(f"s_x{q}") for q in range(4)]
        s_stage = [sem(f"s_stage{k}") for k in range(RING)]
        s_hi, s_lo = sem("s_hi"), sem("s_lo")
        s_sub = sem("s_sub")
        s_evac = [sem(f"s_evac{k}") for k in range(3)]
        s_dv, s_ac = sem("s_dv_chain"), sem("s_ac_chain")
        s_zero = sem("s_zero")
        s_yhi, s_y = sem("s_yhi"), sem("s_y")

        def plus(ev, *more):
            return [a + b for a, b in zip(ev, more)]

        EV_PRO = [0, 0, 0]
        EV_RW0 = plus(EV_PRO, 4, 4, 4)
        EV_T1 = plus(EV_RW0, 2, 2, 2)
        EV_WOUT = plus(EV_T1, *[2 * RWKV_P - 2] * 3)
        EV_AB = plus(EV_WOUT, 6, 5, 5)
        EV_DN0 = plus(EV_AB, 1, 0, 0)
        EV_T2 = plus(EV_DN0, 2, 2, 2)
        EV_HOUT = plus(EV_T2, *[4 * DN_H - 2] * 3)
        EV_SC = plus(EV_HOUT, 8, 8, 0)
        EV_SOUT = plus(EV_SC, 32, 32, 32)
        Y_T1, Y_T2, Y_SC = 1, 17, 33
        SUMMED = [8, 15, 12, 15, 15]
        ACC = [sum(SUMMED[:n]) - n for n in range(6)]
        LOADS = 4

        def loop(eng, n, body):
            with eng.Fori(0, n) as i:
                body(i)

        class Chain:

            def __init__(self, eng, s):
                self.eng, self.s, self.base, self.k, self.at = eng, s, 0, 0, None

            def link(self, ins):
                self.k += 1
                ins.then_inc(self.s, 1)
                self.eng.wait_ge(self.s, self.base + self.k if self.at is None else self.at + self.k)

            def loop(self, n, links, body):
                start = self.base + self.k
                with self.eng.Fori(0, n) as i:
                    self.at, self.k = start + links * i, 0
                    body(i)
                    assert self.k == links, self.k
                self.at, self.k, self.base = None, 0, start + links * n

            def turn(self, links, body, i):
                k = self.k
                body(i)
                assert self.k - k == links, self.k - k

        (notsel, tanh_a, sig1, sig2), L1 = areas(0, [(NT, S), (S,), (S,), (S,)])
        (kraw, misc, dwda, dg1, mixd, qraw, t_1, t_2, krope, qrope, relu, isc, wtok, top8), _ = areas(
            L1, [(S,), (S + 1,), (S + 1,), (S + 1,), (S,), (2, S), (S,), (S,), (S,), (2, S), (2, 512), (NT, S), (NT, 16),
                 (NT, 8)])
        (r_raw, d_raw, r_S, r_lora), _ = areas(ARENA - 2051, [(3, S + 1), (3, S), (P,), (3 * P,)])
        (r_mix, r_D, r_lw, r_cum, r_P, r_Pi, r_a, r_g, r_sq, r_tmp, r_at, r_bt, r_kt, r_rt, r_tok, r_Aak, r_R,
         r_negm, r_em, r_sc, r_A, r_X), r_end = areas(
            L1, [(3, S), (3, S), (S,), (S,), (S,), (S,), (S,), (S,), (S,), (S,), (S,), (S,), (S,), (S,),
                 (4, P), (4, P), (2, 4, P), (NT,), (NT,), (1,), (4, P), (4, P)])
        (r_Y,), r_end = areas(r_end, [(4, P)])
        assert r_end <= ARENA - 2051
        lw0 = L1 + 6 * S
        r_rhs, r_U = [v.rearrange("p (c t) -> p c t", c=NT) for v in (r_bt, r_kt)]
        (r_T, r_al0), _ = areas(lw0, [(4, P), (4, P)])
        (r_al1,), _ = areas(lw0 + 6 * S, [(4, P)])
        r_Al = [r_al0, r_al1]
        head = sb("head", [P, 2 * S + 4])
        d_sq = d_rs = head[:, 0:2 * S]
        d_qk = d_rs.rearrange("p (a b) -> p a b", a=2)
        d_nm, d_sum = head[:, 2 * S:2 * S + NT], head[:, 2 * S + NT:2 * S + 2 * NT]
        ci = C1["cos_i"][0]
        d_qn = d_pT = c12[:, ci:ci + 2 * S].rearrange("p (a b) -> p a b", a=2)
        d_t1 = d_lg = r_D[:, 0:2, :]
        bt0 = L1 + 6 * S + 9 * S
        d_t2 = d_pr = arena[:, bt0:bt0 + 2 * S].rearrange("p (a b) -> p a b", a=2)
        d_v = r_mix[:, 1:2, :].rearrange("p a (b c) -> p (a b) c", b=NT)
        (hf, n_rs), _ = areas(0, [(KT, S), (S,)])
        (rl, g1v, g4, gs, gr, w16, w16b, m8, m8b, pg, oneh, es, es2, e4, w4, comb, combT, csel, bce, sg, hef, he2), _ = areas(
            KT * S + S, [(NT, 20), (NT,), (NT, 4), (NT,), (NT,), (NT, 16), (NT, 16), (NT, 8), (NT, 8), (NT,), (NT, 4),
                         (NT, 4), (NT, 4), (NT, 4), (NT, 4), (NT, P), (S,), (S,), (S,), (2, S), (2, S), (2, S)])
        (ab, g_x, g_e, g_s, gb, gtok, nbeta, egt, neg_eg, ea), L2 = areas(
            0, [(S,), (S,), (S,), (S,), (S,), (NT, P), (NT, 16), (NT, 16), (NT, 16), (1,)])
        (n_qkv, n_sq, n_rn, n_v, n_kd, n_gs, n_E1, n_E2, n_A, n_QK, n_X, n_Y, n_r0, n_r1, n_S, n_ss, n_or), n_end = areas(
            L2, [(4, S), (512,), (512,), (4, P), (2, P), (2, S), (4, P), (4, P), (4, P), (4, P), (4, P),
                 (4, P), (2, P), (2, P), (2, P), (4,), (4,)])
        (n_o,), _ = areas(n_end - 8 - 6 * P, [(4, P)])
        n_vn = n_gs.rearrange("p v (c t) -> p (v c) t", c=NT)
        assert n_end <= ARENA - 3084
        (n_raw, n_z, w_raw, w_v0, w_z), _ = areas(ARENA - 3084, [(4, S + 3), (2, S), (4, S), (S,), (S,)])
        n_at = L2 + 4 * S
        (n_al0, n_al1), _ = areas(n_at, [(4, P), (4, P)])
        n_Al = [n_al0, n_al1]
        n_T = n_E1
        n_yf = n_E2[:, :, :].rearrange("p (h c) t -> p h (c t)", h=2)
        (w_t1, w_t2, w_qk, w_v, w_l0, w_l1, w_p0, w_p1, w_pT, w_nm, w_sum, w_yf), w_end = areas(
            L2, [(4, S), (4, S), (4, S), (NT, P), (3 * P,), (3 * S,), (P,), (S,), (3, P), (NT,), (NT,), (S,)])
        assert w_end <= ARENA - 3084
        (q_b, q_c, q_cu, q_z, q_a), _ = areas(0, [(3, S), (3, S), (3, S + 2), (3, S), (3, S)])

        solve = [sem(f"s_solve_{n}") for n in ("level", "t1", "t1_out", "dy", "dx", "y", "x")]
        s_al, s_t1, s_t1o, s_dy, s_dx, s_sy, s_sx = solve

        block = ctx.enter_context(nc.Block())

        @block.sync
        def _(sp):
            for q in range(4):
                sp.dma_start(x[:, 4 * q:4 * q + 4, :], x_in[:, 4 * q:4 * q + 4, :]).then_inc(s_x[q], 16)
            for u in range(RING):
                sp.dma_start(stage[:, u, :], stream[u]).then_inc(s_stage[u], 16)
            turns = (N_UNITS - RING) // RING
            with sp.Fori(0, turns) as t:
                for k in range(RING):
                    sp.wait_ge(s_lo, 2 * RING * t + 2 * k + 2)
                    sp.dma_start(stage[:, k, :], stream[RING * t + (RING + k)]).then_inc(s_stage[k], 16)
            for u in range(RING + turns * RING, N_UNITS):
                sp.wait_ge(s_lo, 2 * (u - RING) + 2)
                sp.dma_start(stage[:, u % RING, :], stream[u]).then_inc(s_stage[u % RING], 16)
            for q in range(4):
                sp.wait_ge(sem("s_hf"), 4 * 4 + q + 1)
                sp.dma_start(out[:, 4 * q:4 * q + 4, :], hf[:, 4 * q:4 * q + 4, :]).then_inc(sem("s_out"), 16)
            sp.wait_ge(sem("s_out"), 16 * 4)

        @block.gpsimd
        def _(pool):
            G = nc.gpsimd
            G.memset(ones[:, :], 1.0).then_inc(s_zero, 1)

            def sum_blocks(n, m, at):
                pool.wait_ge(sem("s_sq"), KT * n + 2)
                G.tensor_tensor(n_rs, hf[:, 0, :], hf[:, 1, :], ALU.add).then_inc(sem("s_acc"), 1)
                with pool.Fori(2, m) as k:
                    pool.wait_ge(sem("s_sq"), KT * n + 1 + k)
                    pool.wait_ge(sem("s_acc"), at - 1 + k)
                    G.tensor_tensor(n_rs, n_rs, hf[:, bass.ds(k, 1), :].rearrange("p a b -> p (a b)"),
                                    ALU.add).then_inc(sem("s_acc"), 1)

            sum_blocks(0, SUMMED[0], ACC[0])
            pool.wait_ge(sem("s_hlo"), 4)
            for v in (misc, dwda, dg1):
                G.memset(v[:, 0:1], 0.0).then_inc(s_zero, 1)

            G.memset(r_raw[:, :, 0:1], 0.0).then_inc(s_zero, 1)
            G.memset(r_S[:, :], 0.0).then_inc(s_zero, 1)

            def level_masks(A, Al, it):
                for lv in range(7):
                    if lv == 2:
                        pool.wait_ge(s_sx, 6 * it + 1)
                    if lv >= 2:
                        pool.wait_ge(s_t1, 7 * it + lv - 1)
                    G.tensor_tensor(Al[lv % 2], A, levels[:, lv, :].unsqueeze(1).broadcast_to([P, 4, P]),
                                    ALU.mult).then_inc(s_al, 1)

            def feed(n, i, u0, per):
                sub = 2 * u0 + n + 2
                pool.wait_ge(s_hi, sub + 1 + 2 * per * i)
                G.tensor_tensor(w_lo[:, sub % RING, :], stage[:, (sub // 2) % RING, (sub % 2) * SUB * P:(sub % 2 + 1) * SUB * P],
                                w_hi[:, sub % RING, :].bitcast(F32), ALU.subtract).then_inc(s_lo, 1)

            def feed1(n, i, last):
                if not last:
                    feed(n, i, U_T1, 6)

            def rwkv(p, last=False):
                for n in range(5):
                    feed1(n, p, last)
                pool.wait_ge(sem("s_rw_A"), p + 1)
                level_masks(r_A, r_Al, p)
                if not last:
                    pool.dma_start(r_lora, lora_in[p + 1]).then_inc(sem("s_rw_lw"), 16)
                    pool.wait_ge(s_lo, 2 * U_T1 + 10 + 12 * p)
                for n in range(8, 12):
                    feed1(n, p, last)

            pool.dma_start(r_lora, lora_in[0]).then_inc(sem("s_rw_lw"), 16)
            pool.wait_ge(s_lo, 2 * U_T1 + 2)
            loop(pool, RWKV_P - 1, rwkv)
            rwkv(RWKV_P - 1, True)

            pool.wait_ge(s_y, Y_T2)
            pool.dma_start(c12[:, 0:N2], c2_in).then_inc(s_c2, 16)

            sum_blocks(1, SUMMED[1], ACC[1])
            sum_blocks(2, SUMMED[2], ACC[2])
            pool.wait_ge(sem("s_hlo"), 12)
            G.memset(gb, 0.0).then_inc(s_zero, 1)
            G.memset(n_raw[:, :, 0:3], 0.0).then_inc(s_zero, 1)

            def turn2(i, last=False):
                for n in range(5):
                    feed(n, i, U_T2, 12)
                pool.wait_ge(sem("s_dn_E"), i + 1)
                G.tensor_tensor(n_E2, n_E2, con("incl").unsqueeze(1).broadcast_to([P, 4, P]),
                                ALU.mult).then_inc(sem("s_dn_E2"), 1)
                for n in range(5, 7):
                    feed(n, i, U_T2, 12)
                pool.wait_ge(sem("s_dn_A"), i + 1)
                level_masks(n_A, n_Al, i + RWKV_P)
                if not last:
                    pool.wait_ge(s_lo, 2 * U_T2 + 14 + 24 * i)
                    for n in range(12, 24):
                        feed(n, i, U_T2, 12)

            pool.wait_ge(s_lo, 2 * U_T2 + 2)
            loop(pool, DN_H - 1, turn2)
            turn2(DN_H - 1, True)
            sum_blocks(3, SUMMED[3], ACC[3])
            pool.wait_ge(s_evac[0], EV_SC[0])
            pool.wait_ge(s_evac[1], EV_SC[1])
            pool.wait_ge(sem("s_hlo"), 4 * 4)
            G.memset(q_cu[:, :, 0:2], 0.0).then_inc(s_zero, 1)
            sum_blocks(4, SUMMED[4], ACC[4])

        @block.tensor
        def _(pe):
            T = nc.tensor

            def half(out_ap, sub, i, step, hi, lo, kts, first, last, tiles=(0, SUB)):
                slot = sub % RING
                if tiles[0] == 0:
                    pe.wait_ge(s_lo, sub + 1 + step * i)
                for t in range(*tiles):
                    w = slice(t * P, (t + 1) * P)
                    o, k = out_ap[t] if isinstance(out_ap, list) else out_ap, kts[t]
                    T.matmul(o, w_hi[:, slot, w], hi[:, k, :], start=first[t], stop=False)
                    T.matmul(o, w_hi[:, slot, w], lo[:, k, :], start=False, stop=False)
                    ins = T.matmul(o, w_lo[:, slot, w], hi[:, k, :], start=False, stop=last[t])
                if tiles[1] == SUB:
                    ins.then_inc(s_sub, 1)

            def unit(k, u, i, step, hi, lo):
                for hf_ in range(2):
                    half(gp[:, k, 0:S], 2 * u + hf_, i, 2 * step, hi, lo, [SUB * hf_ + t for t in range(SUB)],
                         [hf_ == 0 and t == 0 for t in range(SUB)], [hf_ == 1 and t == SUB - 1 for t in range(SUB)])

            def feed(n, i, u0, per, ev, tiles=(0, SUB)):
                j = n // 2
                k, first = j % 3, n % 2 == 0
                if first and tiles[0] == 0:
                    pe.wait_ge(s_evac[k], ev[k] + per // 3 * i + j // 3)
                half(gp[:, k, 0:S], 2 * u0 + n, i, 2 * per, h_hi, h_lo, [SUB * (n % 2) + t for t in range(SUB)],
                     [first and t == 0 for t in range(SUB)], [not first and t == SUB - 1 for t in range(SUB)], tiles)

            def norm_sum(n):
                pe.wait_ge(sem("s_acc"), ACC[n + 1])
                T.matmul(pm[:, 4, 0:S], ones[:, :], n_rs, start=True, stop=False)
                for k in range(SUMMED[n], KT):
                    pe.wait_ge(sem("s_sq"), KT * n + k + 1)
                    ins = T.matmul(pm[:, 4, 0:S], ones[:, :], hf[:, k, :], start=False, stop=k == KT - 1)
                ins.then_inc(sem("s_nsum"), 1)

            def first_unit(k, u, n):
                for hf_ in range(2):
                    pe.wait_ge(sem("s_hlo"), 4 * n + 2 * hf_ + 2)
                    half(gp[:, k, 0:S], 2 * u + hf_, 0, 0, h_hi, h_lo, [SUB * hf_ + t for t in range(SUB)],
                         [hf_ == 0 and t == 0 for t in range(SUB)], [hf_ == 1 and t == SUB - 1 for t in range(SUB)])

            def transposes(pairs, s):
                for o, i_ in pairs:
                    ins = T.transpose(o, i_, ident)
                ins.then_inc(s, 1)

            def inverse(Al, X, Y, Tt, it, between, after=None):
                for lv in range(7):
                    pe.wait_ge(s_al, 7 * it + lv + 1)
                    if lv:
                        pe.wait_ge(s_sy, 7 * it + lv)
                    for s_ in range(4):
                        ins = T.matmul(pm[:, 0, s_ * P:(s_ + 1) * P], Al[lv % 2][:, s_, :], ident if lv == 0 else Y[:, s_, :],
                                       start=True, stop=True)
                    ins.then_inc(s_t1, 1)
                    if lv == 0:
                        continue
                    between(lv)
                    pe.wait_ge(s_t1o, 6 * it + lv)
                    pe.wait_ge(s_sx, 6 * it + lv)
                    for s_ in range(4):
                        ins = T.matmul(pm[:, 1, s_ * P:(s_ + 1) * P], X[:, s_, :], Tt[:, s_, :], start=True, stop=True)
                    ins.then_inc(s_dy, 1)
                    if lv < 6:
                        for s_ in range(4):
                            ins = T.matmul(pm[:, 2, s_ * P:(s_ + 1) * P], Tt[:, s_, :], X[:, s_, :], start=True, stop=True)
                        ins.then_inc(s_dx, 1)
                    if after is not None:
                        after(lv)

            pe.wait_ge(s_zero, 1)

            norm_sum(0)
            pe.wait_ge(s_load, 16 * LOADS)
            for j in range(4):
                if j == 0:
                    first_unit(0, U_PRO, 0)
                else:
                    if j >= 3:
                        pe.wait_ge(s_evac[j % 3], EV_PRO[j % 3] + j // 3)
                    unit(j % 3, U_PRO + j, 0, 0, h_hi, h_lo)
                if j == 0:
                    pe.wait_ge(s_evac[0], 1)
                    T.matmul(pm[:, 0, 0:S], con("perm_i"), kraw, start=True, stop=True).then_inc(sem("s_ix_rot"), 1)
                if j == 1:
                    pe.wait_ge(s_evac[1], 1)
                    transposes([(pm[:, 4, c * P:(c + 1) * P], misc[:, 1 + c * P:1 + (c + 1) * P]) for c in range(NT)],
                               sem("s_ix_wT"))
            def rotation(b):
                pe.wait_ge(s_evac[(4 + b) % 3], (4 + b) // 3 + 1)
                pe.wait_ge(sem("s_ix_rope"), 1 + b)
                T.matmul(pm[:, 0, 0:S], con("perm_i"), qraw[:, b % 2, :], start=True, stop=True).then_inc(sem("s_ix_rot"), 1)

            def scores(b):
                pe.wait_ge(sem("s_ix_rope"), 2 + b)
                if b:
                    pe.wait_ge(sem("s_ix_relu"), 2 * b)
                for hd in range(2):
                    rows = slice(64 * hd, 64 * hd + 64)
                    for qt in range(NT):
                        ins = T.matmul(pm[:, 2 + hd, qt * S:(qt + 1) * S], qrope[rows, b % 2, qt * P:(qt + 1) * P],
                                       krope[rows, :], start=True, stop=True)
                    ins.then_inc(sem("s_ix_sc"), 1)

            for b in range(IDX_H // 2 + 6):
                u = 4 + b
                pe.wait_ge(s_evac[u % 3], u // 3)
                for hf_ in range(2):
                    half(gp[:, u % 3, 0:S], 2 * (U_PRO + u) + hf_, 0, 0, h_hi, h_lo, [SUB * hf_ + t for t in range(SUB)],
                         [hf_ == 0 and t == 0 for t in range(SUB)], [hf_ == 1 and t == SUB - 1 for t in range(SUB)])
                    if 1 <= b <= IDX_H // 2:
                        (rotation, scores)[hf_](b - 1)

            def feed1(n, i, last, tiles=(0, SUB)):
                if not last:
                    feed(n, i, U_T1, 6, EV_T1, tiles)

            def feed1_quarter(q, i, last):
                feed1(5 + q // 2, i, last, ((0, SUB // 2), (SUB // 2, SUB))[q % 2])

            def dsa(lv, i):
                if lv == 1:
                    pe.wait_ge(sem("s_ds_qn"), i + 1)
                    pe.wait_ge(sem("s_rw_tok"), i + 1)
                    T.matmul(pm[:, 3, :], con("perm_q"), d_qn.rearrange("p a b -> p (a b)"), start=True,
                             stop=True).then_inc(sem("s_at_rot"), 1)
                    transposes([(pm[:, 4, c * P:(c + 1) * P], d_raw[:, 2, c * P:(c + 1) * P]) for c in range(NT)],
                               sem("s_at_vT"))
                if lv == 2:
                    pe.wait_ge(sem("s_at_v"), i + 1)
                    pe.wait_ge(sem("s_at_qk"), i + 1)
                    for qt in range(NT):
                        ins = T.matmul(pm[:, 4, qt * S:(qt + 1) * S], d_qk[:, 0, qt * P:(qt + 1) * P], d_qk[:, 1, :],
                                       start=True, stop=True)
                    ins.then_inc(sem("s_ds_sc"), 1)
                if lv == 5:
                    pe.wait_ge(sem("s_at_pr"), i + 1)
                    transposes([(pm[:, 3, kt * S + qt * P:kt * S + (qt + 1) * P], d_pr[:, qt, kt * P:(kt + 1) * P])
                                for kt in range(NT) for qt in range(NT)], sem("s_at_pT"))
                if lv == 6:
                    pe.wait_ge(sem("s_at_pTo"), i + 1)
                    for kt in range(NT):
                        ins = T.matmul(pm[:, 4, 0:S], d_v[:, kt, :], d_pT[:, kt, :], start=kt == 0, stop=kt == NT - 1)
                    ins.then_inc(sem("s_at_o"), 1)

            def rwkv(p, last=False):
                pe.wait_ge(sem("s_rw_lw"), 16 * p + 16)
                T.matmul(pm[:, 0, 0:S], r_lora[0:64, 0:P], tanh_a[0:64, :], start=True, stop=True)
                T.matmul(pm[:, 1, 0:S], r_lora[64:P, 0:P], tanh_a[64:P, :], start=True, stop=True)
                T.matmul(pm[:, 2, 0:S], r_lora[:, P:2 * P], sig1, start=True, stop=False)
                T.matmul(pm[:, 2, 0:S], r_lora[0:32, 2 * P:3 * P], sig2[0:32, :], start=False,
                         stop=True).then_inc(sem("s_lora_in"), 1)
                feed1(0, p, last)
                feed1(1, p, last)
                pe.wait_ge(s_y, Y_T1 + 2 * p)
                pe.wait_ge(sem("s_rw_kk2"), p + 1)
                T.matmul(pm[:, 3, 0:S], con("heads"), r_sq, start=True, stop=True).then_inc(sem("s_rw_kkn"), 1)
                feed1(2, p, last)
                pe.wait_ge(sem("s_qk_sq"), p + 1)
                T.matmul(pm[:, 4, :], ones[:, :], d_sq, start=True, stop=True).then_inc(sem("s_qk_ss"), 1)
                feed1(3, p, last)
                feed1(4, p, last)
                pe.wait_ge(sem("s_rw_ops"), p + 1)
                transposes([(pm[:, 3, 0:P], r_mix[:, 2, 0:P]), (pm[:, 3, P:2 * P], r_mix[:, 2, P:S]),
                            (pm[:, 3, 2 * P:3 * P], r_bt[:, 0:P]), (pm[:, 3, 3 * P:4 * P], r_kt[:, 0:P])], sem("s_rw_tT"))
                pe.wait_ge(sem("s_rw_g"), p + 1)
                for hd in range(2):
                    rows = slice(64 * hd, 64 * hd + 64)
                    for c in range(NT):
                        cols = slice(c * P, (c + 1) * P)
                        T.matmul(pm[:, hd, c * P:(c + 1) * P], r_at[rows, cols], r_bt[rows, cols], start=True, stop=True)
                        ins = T.matmul(pm[:, hd, (2 + c) * P:(3 + c) * P], r_kt[rows, cols], r_at[rows, cols], start=True,
                                       stop=True)
                    ins.then_inc(sem("s_rw_mA"), 1)
                for hd in range(2):
                    rows = slice(64 * hd, 64 * hd + 64)
                    bank = (2, 4)[hd]
                    if hd:
                        pe.wait_ge(sem("s_qk_rv"), p + 1)
                    for c in range(NT):
                        cols = slice(c * P, (c + 1) * P)
                        T.matmul(pm[:, bank, c * P:(c + 1) * P], r_bt[rows, cols], r_rt[rows, cols], start=True, stop=True)
                        ins = T.matmul(pm[:, bank, (2 + c) * P:(3 + c) * P], r_kt[rows, cols], r_rt[rows, cols], start=True,
                                       stop=True)
                    ins.then_inc(sem("s_rw_mR"), 1)
                pe.wait_ge(sem("s_rw_R"), 2 * p + 1)

                def between(lv):
                    feed1_quarter(lv - 1, p, last)
                    if lv == 1:
                        pe.wait_ge(sem("s_rw_R"), 2 * p + 2)

                inverse(r_Al, r_X, r_Y, r_T, p, between, lambda lv: dsa(lv, p))
                pe.wait_ge(s_sy, 7 * p + 7)
                for c in range(NT):
                    if c:
                        pe.wait_ge(sem("s_rw_S"), p + 1)
                    for hd in range(2):
                        o = slice(c * P + 64 * hd, c * P + 64 * hd + 64)
                        if c:
                            T.matmul(pm[:, 3, o], r_at[:, P:S], r_S[:, 64 * hd:64 * hd + 64], start=True, stop=False)
                        ins = T.matmul(pm[:, 3, o], r_Aak[:, 2 * hd + c, :], r_tok[:, c, 64 * hd:64 * hd + 64],
                                       start=c == 0, stop=True)
                    ins.then_inc(sem("s_rw_mrhs"), 1)
                    if c == 0:
                        pe.wait_ge(s_y, Y_T1 + 2 * p + 1)
                        feed1(8, p, last)
                    pe.wait_ge(sem("s_rw_rhs"), NT * p + c + 1)
                    for hd in range(2):
                        o = slice(c * P + 64 * hd, c * P + 64 * hd + 64)
                        ins = T.matmul(pm[:, 4, o], r_Y[:, 2 * hd + c, :], r_rhs[:, c, 64 * hd:64 * hd + 64], start=True,
                                       stop=True)
                    ins.then_inc(sem("s_rw_mU"), 1)
                    feed1(9 + c, p, last)
                    pe.wait_ge(sem("s_rw_U"), NT * p + c + 1)
                    if c == 0:
                        T.matmul(pm[:, 0, 0:P], r_tok[:, 2, :], r_U[:, 0, :], start=True, stop=False)
                        T.matmul(pm[:, 0, 0:P], r_tok[:, 3, :], r_tok[:, 0, :], start=False,
                                 stop=True).then_inc(sem("s_rw_mS"), 1)
                    for hd in range(2):
                        o = slice(c * P + 64 * hd, c * P + 64 * hd + 64)
                        v = slice(64 * hd, 64 * hd + 64)
                        if c:
                            T.matmul(pm[:, 1, o], r_rt[:, P:S], r_S[:, v], start=True, stop=False)
                        T.matmul(pm[:, 1, o], r_R[:, hd, c, :], r_U[:, c, v], start=c == 0, stop=False)
                        ins = T.matmul(pm[:, 1, o], r_R[:, hd, 2 + c, :], r_tok[:, c, v], start=False, stop=True)
                ins.then_inc(sem("s_rw_my"), 1)
                pe.wait_ge(sem("s_rw_yt"), p + 1)
                transposes([(pm[:, 2, c * P:(c + 1) * P], r_X[:, c, :]) for c in range(NT)], sem("s_rw_yT"))
                feed1(11, p, last)
                pe.wait_ge(sem("s_rw_yTo"), p + 1)
                T.matmul(pm[:, 3, 0:S], con("heads"), r_X[:, 2:4, :].rearrange("p a b -> p (a b)"), start=True, stop=True)
                T.matmul(pm[:, 3, S:2 * S], con("heads"), r_D[:, 2, :], start=True, stop=True).then_inc(sem("s_rw_mean"), 1)
                pe.wait_ge(sem("s_rw_yc2"), p + 1)
                T.matmul(pm[:, 4, 0:S], con("heads"), r_Y[:, 2:4, :].rearrange("p a b -> p (a b)"), start=True,
                         stop=True).then_inc(sem("s_rw_var"), 1)

            pe.wait_ge(sem("s_lora_in"), 4)
            loop(pe, RWKV_P - 1, rwkv)
            rwkv(RWKV_P - 1, True)

            pe.wait_ge(s_y, Y_T2 - 1)

            def wout(i, first=False):
                for j in range(3):
                    pe.wait_ge(s_evac[j], EV_WOUT[j] + i)
                    for hf_ in range(2):
                        if first and j == 0 and hf_:
                            pe.wait_ge(s_y, Y_T2)
                        half(gp[:, j, 0:S], 2 * (U_WOUT + j) + hf_, i, 6, y_hi, y_lo, [SUB * hf_ + t for t in range(SUB)],
                             [hf_ == 0 and t == 0 for t in range(SUB)], [hf_ == 1 and t == SUB - 1 for t in range(SUB)])

            wout(0, True)
            loop(pe, 4, lambda i: wout(i + 1))
            pe.wait_ge(s_evac[0], EV_WOUT[0] + 5)
            unit(0, U_WOUT + 15, 0, 0, y_hi, y_lo)
            norm_sum(1)

            pe.wait_ge(sem("s_hf"), 8)
            for tt in range(NT):
                for kt in range(KT):
                    ins = T.matmul(pm[:, 1, tt * 32:tt * 32 + 20], hf[:, kt, tt * P:(tt + 1) * P], route[:, kt, :],
                                   start=kt == 0, stop=kt == KT - 1)
            ins.then_inc(sem("s_rt_lg"), 1)

            def gate_up(b, u, e, step, ready):
                pe.wait_ge(sem(f"s_me_pair{b % 2}"), ready)
                for j in range(2):
                    o = (gp[:, 0, 0:S], gp[:, 1, 0:S], gp[:, 2, 0:S], pm[:, 4, 0:S])[2 * (b % 2) + j]
                    for hf_ in range(2):
                        half(o, 2 * (u + j) + hf_, e, 2 * step, h_hi, h_lo, [SUB * hf_ + t for t in range(SUB)],
                             [hf_ == 0 and t == 0 for t in range(SUB)], [hf_ == 1 and t == SUB - 1 for t in range(SUB)])

            def token_weights(e):
                pe.wait_ge(sem("s_me_sel"), e + 1)
                T.matmul(gp[:, 2, 0:S], ones[0:16, :], csel[0:16, :], start=True, stop=True).then_inc(sem("s_me_bcm"), 1)

            def moe(e, last=False):
                pe.wait_ge(sem("s_me_bc"), e + 1)
                for b in range(1, 4):
                    gate_up(b, U_TM + 2 * (b - 1), e, 12, 2 * e + b // 2 + 1)
                if not last:
                    gate_up(0, U_TM + 6, e, 12, 2 * e + 3)
                pe.wait_ge(sem("s_me_he"), 4 * e + 4)
                if not last:
                    token_weights(e + 1)
                for d in range(4):
                    u = U_TM + (6 if last else 8) + d
                    pe.wait_ge(sem(f"s_me_down{d % 2}"), 2 * e + d // 2 + 1)
                    for hf_ in range(2):
                        nb = [2 * hf_ + t // 4 for t in range(SUB)]
                        o = [pm[:, 2 * (d % 2) + n // 2, (n % 2) * S:(n % 2) * S + S] for n in nb]
                        half(o, 2 * u + hf_, e, 24, y_hi, y_lo, [t % 4 for t in range(SUB)],
                             [t % 4 == 0 for t in range(SUB)], [t % 4 == 3 for t in range(SUB)])

            pe.wait_ge(sem("s_hlo"), 8)
            gate_up(0, U_MOE, 0, 0, 1)
            pe.wait_ge(sem("s_rt_comb"), 1)
            transposes([(pm[:, 2, tt * P:(tt + 1) * P], comb[:, tt, :]) for tt in range(NT)], sem("s_rt_cT"))
            token_weights(0)
            loop(pe, NEXP - 1, moe)
            moe(NEXP - 1, True)

            norm_sum(2)
            first_unit(0, U_AB, 2)

            for j in range(6):
                pe.wait_ge(s_evac[j % 3], EV_DN0[j % 3] + j // 3)
                unit(j % 3, U_DN0 + j, 0, 0, h_hi, h_lo)
                if j == 2:
                    pe.wait_ge(sem("s_ab_kd"), 1)
                    transposes([(pm[:, 0, c * P:(c + 1) * P], gb[:, c * P:(c + 1) * P]) for c in range(NT)], sem("s_ab_T"))

            def feed2(n, i, last, tiles=(0, SUB)):
                if not (last and n >= 12):
                    feed(n, i, U_T2, 12, EV_T2, tiles)

            def feed2_quarter(q, i, last):
                feed2(9 + q // 2, i, last, ((0, SUB // 2), (SUB // 2, SUB))[q % 2])

            def delta(i, last=False):
                feed2(0, i, last)
                pe.wait_ge(s_y, Y_T2 + 2 * i)
                pe.wait_ge(sem("s_dn_gs"), i + 1)
                T.matmul(pm[:, 4, :], ones[0:16, :], n_gs[0:16, :, :].rearrange("p a b -> p (a b)"), start=True,
                         stop=True).then_inc(sem("s_dn_gb"), 1)
                feed2(1, i, last)
                feed2(2, i, last)
                feed2(3, i, last)
                feed2(4, i, last)
                pe.wait_ge(sem("s_qk_sq"), DSA_H + i + 1)
                T.matmul(pm[:, 0, :], ones[:, :], n_sq, start=True, stop=True).then_inc(sem("s_qk_ss"), 1)
                transposes([(pm[:, 1, (2 * v + c) * P:(2 * v + c + 1) * P], n_qkv[:, 2 + v, c * P:(c + 1) * P])
                            for v in range(2) for c in range(NT)], sem("s_dn_vT"))
                feed2(5, i, last)
                feed2(6, i, last)
                pe.wait_ge(sem("s_dn_qk"), i + 1)
                for c in range(NT):
                    cols = slice(c * P, (c + 1) * P)
                    T.matmul(pm[:, 3, c * P:(c + 1) * P], n_qkv[:, 1, cols], n_qkv[:, 1, cols], start=True, stop=True)
                    ins = T.matmul(pm[:, 3, (2 + c) * P:(3 + c) * P], n_qkv[:, 1, cols], n_qkv[:, 0, cols], start=True,
                                   stop=True)
                ins.then_inc(sem("s_dn_kk"), 1)
                transposes([(pm[:, 2, 0:P], n_qkv[:, 1, 0:P])], sem("s_dn_kT"))
                feed2(7, i, last)
                feed2(8, i, last)
                pe.wait_ge(sem("s_dn_kd"), i + 1)
                pe.wait_ge(sem("s_dn_QK"), i + 1)
                pe.wait_ge(sem("s_dn_v"), i + 1)
                inverse(n_Al, n_X, n_Y, n_T, i + RWKV_P, lambda lv: feed2_quarter(lv - 1, i, last))
                pe.wait_ge(s_sy, 7 * (i + RWKV_P) + 7)
                for v in range(2):
                    ins = T.matmul(pm[:, 0, v * P:(v + 1) * P], n_Y[:, 2 * v, :], n_r0[:, v, :], start=True, stop=True)
                ins.then_inc(sem("s_dn_m0"), 1)
                feed2(12, i, last)
                pe.wait_ge(sem("s_dn_vn"), 2 * i + 1)
                for v in range(2):
                    ins = T.matmul(pm[:, 1, v * P:(v + 1) * P], n_kd[:, v, :], n_vn[:, v, :], start=True, stop=True)
                ins.then_inc(sem("s_dn_mS"), 1)
                for v in range(2):
                    T.matmul(pm[:, 2, v * P:(v + 1) * P], n_QK[:, 2 * v, :], n_vn[:, v, :], start=True, stop=True)
                pe.wait_ge(sem("s_dn_S"), i + 1)
                state = n_S.rearrange("p a b -> p (a b)")
                T.matmul(pm[:, 3, 0:S], n_qkv[:, 1, P:S], state, start=True, stop=True)
                T.matmul(pm[:, 3, S:2 * S], n_qkv[:, 0, P:S], state, start=True, stop=True).then_inc(sem("s_dn_mks"), 1)
                feed2(13, i, last)
                pe.wait_ge(sem("s_dn_r1"), i + 1)
                for v in range(2):
                    ins = T.matmul(pm[:, 0, S + v * P:S + (v + 1) * P], n_Y[:, 2 * v + 1, :], n_r1[:, v, :], start=True,
                                   stop=True)
                ins.then_inc(sem("s_dn_m0"), 1)
                feed2(14, i, last)
                pe.wait_ge(sem("s_dn_vn"), 2 * i + 2)
                for v in range(2):
                    ins = T.matmul(pm[:, 2, S + v * P:S + (v + 1) * P], n_QK[:, 2 * v + 1, :], n_vn[:, 2 + v, :], start=True,
                                   stop=True)
                ins.then_inc(sem("s_dn_mo"), 1)
                feed2(15, i, last)
                feed2(16, i, last)
                feed2(17, i, last)
                pe.wait_ge(sem("s_dn_on"), i + 1)
                transposes([(pm[:, 4, v * S + c * P:v * S + (c + 1) * P], n_o[:, 2 * c + v, :]) for v in range(2)
                            for c in range(NT)], sem("s_dn_oT"))

            def swa(i, last=False):
                feed2(18, i, last)
                pe.wait_ge(s_y, Y_T2 + 2 * i + 1)
                for k in range(3):
                    pe.wait_ge(s_evac[k], EV_T2[k] + 4 * i + 2)
                for n in range(2):
                    ins = T.matmul(pm[:, n, :], con("perm_w"), w_raw[:, 2 * n:2 * n + 2, :].rearrange("p a b -> p (a b)"),
                                   start=True, stop=True)
                ins.then_inc(sem("s_at_rot"), 1)
                transposes([(pm[:, 4, c * P:(c + 1) * P], w_v0[:, c * P:(c + 1) * P]) for c in range(NT)], sem("s_at_vT"))
                feed2(19, i, last)
                pe.wait_ge(sem("s_at_qk"), DSA_H + i + 1)
                for g in range(3):
                    ins = T.matmul(pm[:, 0, g * P:(g + 1) * P], w_qk[:, g, 0:P], w_qk[:, 3, 0:P], start=True, stop=True)
                ins.then_inc(sem("s_sw_sc"), 1)
                for g in range(3):
                    ins = T.matmul(pm[:, 1 + g // 2, (g % 2) * S:(g % 2) * S + S], w_qk[:, g, P:S], w_qk[:, 3, :], start=True,
                                   stop=True)
                ins.then_inc(sem("s_sw_sc"), 1)
                feed2(20, i, last)
                feed2(21, i, last)
                pe.wait_ge(sem("s_at_pr"), DSA_H + i + 1)
                transposes([(pm[:, 3, 0:P], w_p0), (pm[:, 3, P:2 * P], w_p1[:, 0:P]), (pm[:, 3, 2 * P:3 * P], w_p1[:, P:S])],
                           sem("s_at_pT"))
                feed2(22, i, last)
                pe.wait_ge(sem("s_at_v"), DSA_H + i + 1)
                pe.wait_ge(sem("s_at_pTo"), DSA_H + i + 1)
                T.matmul(pm[:, 0, 0:P], w_v[:, 0, :], w_pT[:, 0, :], start=True, stop=True)
                T.matmul(pm[:, 0, P:S], w_v[:, 0, :], w_pT[:, 1, :], start=True, stop=False)
                T.matmul(pm[:, 0, P:S], w_v[:, 1, :], w_pT[:, 2, :], start=False, stop=True).then_inc(sem("s_at_o"), 1)
                feed2(23, i, last)

            def turn2(i, last=False):
                delta(i, last)
                swa(i, last)

            pe.wait_ge(sem("s_ab_tok"), 1)
            pe.wait_ge(s_c2, 16)
            loop(pe, DN_H - 1, turn2)
            turn2(DN_H - 1, True)

            def project(u0, ev, n, y_all):
                def turn(i, first=False):
                    for b in range(2):
                        pe.wait_ge(s_evac[b], ev[b] + i)
                        for s_ in range(3):
                            if first and b == 0 and s_ == 2:
                                pe.wait_ge(s_y, y_all)
                            half(gp[:, b, 0:S], 2 * u0 + 3 * b + s_, i, 6, y_hi, y_lo, [SUB * s_ + t for t in range(SUB)],
                                 [s_ == 0 and t == 0 for t in range(SUB)], [s_ == 2 and t == SUB - 1 for t in range(SUB)])
                turn(0, True)
                loop(pe, 7, lambda i: turn(i + 1))
                norm_sum(n)

            pe.wait_ge(s_y, Y_SC - 1)
            project(U_HOUT, EV_HOUT, 3, Y_SC)

            def shortconv(i, first=False):
                for n in range(12):
                    if first and n == 0:
                        first_unit(0, U_SC, 3)
                        continue
                    pe.wait_ge(s_evac[n % 3], EV_SC[n % 3] + 4 * i + n // 3)
                    unit(n % 3, U_SC + n, i, 12, h_hi, h_lo)

            shortconv(0, True)
            loop(pe, 7, lambda i: shortconv(i + 1))
            pe.wait_ge(s_y, Y_SC + 16)
            project(U_SOUT, EV_SOUT, 4, Y_SC + 24)

        @block.scalar
        def _(act):
            A = nc.scalar
            chain = Chain(act, s_ac)

            def split(sub, i=0, step=0):
                if isinstance(i, int) and sub + step * i >= N_SUBS:
                    return
                u, slot = sub // 2, sub % RING
                act.wait_ge(s_stage[u % RING], 16 * (u // RING + 1) + 16 * (step // (2 * RING)) * i)
                if sub >= RING:
                    act.wait_ge(s_sub, sub - RING + 1 + step * i)
                A.activation(w_hi[:, slot, :], stage[:, u % RING, (sub % 2) * SUB * P:(sub % 2 + 1) * SUB * P],
                             ACT.Copy).then_inc(s_hi, 1)

            def ahead(u, i=0, step=0):
                split(2 * u + RING, i, 2 * step)
                split(2 * u + RING + 1, i, 2 * step)

            def feed(n, i, u0, per):
                split(2 * u0 + n + 2, i, 2 * per)

            def done(u, i=0, step=0):
                act.wait_ge(s_sub, 2 * u + 2 + 2 * step * i)

            act.dma_start(vecs[:, :], vecs_in).then_inc(sem("s_vecs"), 16)
            for o, src in ((c0[:, :], c0_in), (c12[:, 0:N1], c1_in),
                           (route[:, :, :], route_in), (rbias[:, :], rbias_in)):
                act.dma_start(o, src).then_inc(s_load, 16)

            def square(k, n=1):
                A.activation(hf[:, bass.ds(k, n), :], x[:, bass.ds(k, n), :], ACT.Square).then_inc(sem("s_sq"), n)

            def norm(n, last=False):
                act.wait_ge(sem("s_nrv"), n + 1)
                A.activation(n_rs, n_rs, ACT.Sqrt).then_inc(sem("s_nrs"), 1)
                if last:
                    return
                for q in range(4):
                    act.wait_ge(sem("s_hf"), 4 * n + q + 1)
                    A.activation(h_hi[:, 4 * q:4 * q + 4, :], hf[:, 4 * q:4 * q + 4, :], ACT.Copy).then_inc(sem("s_hhi"), 1)

            for q in range(4):
                act.wait_ge(s_x[q], 16)
                square(4 * q, 4)
            for sub in range(RING):
                split(sub)
            norm(0)
            act.wait_ge(sem("s_vecs"), 16)
            act.wait_ge(s_load, 16 * LOADS)
            act.wait_ge(sem("s_hlo"), 4)
            act.wait_ge(s_zero, 4)
            for j in range(4):
                ahead(U_PRO + j)
                done(U_PRO + j)
                o = (kraw, misc[:, 1:S + 1], dwda[:, 1:S + 1], dg1[:, 1:S + 1])[j]
                A.activation(o, gp[:, j % 3, 0:S], ACT.Copy).then_inc(s_evac[j % 3], 1)
            act.wait_ge(sem("s_lora_mix"), 1)
            A.activation(tanh_a[0:64, :], t_2[0:64, :], ACT.Tanh).then_inc(sem("s_lora_in"), 1)
            A.activation(tanh_a[64:P, :], t_2[64:P, :], ACT.Copy).then_inc(sem("s_lora_in"), 1)
            act.wait_ge(sem("s_lora_mix"), 2)
            A.activation(sig1, mixd, ACT.Sigmoid).then_inc(sem("s_lora_in"), 1)
            act.wait_ge(sem("s_lora_mix"), 3)
            A.activation(sig2, sig2, ACT.Sigmoid).then_inc(sem("s_lora_in"), 1)
            def relus(b):
                for hd in range(2):
                    act.wait_ge(sem("s_ix_sc"), 2 * b + hd + 1)
                    if b:
                        act.wait_ge(sem("s_ix_acc"), 2 * b - 1 + hd)
                    A.activation(relu[:, hd, :], pm[:, 2 + hd, :], ACT.Relu).then_inc(sem("s_ix_relu"), 1)

            for b in range(IDX_H // 2):
                u = 4 + b
                ahead(U_PRO + u)
                done(U_PRO + u)
                if b >= 2:
                    act.wait_ge(sem("s_ix_rope"), b)
                A.activation(qraw[:, b % 2, :], gp[:, u % 3, 0:S], ACT.Copy).then_inc(s_evac[u % 3], 1)
                if b:
                    relus(b - 1)

            def next1(j):
                return r_raw[:, j, 1:S + 1] if j < 3 else d_raw[:, j - 3, :]

            for j in range(6):
                if j < 5:
                    ahead(U_RW0 + j)
                else:
                    split(2 * (U_RW0 + j) + RING)
                done(U_RW0 + j)
                A.activation(next1(j), gp[:, j % 3, 0:S], ACT.Copy).then_inc(s_evac[j % 3], 1)
                if j == 0:
                    relus(IDX_H // 2 - 1)

            def take1(j, i):
                done(U_T1 + j, i, 6)
                A.activation(next1(j), gp[:, j % 3, 0:S], ACT.Copy).then_inc(s_evac[j % 3], 1)

            def feed1(n, i, last):
                if not last:
                    feed(n, i, U_T1, 6)
                    if n % 2 == 0 and n:
                        take1(n // 2 - 1, i)

            def dsa(lv, i):
                if lv == 4:
                    act.wait_ge(sem("s_at_nm"), i + 1)
                    for qt in range(NT):
                        A.activation(d_pr[:, qt, :], d_lg[:, qt, :], ACT.Exp, bias=d_nm[:, qt:qt + 1],
                                     accum_out=d_sum[:, qt:qt + 1]).then_inc(sem("s_ds_ex"), 1)
                if lv == 6:
                    act.wait_ge(sem("s_at_pT"), i + 1)
                    A.activation(d_pT.rearrange("p a b -> p (a b)"), pm[:, 3, :], ACT.Copy).then_inc(sem("s_at_pTo"), 1)
                    act.wait_ge(sem("s_at_o"), i + 1)
                    A.activation(y_hi[:, i, :], pm[:, 4, 0:S], ACT.Copy).then_inc(s_yhi, 1)

            def solver(Tt, it, between, after=None):
                for lv in range(1, 7):
                    act.wait_ge(s_t1, 7 * it + lv + 1)
                    A.activation(Tt.rearrange("p a b -> p (a b)"), pm[:, 0, :], ACT.Copy).then_inc(s_t1o, 1)
                    between(lv)
                    if after is not None:
                        after(lv)

            def rwkv(p, last=False):
                for k in range(3):
                    act.wait_ge(s_evac[k], EV_RW0[k] + 2 + 2 * p)
                A.activation(d_sq, d_raw[:, 0:2, :].rearrange("p a b -> p (a b)"), ACT.Square).then_inc(sem("s_qk_sq"), 1)
                feed1(0, p, last)
                feed1(1, p, last)
                act.wait_ge(s_y, Y_T1 + 2 * p)
                act.wait_ge(sem("s_lora_in"), 5 + p)
                A.activation(r_lw, pm[:, 0, 0:S], ACT.Sigmoid, bias=vec("w0", p))
                A.activation(r_a, pm[:, 1, 0:S], ACT.Sigmoid, bias=vec("a0", p)).then_inc(sem("s_rw_sig"), 1)
                A.activation(r_g, pm[:, 2, 0:S], ACT.Copy).then_inc(sem("s_rw_g"), 1)
                act.wait_ge(sem("s_rw_kkn"), p + 1)
                A.activation(r_tmp, pm[:, 3, 0:S], ACT.Sqrt).then_inc(sem("s_rw_nrm"), 1)
                feed1(2, p, last)
                act.wait_ge(sem("s_rw_cc"), p + 1)
                A.activation(r_P, r_cum, ACT.Exp)
                A.activation(r_Pi, r_cum, ACT.Exp, scale=-1.0)
                A.activation(r_em, r_negm, ACT.Exp, scale=-1.0)
                A.activation(r_lw, r_lw, ACT.Exp).then_inc(sem("s_rw_exp"), 1)
                feed1(3, p, last)
                feed1(4, p, last)
                act.wait_ge(sem("s_rw_tT"), p + 1)
                A.activation(r_tok.rearrange("p a b -> p (a b)"), pm[:, 3, :], ACT.Copy).then_inc(sem("s_rw_tok"), 1)
                for hd in range(2):
                    act.wait_ge(sem("s_rw_mA"), 2 * p + hd + 1)
                    ins = A.activation(r_A[:, 2 * hd:2 * hd + 2, :].rearrange("p a b -> p (a b)"), pm[:, hd, 0:S], ACT.Copy)
                ins.then_inc(sem("s_rw_A"), 1)
                act.wait_ge(sem("s_qk_rv"), p + 1)
                A.activation(d_rs, d_rs, ACT.Sqrt).then_inc(sem("s_qk_rs"), 1)
                solver(r_T, p, lambda lv: feed1(5 + lv // 2, p, last) if lv % 2 else None, lambda lv: dsa(lv, p))
                for c in range(NT):
                    act.wait_ge(sem("s_rw_mrhs"), NT * p + c + 1)
                    A.activation(r_rhs[:, c, :], pm[:, 3, c * P:(c + 1) * P], ACT.Copy).then_inc(sem("s_rw_rhs"), 1)
                    if c == 0:
                        feed1(8, p, last)
                    act.wait_ge(sem("s_rw_mU"), NT * p + c + 1)
                    A.activation(r_U[:, c, :], pm[:, 4, c * P:(c + 1) * P], ACT.Copy).then_inc(sem("s_rw_U"), 1)
                    feed1(9 + c, p, last)
                act.wait_ge(sem("s_rw_my"), p + 1)
                A.activation(r_X[:, 0:2, :].rearrange("p a b -> p (a b)"), pm[:, 1, 0:S], ACT.Copy).then_inc(sem("s_rw_yt"), 1)
                act.wait_ge(sem("s_rw_yT"), p + 1)
                A.activation(r_X[:, 2:4, :].rearrange("p a b -> p (a b)"), pm[:, 2, 0:S], ACT.Copy).then_inc(sem("s_rw_yTo"), 1)
                feed1(11, p, last)
                act.wait_ge(sem("s_rw_yc"), p + 1)
                A.activation(r_Y[:, 2:4, :], r_Y[:, 0:2, :], ACT.Square).then_inc(sem("s_rw_yc2"), 1)
                act.wait_ge(sem("s_ho_rv"), p + 1)
                A.activation(r_tmp, r_tmp, ACT.Sqrt).then_inc(sem("s_ho_rs"), 1)
                act.wait_ge(sem("s_yf"), p + 1)
                A.activation(y_hi[:, p + DSA_H, :], r_sq, ACT.Copy).then_inc(s_yhi, 1)
                if not last:
                    take1(5, p)

            act.wait_ge(s_zero, 6)
            loop(act, RWKV_P - 1, rwkv)
            rwkv(RWKV_P - 1, True)
            split(2 * U_WOUT + 2)

            def wout(i):
                for j in range(3):
                    ahead(U_WOUT + j, i, 3)
                    act.wait_ge(s_evac[j], EV_WOUT[j] + 1 + i)
                    square(3 * i + j)

            loop(act, 5, wout)
            ahead(U_WOUT + 15)
            act.wait_ge(s_evac[0], EV_AB[0])
            square(15)
            norm(1)
            for n in range(2):
                act.wait_ge(sem("s_rt_d"), n + 1)
                A.activation(e4, g4, ACT.Exp).then_inc(sem("s_rt_e"), 1)
                ahead(U_MOE + n)
            act.wait_ge(sem("s_rt_cT"), 1)
            A.activation(combT, pm[:, 2, 0:S], ACT.Copy).then_inc(sem("s_rt_cTo"), 1)

            def gate(b, u, e, step, splits=True):
                if splits:
                    ahead(u, e, step)
                    ahead(u + 1, e, step)
                done(u + 1, e, step)
                A.activation(sg[:, b % 2, :], gp[:, 2 * (b % 2), 0:S], ACT.Silu).then_inc(sem("s_me_sg"), 1)

            def hidden(b, n):
                act.wait_ge(sem("s_me_he2"), n)
                A.activation(y_hi[:, b, :], he2[:, b % 2, :], ACT.Copy).then_inc(sem("s_me_hhi"), 1)

            def moe(e, last=False):
                for b in range(1, 4):
                    gate(b, U_TM + 2 * (b - 1), e, 12)
                    hidden(b, 4 * e + b + 1)
                if not last:
                    gate(0, U_TM + 6, e, 12)
                    token_weights(e + 1)
                for d in range(4):
                    ahead(U_TM + (6 if last else 8) + d, e, 12)
                    if last:
                        act.wait_ge(sem(f"s_me_down{d % 2}"), 2 * NEXP + d // 2)
                        square(4 * d, 4)
                if not last:
                    done(U_TM + 11, e, 12)
                    hidden(0, 4 * e + 5)

            def token_weights(e):
                act.wait_ge(sem("s_me_bcm"), e + 1)
                if not isinstance(e, int):
                    act.wait_ge(sem("s_me_he"), 4 * e)
                A.activation(bce, gp[:, 2, 0:S], ACT.Copy).then_inc(sem("s_me_bc"), 1)

            gate(0, U_MOE, 0, 0, False)
            token_weights(0)
            hidden(0, 1)
            loop(act, NEXP - 1, moe)
            moe(NEXP - 1, True)

            norm(2)
            ahead(U_AB)
            act.wait_ge(sem("s_hlo"), 12)
            done(U_AB)
            A.activation(ab, gp[:, 0, 0:S], ACT.Copy).then_inc(s_evac[0], 1)
            act.wait_ge(s_evac[0], EV_DN0[0])
            act.wait_ge(s_zero, 7)
            ahead(U_DN0)
            A.activation(gb[32:48, :], ab[32:48, :], ACT.Sigmoid)
            act.wait_ge(sem("s_ab_x"), 1)
            chain.link(A.activation(g_e[0:16, :], g_e[0:16, :], ACT.Exp))
            A.activation(ea[0:16, :], vecs[0:16, VEC["a_log"]:VEC["a_log"] + 1], ACT.Exp)
            A.activation(g_s[0:16, :], g_e[0:16, :], ACT.Ln, bias=1.0).then_inc(sem("s_ab_ln"), 1)
            act.wait_ge(sem("s_ab_cum"), 1)
            A.activation(gb[64:80, 0:P], g_x[0:16, 0:P], ACT.Exp).then_inc(sem("s_ab_kd"), 1)

            for j in range(6):
                if j == 0:
                    pass
                elif j < 5:
                    ahead(U_DN0 + j)
                else:
                    split(2 * (U_DN0 + j) + RING)
                done(U_DN0 + j)
                o = n_raw[:, j, 3:S + 3] if j < 4 else n_z[:, j - 4, :]
                A.activation(o, gp[:, j % 3, 0:S], ACT.Copy).then_inc(s_evac[j % 3], 1)

            act.wait_ge(sem("s_ab_tokg"), 1)
            A.activation(egt, gtok[:, :, 0:16], ACT.Exp).then_inc(sem("s_ab_eg"), 1)

            def take2(j, i):
                done(U_T2 + j, i, 12)
                if j < 6:
                    o = w_raw[:, j, :] if j < 4 else w_v0 if j == 4 else w_z
                else:
                    o = n_raw[:, j - 6, 3:S + 3] if j < 10 else n_z[:, j - 10, :]
                A.activation(o, gp[:, j % 3, 0:S], ACT.Silu if j == 5 else ACT.Copy).then_inc(s_evac[j % 3], 1)

            def feed2(n, i, last):
                if not (last and n >= 12):
                    feed(n, i, U_T2, 12)
                if n % 2 == 0 and n and not (last and n > 12):
                    take2(n // 2 - 1, i)

            def delta(i, last=False):
                act.wait_ge(s_y, Y_T2 + 2 * i)
                for n in range(3):
                    feed2(n, i, last)
                act.wait_ge(sem("s_dn_cv"), i + 1)
                chain.link(A.activation(n_qkv, n_qkv, ACT.Silu))
                for k in (1, 2):
                    act.wait_ge(s_evac[k], EV_DN0[k] + 4 * i + 2)
                A.activation(n_z, n_z, ACT.Silu).then_inc(sem("s_dn_z"), 1)
                A.activation(n_sq, n_qkv[:, 0:2, :].rearrange("p a b -> p (a b)"), ACT.Square).then_inc(sem("s_qk_sq"), 1)
                feed2(3, i, last)
                feed2(4, i, last)
                act.wait_ge(sem("s_dn_vT"), i + 1)
                A.activation(n_v.rearrange("p a b -> p (a b)"), pm[:, 1, :], ACT.Copy).then_inc(sem("s_dn_v"), 1)
                act.wait_ge(sem("s_dn_D"), i + 1)
                A.activation(n_E2, n_E2, ACT.Exp).then_inc(sem("s_dn_E"), 1)
                A.activation(n_E1, n_E1, ACT.Exp, scale=-1.0).then_inc(sem("s_dn_E1"), 1)
                feed2(5, i, last)
                act.wait_ge(sem("s_qk_rv"), DSA_H + i + 1)
                A.activation(n_rn, n_rn, ACT.Sqrt).then_inc(sem("s_qk_rs"), 1)
                feed2(6, i, last)
                feed2(7, i, last)
                feed2(8, i, last)
                solver(n_T, i + RWKV_P, lambda lv: feed2(9 + lv // 2, i, last) if lv % 2 else None)
                act.wait_ge(sem("s_dn_m0"), 2 * i + 1)
                A.activation(n_vn[:, 0:2, :].rearrange("p a b -> p (a b)"), pm[:, 0, 0:S], ACT.Copy).then_inc(sem("s_dn_vn"), 1)
                feed2(12, i, last)
                act.wait_ge(sem("s_dn_mS"), i + 1)
                A.activation(n_S.rearrange("p a b -> p (a b)"), pm[:, 1, 0:S], ACT.Copy).then_inc(sem("s_dn_S"), 1)
                feed2(13, i, last)
                act.wait_ge(sem("s_dn_m0"), 2 * i + 2)
                A.activation(n_vn[:, 2:4, :].rearrange("p a b -> p (a b)"), pm[:, 0, S:2 * S], ACT.Copy).then_inc(sem("s_dn_vn"), 1)
                feed2(14, i, last)
                act.wait_ge(sem("s_dn_mo"), i + 1)
                A.activation(n_o.rearrange("p a b -> p (a b)"), pm[:, 2, :], ACT.Copy).then_inc(sem("s_dn_o"), 1)
                feed2(15, i, last)
                act.wait_ge(sem("s_dn_ot"), i + 1)
                for k in range(4):
                    ins = A.activation(n_A[:, k, :], n_o[:, k, :], ACT.Square, accum_out=n_ss[:, k:k + 1])
                ins.then_inc(sem("s_dn_os"), 1)
                feed2(16, i, last)
                act.wait_ge(sem("s_ho_rv"), RWKV_P + i + 1)
                A.activation(n_or, n_or, ACT.Sqrt).then_inc(sem("s_ho_rs"), 1)
                feed2(17, i, last)
                act.wait_ge(sem("s_yf"), RWKV_P + 2 * i + 1)
                A.activation(y_hi[:, bass.ds(2 * i, 2), :], n_yf, ACT.Copy).then_inc(s_yhi, 1)

            def swa(i, last=False):
                feed2(18, i, last)
                feed2(19, i, last)
                act.wait_ge(sem("s_at_nm"), DSA_H + i + 1)
                A.activation(w_l0, w_l0, ACT.Exp, bias=w_nm[:, 0:1], accum_out=w_sum[:, 0:1])
                A.activation(w_l1, w_l1, ACT.Exp, bias=w_nm[:, 1:2], accum_out=w_sum[:, 1:2]).then_inc(sem("s_sw_ex"), 1)
                feed2(20, i, last)
                feed2(21, i, last)
                act.wait_ge(sem("s_at_pT"), DSA_H + i + 1)
                A.activation(w_pT.rearrange("p a b -> p (a b)"), pm[:, 3, 0:3 * P], ACT.Copy).then_inc(sem("s_at_pTo"), 1)
                feed2(22, i, last)
                act.wait_ge(sem("s_yf"), RWKV_P + 2 * i + 2)
                A.activation(y_hi[:, i + 16, :], w_yf, ACT.Copy).then_inc(s_yhi, 1)
                feed2(23, i, last)

            def turn2(i, last=False):
                delta(i, last)
                swa(i, last)
                if not last:
                    take2(11, i)

            act.wait_ge(s_zero, 8)
            chain.loop(DN_H - 1, 1, turn2)
            chain.turn(1, lambda i: turn2(i, True), DN_H - 1)
            split(2 * U_HOUT + 2)

            def project(u0, ev):
                def turn(i):
                    for j in range(3):
                        ahead(u0 + j, i, 3)
                        if j:
                            act.wait_ge(s_evac[j - 1], ev[j - 1] + 1 + i)
                            square(2 * i + j - 1)
                return turn

            loop(act, 8, project(U_HOUT, EV_HOUT))

            norm(3)
            act.wait_ge(sem("s_hlo"), 16)

            def shortconv(i):
                for n in range(12):
                    bb, j, k = n // 4, n % 4, n % 3
                    ahead(U_SC + n, i, 12)
                    if j == 2:
                        continue
                    if j == 0:
                        act.wait_ge(s_y, Y_SC - 2 + bb + 3 * i)
                    done(U_SC + n, i, 12)
                    o = (q_b, q_c, None, q_z)[j][:, bb, :]
                    A.activation(o, gp[:, k, 0:S], ACT.Silu if j == 3 else ACT.Copy).then_inc(s_evac[k], 1)
                    if j == 3:
                        act.wait_ge(sem("s_sc_y"), 3 * i + bb + 1)
                        A.activation(y_hi[:, 3 * i + bb, :], q_a[:, bb, :], ACT.Copy).then_inc(s_yhi, 1)

            loop(act, 8, shortconv)
            loop(act, 7, project(U_SOUT, EV_SOUT))
            project(U_SOUT, EV_SOUT)(7)
            norm(4, last=True)

        @block.vector
        def _(dve):
            V = nc.vector
            chain = Chain(dve, s_dv)
            link = chain.link

            def split(sub, i=0, step=0):
                if isinstance(i, int) and sub + step * i >= N_SUBS:
                    return
                u, slot = sub // 2, sub % RING
                dve.wait_ge(s_hi, sub + 1 + step * i)
                V.tensor_tensor(w_lo[:, slot, :], stage[:, u % RING, (sub % 2) * SUB * P:(sub % 2 + 1) * SUB * P],
                                w_hi[:, slot, :].bitcast(F32), ALU.subtract).then_inc(s_lo, 1)

            def ahead(u, i=0, step=0):
                split(2 * u + RING, i, 2 * step)
                split(2 * u + RING + 1, i, 2 * step)

            def feed(n, i, u0, per):
                split(2 * u0 + n + 2, i, 2 * per)

            def lower(lo, hi, full, s):
                V.tensor_tensor(lo, full, hi.bitcast(F32), ALU.subtract).then_inc(s, 1)

            def norm(n, gain, last=False):
                dve.wait_ge(sem("s_nsum"), n + 1)
                link(V.tensor_scalar(n_rs, pm[:, 4, 0:S], 1.0 / D, EPS, ALU.mult, ALU.add))
                V.reciprocal(n_rs, n_rs).then_inc(sem("s_nrv"), 1)
                dve.wait_ge(sem("s_nrs"), n + 1)

                def scaled(q):
                    for kt in range(4 * q, 4 * q + 4):
                        ins = V.scalar_tensor_tensor(hf[:, kt, :], x[:, kt, :], vecs[:, gain + kt:gain + kt + 1], n_rs, ALU.mult,
                                                     ALU.mult)
                    ins.then_inc(sem("s_hf"), 1)

                def lowered(q):
                    dve.wait_ge(sem("s_hhi"), 4 * n + q + 1)
                    lower(h_lo[:, 4 * q:4 * q + 4, :], h_hi[:, 4 * q:4 * q + 4, :], hf[:, 4 * q:4 * q + 4, :], sem("s_hlo"))

                scaled(0)
                scaled(1)
                if last:
                    scaled(2)
                    scaled(3)
                    return
                lowered(0)
                lowered(1)
                scaled(2)
                scaled(3)
                lowered(2)
                lowered(3)

            def bc(ap, n):
                return ap.unsqueeze(1).broadcast_to([P, n, ap.shape[-1]])

            for sub in range(RING):
                split(sub)
            dve.wait_ge(sem("s_vecs"), 16)
            for q in range(4):
                dve.wait_ge(s_x[q], 16)
            norm(0, VEC["g_mix"])
            dve.wait_ge(sem("s_hlo"), 4)
            for j in range(4):
                ahead(U_PRO + j)
            dve.wait_ge(s_load, 16 * LOADS)
            dve.wait_ge(sem("s_ix_rot"), 1)
            V.tensor_tensor(t_1, kraw, con("cos_i"), ALU.mult)
            link(V.tensor_tensor(t_2, pm[:, 0, 0:S], con("sin_i"), ALU.mult))
            link(V.tensor_tensor(krope, t_1, t_2, ALU.add))
            dve.wait_ge(sem("s_ix_wT"), 1)
            V.tensor_scalar(wtok, pm[:, 4, 0:S].rearrange("p (a b) -> p a b", a=NT)[:, :, 32:48],
                            float(IDX_H ** -0.5 * 64 ** -0.5), None, ALU.mult).then_inc(sem("s_ix_rope"), 1)
            dve.wait_ge(s_evac[2], 1)
            link(V.tensor_tensor(t_1, dwda[:, 0:S], dwda[:, 1:S + 1], ALU.subtract))
            V.scalar_tensor_tensor(t_2, t_1, vec("mu_dwda"), dwda[:, 1:S + 1], ALU.mult,
                                   ALU.add).then_inc(sem("s_lora_mix"), 1)
            dve.wait_ge(s_evac[0], 2)
            dve.wait_ge(sem("s_lora_mix"), 1)
            link(V.tensor_tensor(t_1, dg1[:, 0:S], dg1[:, 1:S + 1], ALU.subtract))
            V.scalar_tensor_tensor(mixd, t_1, vec("mu_dg1"), dg1[:, 1:S + 1], ALU.mult,
                                   ALU.add).then_inc(sem("s_lora_mix"), 1)
            dve.wait_ge(sem("s_lora_mix"), 2)
            link(V.tensor_tensor(t_1, misc[:, 0:S], misc[:, 1:S + 1], ALU.subtract))
            V.scalar_tensor_tensor(sig2, t_1, vec("mu_dg2"), misc[:, 1:S + 1], ALU.mult,
                                   ALU.add).then_inc(sem("s_lora_mix"), 1)
            dve.wait_ge(sem("s_lora_mix"), 3)
            dve.wait_ge(sem("s_lora_in"), 2)
            def rope(b):
                dve.wait_ge(sem("s_ix_rot"), b + 2)
                V.tensor_tensor(t_1, qraw[:, b % 2, :], con("cos_i"), ALU.mult)
                link(V.tensor_tensor(t_2, pm[:, 0, 0:S], con("sin_i"), ALU.mult))
                V.tensor_tensor(qrope[:, b % 2, :], t_1, t_2, ALU.add).then_inc(sem("s_ix_rope"), 1)
                dve.wait_ge(sem("s_ix_rope"), b + 2)

            def weigh(b):
                for hd in range(2):
                    dve.wait_ge(sem("s_ix_relu"), 2 * b + hd + 1)
                    if b or hd:
                        dve.wait_ge(sem("s_ix_acc"), 2 * b + hd)
                    for qt in range(NT):
                        r = relu[:, hd, qt * S:(qt + 1) * S]
                        w = wtok[:, qt, 2 * b + hd:2 * b + hd + 1]
                        if b == 0 and hd == 0:
                            ins = V.tensor_scalar(isc[:, qt, :], r, w, None, ALU.mult)
                        else:
                            ins = V.scalar_tensor_tensor(isc[:, qt, :], r, w, isc[:, qt, :], ALU.mult, ALU.add)
                    ins.then_inc(sem("s_ix_acc"), 1)

            for b in range(IDX_H // 2 + 1):
                split(2 * (U_PRO + 4 + b) + RING)
                if b:
                    rope(b - 1)
                split(2 * (U_PRO + 4 + b) + RING + 1)
                if b:
                    weigh(b - 1)
            dve.wait_ge(sem("s_ix_acc"), IDX_H)
            V.memset(isc[0:64, 0, 64:S], NEG)
            V.memset(isc[64:P, 0, P:S], NEG)
            link(V.memset(isc[0:64, 1, 192:S], NEG))
            for r in range(TOPK // 8):
                if r < 4:
                    ahead(U_RW0 + 1 + r)
                elif r == 4:
                    split(2 * (U_RW0 + 1 + r) + RING)
                V.max(top8[:, 0, :], isc[:, 0, :])
                link(V.max(top8[:, 1, :], isc[:, 1, :]))
                V.match_replace(isc[:, 0, :], top8[:, 0, :], isc[:, 0, :], MARK)
                link(V.match_replace(isc[:, 1, :], top8[:, 1, :], isc[:, 1, :], MARK))
            V.tensor_scalar(notsel, isc, MARK, BIG, ALU.not_equal, ALU.mult).then_inc(s_y, 1)
            dve.wait_ge(s_y, Y_T1)

            def feed1(n, i, last):
                if not last:
                    feed(n, i, U_T1, 6)

            def dsa(lv, i):
                if lv == 1:
                    dve.wait_ge(sem("s_at_rot"), i + 1)
                    V.tensor_tensor(d_t1, d_qn, bc(con("cos_q"), 2), ALU.mult)
                    link(V.tensor_tensor(d_t2, pm[:, 3, :].rearrange("p (a b) -> p a b", a=2), bc(con("sin_q"), 2), ALU.mult))
                    V.tensor_tensor(d_qk, d_t1, d_t2, ALU.add).then_inc(sem("s_at_qk"), 1)
                    dve.wait_ge(sem("s_at_vT"), i + 1)
                    V.tensor_copy(d_v.rearrange("p a b -> p (a b)"), pm[:, 4, 0:S]).then_inc(sem("s_at_v"), 1)
                if lv == 3:
                    dve.wait_ge(sem("s_ds_sc"), i + 1)
                    link(V.scalar_tensor_tensor(d_lg.rearrange("p a b -> p (a b)"), pm[:, 4, :], float(P ** -0.5),
                                                notsel.rearrange("p a b -> p (a b)"), ALU.mult, ALU.subtract))
                    V.reduce_max(d_nm, d_lg, AX, negate=True).then_inc(sem("s_at_nm"), 1)
                if lv == 5:
                    dve.wait_ge(sem("s_ds_ex"), NT * i + NT)
                    link(V.reciprocal(d_sum, d_sum))
                    for qt in range(NT):
                        ins = V.tensor_scalar(d_pr[:, qt, :], d_pr[:, qt, :], d_sum[:, qt:qt + 1], None, ALU.mult)
                    ins.then_inc(sem("s_at_pr"), 1)
                if lv == 6:
                    dve.wait_ge(s_yhi, Y_T1 + 2 * i)
                    lower(y_lo[:, i, :], y_hi[:, i, :], pm[:, 4, 0:S], s_y)

            def solver(Al, X, Y, it, between, after=None):
                dve.wait_ge(s_t1, 7 * it + 1)
                V.tensor_tensor(Y, pm[:, 0, :].rearrange("p (a b) -> p a b", a=4), bc(ident, 4), ALU.add).then_inc(s_sy, 1)
                V.tensor_tensor(X, Al[0], bc(ident, 4), ALU.add).then_inc(s_sx, 1)
                for lv in range(1, 7):
                    between(lv)
                    dve.wait_ge(s_sy, 7 * it + lv)
                    dve.wait_ge(s_dy, 6 * it + lv)
                    V.tensor_tensor(Y, Y, pm[:, 1, :].rearrange("p (a b) -> p a b", a=4), ALU.add).then_inc(s_sy, 1)
                    if lv < 6:
                        dve.wait_ge(s_sx, 6 * it + lv)
                        dve.wait_ge(s_dx, 5 * it + lv)
                        V.tensor_tensor(X, X, pm[:, 2, :].rearrange("p (a b) -> p a b", a=4), ALU.add).then_inc(s_sx, 1)
                    if after is not None:
                        after(lv)

            def rwkv(p, last=False):
                for j in range(3):
                    dve.wait_ge(s_evac[j], EV_RW0[j] + 1 + 2 * p)
                link(V.tensor_tensor(r_D, r_raw[:, :, 0:S], r_raw[:, :, 1:S + 1], ALU.subtract))
                for j in range(3):
                    ins = V.scalar_tensor_tensor(r_mix[:, j, :], r_D[:, j, :], vec("mu", p + 8 * j), r_raw[:, j, 1:S + 1],
                                                 ALU.mult, ALU.add)
                link(ins)
                kk, kp, rk = r_D[:, 0, :], r_D[:, 1, :], r_D[:, 2, :]
                link(V.tensor_scalar(kk, r_mix[:, 1, :], vec("k_k", p), None, ALU.mult))
                V.tensor_tensor(r_sq, kk, kk, ALU.mult).then_inc(sem("s_rw_kk2"), 1)
                dve.wait_ge(sem("s_rw_sig"), p + 1)
                link(V.tensor_scalar(r_lw, r_lw, -float(np.exp(-0.5)), None, ALU.mult))
                for c in range(NT):
                    ins = V.tensor_tensor_scan(r_cum[:, c * P:(c + 1) * P], ones[:, :], r_lw[:, c * P:(c + 1) * P], 0.0,
                                               ALU.mult, ALU.add)
                link(ins)
                mid = r_cum.rearrange("p (c t) -> p c t", c=NT)[:, :, P // 2 - 1:P // 2]
                link(V.tensor_scalar(r_negm.unsqueeze(2), mid, -1.0, None, ALU.mult))
                for c in range(NT):
                    ins = V.tensor_scalar(r_cum[:, c * P:(c + 1) * P], r_cum[:, c * P:(c + 1) * P], r_negm[:, c:c + 1], None,
                                          ALU.add)
                link(ins)
                V.tensor_tensor(r_lw, r_cum, r_lw, ALU.subtract).then_inc(sem("s_rw_cc"), 1)
                link(V.tensor_scalar(kp, r_a, -1.0, vec("k_a", p), ALU.add, ALU.mult))
                link(V.scalar_tensor_tensor(kp, kp, 1.0, r_mix[:, 1, :], ALU.add, ALU.mult))
                V.scalar_tensor_tensor(rk, r_mix[:, 0, :], vec("r_k", p), kp, ALU.mult, ALU.mult)
                dve.wait_ge(sem("s_rw_nrm"), p + 1)
                link(V.tensor_scalar(r_tmp, r_tmp, 1e-12, None, ALU.max))
                link(V.reciprocal(r_tmp, r_tmp))
                link(V.tensor_tensor(kk, kk, r_tmp, ALU.mult))
                dve.wait_ge(sem("s_rw_exp"), p + 1)
                V.scalar_tensor_tensor(r_at, kk, -1.0, r_lw, ALU.mult, ALU.mult)
                link(V.tensor_tensor(r_tmp, kk, r_a, ALU.mult))
                V.tensor_tensor(r_bt, r_tmp, r_Pi, ALU.mult)
                V.tensor_tensor(r_kt, kp, r_Pi, ALU.mult)
                V.tensor_tensor(r_sc, r_P[:, P - 1:P], r_em[:, 1:2], ALU.mult)
                V.tensor_tensor(r_rt, r_mix[:, 0, :], r_P, ALU.mult).then_inc(sem("s_rw_ops"), 1)
                dve.wait_ge(sem("s_qk_ss"), p + 1)
                link(V.tensor_scalar(d_rs, pm[:, 4, :], 1.0 / P, EPS, ALU.mult, ALU.add))
                V.reciprocal(d_rs, d_rs).then_inc(sem("s_qk_rv"), 1)
                dve.wait_ge(sem("s_rw_A"), p + 1)
                for hd in range(2):
                    ins = V.tensor_tensor(r_Aak[:, 2 * hd:2 * hd + 2, :], pm[:, hd, S:2 * S].rearrange("p (a b) -> p a b", a=2),
                                          bc(con("strict"), 2), ALU.mult)
                ins.then_inc(sem("s_rw_R"), 1)
                for hd in range(2):
                    dve.wait_ge(sem("s_rw_mR"), 2 * p + hd + 1)
                    ins = V.tensor_tensor(r_R[:, hd, :, :], pm[:, (2, 4)[hd], :].rearrange("p (a b) -> p a b", a=4),
                                          bc(con("incl"), 4), ALU.mult)
                ins.then_inc(sem("s_rw_R"), 1)
                dve.wait_ge(sem("s_qk_rs"), p + 1)
                V.scalar_tensor_tensor(d_qn[:, 0, :], d_raw[:, 0, :], vec("q_gain"), d_rs[:, 0:S], ALU.mult, ALU.mult)
                V.scalar_tensor_tensor(d_qn[:, 1, :], d_raw[:, 1, :], vec("k_gain"), d_rs[:, S:2 * S], ALU.mult,
                                       ALU.mult).then_inc(sem("s_ds_qn"), 1)
                if not last:
                    dve.wait_ge(s_lo, 2 * U_T1 + 7 + 12 * p)
                solver(r_Al, r_X, r_Y, p, lambda lv: feed1(5 + lv // 2, p, last) if lv % 2 else None, lambda lv: dsa(lv, p))
                dve.wait_ge(sem("s_rw_mS"), p + 1)
                for hd in range(2):
                    rows = slice(64 * hd, 64 * hd + 64)
                    ins = V.tensor_scalar(r_S[rows, rows], pm[rows, 0, rows], r_sc[rows, :], None, ALU.mult)
                ins.then_inc(sem("s_rw_S"), 1)
                y_, yc = r_X[:, 2:4, :].rearrange("p a b -> p (a b)"), r_Y[:, 0:2, :].rearrange("p a b -> p (a b)")
                dve.wait_ge(sem("s_rw_yTo"), p + 1)
                dve.wait_ge(sem("s_rw_mean"), p + 1)
                V.scalar_tensor_tensor(yc, pm[:, 3, 0:S], -1.0 / 64, y_, ALU.mult, ALU.add).then_inc(sem("s_rw_yc"), 1)
                V.tensor_tensor(rk, pm[:, 3, S:2 * S], r_mix[:, 2, :], ALU.mult)
                dve.wait_ge(sem("s_rw_var"), p + 1)
                link(V.tensor_scalar(r_tmp, pm[:, 4, 0:S], 1.0 / 64, GN_EPS, ALU.mult, ALU.add))
                V.reciprocal(r_tmp, r_tmp).then_inc(sem("s_ho_rv"), 1)
                dve.wait_ge(sem("s_ho_rs"), p + 1)
                link(V.scalar_tensor_tensor(r_sq, yc, vec("lnw", p), r_tmp, ALU.mult, ALU.mult))
                link(V.scalar_tensor_tensor(r_sq, r_sq, vec("lnb", p), rk, ALU.add, ALU.add))
                V.tensor_tensor(r_sq, r_sq, r_g, ALU.mult).then_inc(sem("s_yf"), 1)
                dve.wait_ge(s_yhi, Y_T1 + 2 * p + 1)
                lower(y_lo[:, p + DSA_H, :], y_hi[:, p + DSA_H, :], r_sq, s_y)

            dve.wait_ge(s_zero, 6)
            chain.loop(RWKV_P - 1, 20, rwkv)
            chain.turn(20, lambda i: rwkv(i, True), RWKV_P - 1)
            dve.wait_ge(s_lo, 2 * U_WOUT + 2)
            split(2 * U_WOUT + 2)

            def wout(i):
                for j in range(3):
                    ahead(U_WOUT + j, i, 3)
                    dve.wait_ge(s_sub, 2 * (U_WOUT + j) + 2 + 6 * i)
                    V.tensor_tensor(x[:, 3 * i + j, :], x[:, 3 * i + j, :], gp[:, j, 0:S], ALU.add).then_inc(s_evac[j], 1)

            loop(dve, 5, wout)
            ahead(U_WOUT + 15)
            dve.wait_ge(s_sub, 2 * (U_WOUT + 15) + 2)
            V.tensor_tensor(x[:, 15, :], x[:, 15, :], gp[:, 0, 0:S], ALU.add).then_inc(s_evac[0], 1)

            norm(1, VEC["g_ffn"])

            def top(w, m, keep, list_out):
                for tt in range(NT):
                    ins = V.max(m[:, tt, :], w[:, tt, :])
                link(ins)
                if list_out is not None:
                    V.tensor_copy(list_out, m[:, :, 0])
                link(V.memset(m8b, -1.0))
                link(V.tensor_copy(m8b[:, :, 0:keep], m[:, :, 0:keep]))
                for tt in range(NT):
                    ins = V.match_replace(w16b[:, tt, :], m8b[:, tt, :], w[:, tt, :], -2.0)
                link(ins)

            def softmax4(src, n):
                link(V.reduce_max(g1v, src, AX))
                V.tensor_tensor(g4, src, g1v.unsqueeze(2).broadcast_to([P, NT, 4]), ALU.subtract).then_inc(sem("s_rt_d"), 1)
                dve.wait_ge(sem("s_rt_e"), n + 1)
                ahead(U_MOE + n)
                link(V.reduce_sum(gs, e4, AX))
                link(V.reciprocal(gr, gs))
                link(V.tensor_tensor(w16[:, :, 0:4], e4, gr.unsqueeze(2).broadcast_to([P, NT, 4]), ALU.mult))

            for k in range(2):
                dve.sem_inc(sem(f"s_me_pair{k}"), 1)
                dve.sem_inc(sem(f"s_me_down{k}"), 1)
            dve.wait_ge(sem("s_rt_lg"), 1)
            V.memset(comb, 0.0)
            V.memset(w16, -1.0)
            link(V.tensor_tensor(rl, pm[:, 1, 0:64].rearrange("p (a b) -> p a b", a=NT)[:, :, 0:20], bc(rbias[:, :], NT),
                                 ALU.add))
            softmax4(rl[:, :, 0:4], 0)
            top(w16, m8, 1, pg)
            link(V.tensor_scalar(oneh, w16b[:, :, 0:4], -2.0, None, ALU.is_equal))
            for g in range(NGRP):
                o = es if g == 0 else es2
                link(V.tensor_tensor(o, rl[:, :, 4 + EPG * g:4 + EPG * (g + 1)], oneh[:, :, g:g + 1].broadcast_to([P, NT, EPG]),
                                     ALU.mult))
                if g:
                    link(V.tensor_tensor(es, es, es2, ALU.add))
            softmax4(es, 1)
            top(w16, m8, 2, None)
            link(V.tensor_scalar(w4, w16b[:, :, 0:4], -2.0, None, ALU.is_equal))
            link(V.tensor_tensor(w4, w4, w16[:, :, 0:4], ALU.mult))
            link(V.tensor_tensor(gs, m8[:, :, 0], m8[:, :, 1], ALU.add))
            link(V.reciprocal(gr, gs))
            link(V.tensor_tensor(w4, w4, gr.unsqueeze(2).broadcast_to([P, NT, 4]), ALU.mult))
            link(V.tensor_tensor(w4, w4, pg.unsqueeze(2).broadcast_to([P, NT, 4]), ALU.mult))
            for g in range(NGRP):
                ins = V.tensor_tensor(comb[:, :, EPG * g:EPG * (g + 1)], w4, oneh[:, :, g:g + 1].broadcast_to([P, NT, EPG]),
                                      ALU.mult)
            ins.then_inc(sem("s_rt_comb"), 1)

            def select(e):
                V.tensor_scalar(csel[0:16, :], combT[0:16, :], c0[0:16, bass.ds(C0["ident"][0] + e, 1)], None,
                                ALU.mult).then_inc(sem("s_me_sel"), 1)

            def weighted(b, u, e, step, n, bc_n):
                if not isinstance(n, int) or n:
                    ahead(u, e, step)
                    ahead(u + 1, e, step)
                dve.wait_ge(sem("s_me_sg"), n + 1)
                up = gp[:, 1, 0:S] if b % 2 == 0 else pm[:, 4, 0:S]
                V.tensor_tensor(hef[:, b % 2, :], sg[:, b % 2, :], up, ALU.mult).then_inc(sem(f"s_me_pair{b % 2}"), 1)
                dve.wait_ge(sem(f"s_me_pair{b % 2}"), bc_n)
                if b == 0:
                    dve.wait_ge(sem("s_me_bc"), bc_n // 2 if isinstance(bc_n, int) else e + 2)
                V.tensor_tensor(he2[:, b % 2, :], hef[:, b % 2, :], bce, ALU.mult).then_inc(sem("s_me_he2"), 1)

            def hidden(b, n):
                dve.wait_ge(sem("s_me_hhi"), n + 1)
                lower(y_lo[:, b, :], y_hi[:, b, :], he2[:, b % 2, :], sem("s_me_he"))

            def moe(e, last=False):
                for b in range(1, 4):
                    weighted(b, U_TM + 2 * (b - 1), e, 12, 4 * e + b, 2 * e + b // 2 + 2)
                    hidden(b, 4 * e + b)
                if not last:
                    select(e + 1)
                    weighted(0, U_TM + 6, e, 12, 4 * e + 4, 2 * e + 4)
                for d in range(4):
                    u = U_TM + (6 if last else 8) + d
                    ahead(u, e, 12)
                    dve.wait_ge(s_sub, 2 * u + 2 + 24 * e)
                    xs = x[:, 4 * d:4 * d + 4, :]
                    V.tensor_tensor(xs, xs, pm[:, 2 * (d % 2):2 * (d % 2) + 2, :].rearrange("p a (b c) -> p (a b) c", b=2),
                                    ALU.add).then_inc(sem(f"s_me_down{d % 2}"), 1)
                if not last:
                    hidden(0, 4 * e + 4)

            dve.wait_ge(sem("s_rt_cTo"), 1)
            select(0)
            weighted(0, U_MOE, 0, 0, 0, 2)
            hidden(0, 0)
            loop(dve, NEXP - 1, moe)
            moe(NEXP - 1, True)

            norm(2, VEC["norm2"])
            dve.wait_ge(sem("s_hlo"), 12)
            ahead(U_AB)
            dve.wait_ge(s_evac[0], EV_DN0[0])
            ahead(U_DN0)
            link(V.tensor_scalar(g_x[0:16, :], ab[0:16, :], vecs[0:16, VEC["dt_bias"]:VEC["dt_bias"] + 1], None, ALU.add))
            V.scalar_tensor_tensor(g_e[0:16, :], g_x[0:16, :], -1.0, g_x[0:16, :], ALU.mult, ALU.min).then_inc(sem("s_ab_x"), 1)
            dve.wait_ge(sem("s_ab_ln"), 1)
            link(V.scalar_tensor_tensor(g_s[0:16, :], g_x[0:16, :], 0.0, g_s[0:16, :], ALU.max, ALU.add))
            link(V.tensor_scalar(g_s[0:16, :], g_s[0:16, :], ea[0:16, :], -1.0, ALU.mult, ALU.mult))
            dve.wait_ge(s_zero, 7)
            for c in range(NT):
                ins = V.tensor_tensor_scan(gb[0:16, c * P:(c + 1) * P], ones[0:16, :], g_s[0:16, c * P:(c + 1) * P], 0.0,
                                           ALU.mult, ALU.add)
            link(ins)
            V.tensor_scalar(g_x[0:16, 0:P], gb[0:16, 0:P], -1.0, gb[0:16, P - 1:P], ALU.mult,
                            ALU.add).then_inc(sem("s_ab_cum"), 1)

            for j in range(1, 6):
                if j < 5:
                    ahead(U_DN0 + j)
                else:
                    split(2 * (U_DN0 + j) + RING)
            dve.wait_ge(sem("s_ab_T"), 1)
            V.tensor_copy(gtok, pm[:, 0, 0:S].rearrange("p (a b) -> p a b", a=NT)).then_inc(sem("s_ab_tokg"), 1)
            dve.wait_ge(sem("s_ab_tokg"), 1)
            V.tensor_scalar(nbeta, gtok[:, :, 32:48], -1.0, None, ALU.mult)
            dve.wait_ge(sem("s_ab_eg"), 1)
            V.tensor_scalar(neg_eg, egt, -1.0, None, ALU.mult).then_inc(sem("s_ab_tok"), 1)
            dve.wait_ge(sem("s_ab_tok"), 1)

            def feed2(n, i):
                feed(n, i, U_T2, 12)

            def delta(i, last=False):
                for v in range(2):
                    ins = V.tensor_scalar(n_gs[0:16, v, :], gb[0:16, :], c0[0:16, bass.ds(C0["ident"][0] + v + 2 * i, 1)], None,
                                          ALU.mult)
                ins.then_inc(sem("s_dn_gs"), 1)
                for k in range(3):
                    dve.wait_ge(s_evac[k], EV_DN0[k] + 4 * i + (2, 1, 1)[k])
                for tap in range(4):
                    for j in range(4):
                        w = vec("dn_conv", 16 * i + 4 * j + tap)
                        src = n_raw[:, j, tap:tap + S]
                        if tap == 0:
                            ins = V.tensor_scalar(n_qkv[:, j, :], src, w, None, ALU.mult)
                        else:
                            ins = V.scalar_tensor_tensor(n_qkv[:, j, :], src, w, n_qkv[:, j, :], ALU.mult, ALU.add)
                    if tap < 3:
                        link(ins)
                ins.then_inc(sem("s_dn_cv"), 1)
                dve.wait_ge(sem("s_dn_gb"), i + 1)
                for v in range(2):
                    for c in range(NT):
                        k = 2 * v + c
                        g = gtok[:, c, bass.ds(v + 2 * i, 1)]
                        V.tensor_scalar(n_E1[:, k, :], pm[:, 4, v * S + c * P:v * S + (c + 1) * P], g, 0.0, ALU.subtract, ALU.max)
                        ins = V.tensor_scalar(n_E2[:, k, :], pm[:, 4, v * S + c * P:v * S + (c + 1) * P], g, 0.0, ALU.subtract,
                                              ALU.min)
                ins.then_inc(sem("s_dn_D"), 1)
                dve.wait_ge(sem("s_qk_ss"), DSA_H + i + 1)
                link(V.tensor_scalar(n_rn, pm[:, 0, :], EPS, None, ALU.add))
                V.reciprocal(n_rn, n_rn).then_inc(sem("s_qk_rv"), 1)
                dve.wait_ge(sem("s_qk_rs"), DSA_H + i + 1)
                V.scalar_tensor_tensor(n_qkv[:, 0, :], n_qkv[:, 0, :], float(P ** -0.5), n_rn[:, 0:S], ALU.mult, ALU.mult)
                V.tensor_tensor(n_qkv[:, 1, :], n_qkv[:, 1, :], n_rn[:, S:2 * S], ALU.mult).then_inc(sem("s_dn_qk"), 1)
                dve.wait_ge(sem("s_dn_kk"), i + 1)
                dve.wait_ge(sem("s_dn_E1"), i + 1)
                for v in range(2):
                    for c in range(NT):
                        ins = V.scalar_tensor_tensor(n_A[:, 2 * v + c, :], pm[:, 3, c * P:(c + 1) * P],
                                                     nbeta[:, c, bass.ds(v + 2 * i, 1)], n_E1[:, 2 * v + c, :], ALU.mult, ALU.mult)
                ins.then_inc(sem("s_dn_A"), 1)
                dve.wait_ge(s_lo, 2 * U_T2 + 9 + 24 * i)
                feed2(7, i)
                dve.wait_ge(sem("s_dn_E2"), i + 1)
                for v in range(2):
                    ins = V.tensor_tensor(n_QK[:, 2 * v:2 * v + 2, :], pm[:, 3, S:2 * S].rearrange("p (a b) -> p a b", a=2),
                                          n_E2[:, 2 * v:2 * v + 2, :], ALU.mult)
                ins.then_inc(sem("s_dn_QK"), 1)
                dve.wait_ge(sem("s_dn_kT"), i + 1)
                dve.wait_ge(sem("s_dn_v"), i + 1)
                for v in range(2):
                    V.tensor_scalar(n_r0[:, v, :], n_v[:, 2 * v, :], gtok[:, 0, bass.ds(32 + v + 2 * i, 1)], None, ALU.mult)
                    ins = V.tensor_scalar(n_kd[:, v, :], pm[:, 2, 0:P], gtok[:, 0, bass.ds(64 + v + 2 * i, 1)], None, ALU.mult)
                ins.then_inc(sem("s_dn_kd"), 1)
                feed2(8, i)
                solver(n_Al, n_X, n_Y, i + RWKV_P, lambda lv: feed2(9 + lv // 2, i) if lv % 2 else None)
                dve.wait_ge(sem("s_dn_mks"), i + 1)
                for v in range(2):
                    ins = V.scalar_tensor_tensor(n_r1[:, v, :], pm[:, 3, v * P:(v + 1) * P], neg_eg[:, 1, bass.ds(v + 2 * i, 1)],
                                                 n_v[:, 2 * v + 1, :], ALU.mult, ALU.add)
                link(ins)
                for v in range(2):
                    ins = V.tensor_scalar(n_r1[:, v, :], n_r1[:, v, :], gtok[:, 1, bass.ds(32 + v + 2 * i, 1)], None, ALU.mult)
                ins.then_inc(sem("s_dn_r1"), 1)
                dve.wait_ge(sem("s_dn_o"), i + 1)
                for v in range(2):
                    ins = V.scalar_tensor_tensor(n_o[:, 2 + v, :], pm[:, 3, S + v * P:S + (v + 1) * P],
                                                 egt[:, 1, bass.ds(v + 2 * i, 1)], n_o[:, 2 + v, :], ALU.mult, ALU.add)
                ins.then_inc(sem("s_dn_ot"), 1)
                dve.wait_ge(sem("s_dn_os"), i + 1)
                link(V.tensor_scalar(n_or, n_ss, 1.0 / P, EPS, ALU.mult, ALU.add))
                V.reciprocal(n_or, n_or).then_inc(sem("s_ho_rv"), 1)
                dve.wait_ge(sem("s_ho_rs"), RWKV_P + i + 1)
                for k in range(4):
                    ins = V.tensor_scalar(n_o[:, k, :], n_o[:, k, :], n_or[:, k:k + 1], None, ALU.mult)
                ins.then_inc(sem("s_dn_on"), 1)
                dve.wait_ge(sem("s_dn_z"), i + 1)
                dve.wait_ge(sem("s_dn_oT"), i + 1)
                V.scalar_tensor_tensor(n_yf, pm[:, 4, :].rearrange("p (a b) -> p a b", a=2), vec("dn_norm"), n_z, ALU.mult,
                                       ALU.mult).then_inc(sem("s_yf"), 1)
                dve.wait_ge(s_yhi, Y_T2 + 2 * i)
                lower(y_lo[:, bass.ds(2 * i, 2), :], y_hi[:, bass.ds(2 * i, 2), :], n_yf, s_y)

            def swa(i, last=False):
                for k in range(3):
                    dve.wait_ge(s_evac[k], EV_T2[k] + 4 * i + 2)
                dve.wait_ge(sem("s_at_rot"), DSA_H + i + 1)
                V.tensor_tensor(w_t1, w_raw, bc(con("cos_w"), 4), ALU.mult)
                link(V.tensor_tensor(w_t2, pm[:, 0:2, :].rearrange("p n (a b) -> p (n a) b", a=2), bc(con("sin_w"), 4), ALU.mult))
                V.tensor_tensor(w_qk, w_t1, w_t2, ALU.add).then_inc(sem("s_at_qk"), 1)
                dve.wait_ge(sem("s_at_vT"), DSA_H + i + 1)
                V.tensor_copy(w_v.rearrange("p a b -> p (a b)"), pm[:, 4, 0:S]).then_inc(sem("s_at_v"), 1)
                dve.wait_ge(sem("s_sw_sc"), 2 * i + 1)
                V.scalar_tensor_tensor(w_l0, pm[:, 0, 0:3 * P], float(P ** -0.5), con("bias0"), ALU.mult, ALU.add)
                dve.wait_ge(sem("s_sw_sc"), 2 * i + 2)
                link(V.scalar_tensor_tensor(w_l1, pm[:, 1:3, :].rearrange("p a b -> p (a b)")[:, 0:3 * S], float(P ** -0.5),
                                            con("bias1"), ALU.mult, ALU.add))
                V.reduce_max(w_nm[:, 0:1], w_l0, AX, negate=True)
                V.reduce_max(w_nm[:, 1:2], w_l1, AX, negate=True).then_inc(sem("s_at_nm"), 1)
                dve.wait_ge(sem("s_sw_ex"), i + 1)
                V.tensor_tensor(w_p0, w_l0[:, 0:P], w_l0[:, P:2 * P], ALU.add)
                V.tensor_tensor(w_p1, w_l1[:, 0:S], w_l1[:, S:2 * S], ALU.add)
                link(V.reciprocal(w_sum, w_sum))
                V.tensor_tensor(w_p0, w_p0, w_l0[:, 2 * P:3 * P], ALU.add)
                link(V.tensor_tensor(w_p1, w_p1, w_l1[:, 2 * S:3 * S], ALU.add))
                V.tensor_scalar(w_p0, w_p0, w_sum[:, 0:1], None, ALU.mult)
                V.tensor_scalar(w_p1, w_p1, w_sum[:, 1:2], None, ALU.mult).then_inc(sem("s_at_pr"), 1)
                dve.wait_ge(sem("s_at_o"), DSA_H + i + 1)
                V.tensor_tensor(w_yf, w_z, pm[:, 0, 0:S], ALU.mult).then_inc(sem("s_yf"), 1)
                dve.wait_ge(s_yhi, Y_T2 + 2 * i + 1)
                lower(y_lo[:, i + 16, :], y_hi[:, i + 16, :], w_yf, s_y)

            def turn2(i, last=False):
                delta(i, last)
                swa(i, last)

            dve.wait_ge(s_zero, 8)
            chain.loop(DN_H - 1, 10, turn2)
            chain.turn(10, lambda i: turn2(i, True), DN_H - 1)
            split(2 * U_HOUT + 2)

            def project(u0):
                def turn(i):
                    for s_ in range(6):
                        split(2 * u0 + RING + s_, i, 6)
                        if s_ % 3 == 2:
                            b = s_ // 3
                            dve.wait_ge(s_sub, 2 * u0 + s_ + 1 + 6 * i)
                            V.tensor_tensor(x[:, 2 * i + b, :], x[:, 2 * i + b, :], gp[:, b, 0:S], ALU.add).then_inc(s_evac[b], 1)
                return turn

            loop(dve, 8, project(U_HOUT))

            norm(3, VEC["norm2"] + KT)
            dve.wait_ge(s_zero, 9)

            def shortconv(i):
                for n in range(12):
                    bb, j, k = n // 4, n % 4, n % 3
                    ahead(U_SC + n, i, 12)
                    if j == 2:
                        kc = (n - 1) % 3
                        dve.wait_ge(s_evac[kc], EV_SC[kc] + (n - 1) // 3 + 1 + 4 * i)
                        dve.wait_ge(s_sub, 2 * (U_SC + n) + 2 + 24 * i)
                        V.tensor_tensor(q_cu[:, bb, 2:S + 2], q_c[:, bb, :], gp[:, k, 0:S], ALU.mult).then_inc(s_evac[k], 1)
                    if j == 3:
                        ku = (n - 1) % 3
                        dve.wait_ge(s_evac[ku], EV_SC[ku] + (n - 1) // 3 + 1 + 4 * i)
                        w = 9 * i + 3 * bb
                        link(V.tensor_scalar(q_a[:, bb, :], q_cu[:, bb, 0:S], vec("sc_conv", w), None, ALU.mult))
                        for tap in (1, 2):
                            link(V.scalar_tensor_tensor(q_a[:, bb, :], q_cu[:, bb, tap:tap + S], vec("sc_conv", w + tap),
                                                        q_a[:, bb, :], ALU.mult, ALU.add))
                        link(V.tensor_tensor(q_a[:, bb, :], q_a[:, bb, :], q_b[:, bb, :], ALU.mult))
                        dve.wait_ge(s_evac[k], EV_SC[k] + n // 3 + 1 + 4 * i)
                        V.tensor_tensor(q_a[:, bb, :], q_a[:, bb, :], q_z[:, bb, :], ALU.mult).then_inc(sem("s_sc_y"), 1)
                        dve.wait_ge(s_yhi, Y_SC + bb + 3 * i)
                        lower(y_lo[:, 3 * i + bb, :], y_hi[:, 3 * i + bb, :], q_a[:, bb, :], s_y)

            chain.loop(8, 12, shortconv)
            out_turn = project(U_SOUT)
            loop(dve, 7, out_turn)
            out_turn(7)
            norm(4, VEC["final"], last=True)


def _constants():
    idx = np.arange(P)
    t, s = idx[:, None], idx[None, :]
    levels = [((t // (2 * b) == s // (2 * b)) & ((t // b) % 2 == 1) & ((s // b) % 2 == 0)) for b in (1, 2, 4, 8, 16, 32, 64)]
    c0 = {"ident": np.eye(P), "levels": np.concatenate(levels, 1), "incl": t <= s, "strict": t < s}

    def swap(size, half):
        m = np.zeros((P, P))
        for b in range(0, P, size):
            for k in range(half):
                m[b + half + k, b + k] = -1
                m[b + k, b + half + k] = 1
        return m

    def angles(theta, dim, half):
        inv = np.float32(theta) ** (-np.arange(half, dtype=np.float32) * np.float32(2.0 / dim))
        a = np.arange(S, dtype=np.float32)[None, :] * inv.astype(np.float32)[:, None]
        return np.cos(a), np.sin(a)

    cq, sq = angles(10000.0, 128, 64)
    ci, si = angles(10000.0, 64, 32)
    cw, sw = angles(500000.0, 32, 16)
    c1 = {"heads": (t // 64) == (s // 64), "perm_q": swap(128, 64), "perm_i": swap(64, 32), "cos_q": np.tile(cq, (2, 1)),
          "sin_q": np.tile(sq, (2, 1)), "cos_i": np.tile(ci, (4, 1)), "sin_i": np.tile(si, (4, 1))}
    cos_w, sin_w = np.ones((P, S)), np.zeros((P, S))
    cos_w[0:32], sin_w[0:32] = np.tile(cw, (2, 1)), np.tile(sw, (2, 1))

    def window(q0, keys):
        d = (q0 + idx)[:, None] - np.arange(keys)[None, :]
        ok = [(d >= 0) & (d <= 128), (d >= 0) & (d % 4 == 0), (d >= 0) & (d % 16 == 0)]
        return np.concatenate([np.where(o, 0.0, -BIG) for o in ok], 1)

    c2 = {"perm_w": swap(128, 16), "cos_w": cos_w, "sin_w": sin_w, "bias0": window(0, P), "bias1": window(P, S)}

    def pack(values, order):
        return np.concatenate([np.asarray(values[n], np.float32) for n, _ in order], 1)

    return pack(c0, _C0), pack(c1, _C1), pack(c2, _C2)


def _blocks(w):
    k, n = w.shape
    return w.reshape(k // P, P, n // P, P).transpose(2, 1, 0, 3)


def _wide(*cols):
    w = np.concatenate(cols, 1)
    return np.concatenate([w, np.zeros((w.shape[0], P - w.shape[1]), w.dtype)], 1)


def _stream(a):
    out = np.empty((N_UNITS, P, UNIT * P), np.float32)
    w = a["w_in"][0]
    q, k, v, qi, ki, wi = np.split(w[:, :4176], np.cumsum([1024, 1024, 1024, 1024, 64]), 1)
    r, dw, kr, vr, da, dg = np.split(w[:, 4176:], np.cumsum([1024, 64, 1024, 1024, 64]), 1)

    def put(u, blocks, step=1):
        n = blocks.shape[0]
        out[u:u + step * (n - 1) + 1:step] = blocks.reshape(n, P, UNIT * P)

    put(U_PRO, _blocks(np.concatenate([_wide(ki, ki), _wide(dg[:, 128:], wi), _wide(dw, da), dg[:, :128], qi], 1)))
    for j, m in enumerate((r, kr, vr, q, k, v)):
        put(U_RW0 + j, _blocks(m), 6)
    put(U_WOUT, _blocks(a["w_out"][0]))
    for e in range(NEXP):
        u = U_TM + 12 * e
        for j, m in enumerate((a["w_e_gate"], a["w_e_up"])):
            b = _blocks(m[0, e])
            put(u - 6 + j if e else U_MOE + j, b[:1])
            put(u + j, b[1:], 2)
        d = _blocks(a["w_e_down"][0, e])
        u += 8 if e < NEXP - 1 else 6
        out[u:u + 4] = d.reshape(4, 4, P, 4 * P).transpose(0, 2, 1, 3).reshape(4, P, UNIT * P)
    w = a["hyb_w_in_2"][0]
    aq, ak, av, az, ab, aa, bq, bk, bv, bz = np.split(
        w, np.cumsum([1024, 1024, 2048, 2048, 16, 16, 3072, 1024, 1024]), 1)
    gap = np.zeros((D, 16), np.float32)
    put(U_AB, _blocks(_wide(aa, gap, ab)))
    bav, baz, bbq = _blocks(av), _blocks(az), _blocks(bq)
    for j, b in enumerate((_blocks(aq), _blocks(ak), bav[0::2], bav[1::2], baz[0::2], baz[1::2])):
        put(U_DN0 + j, b[:1])
        put(U_T2 + 6 + j, b[1:], 12)
    for j, b in enumerate((bbq[0:8], bbq[8:16], bbq[16:24], _blocks(bk), _blocks(bv), _blocks(bz))):
        put(U_T2 + j, b, 12)

    def tall(u, w):
        b = _blocks(w).transpose(0, 2, 1, 3).reshape(-1, UNIT, P, P)
        out[u:u + b.shape[0]] = b.transpose(0, 2, 1, 3).reshape(-1, P, UNIT * P)

    tall(U_HOUT, a["hyb_w_out_2"][0])
    for j, m in enumerate(np.split(a["sc_w_in_2"][0], 4, 1)):
        put(U_SC + j, _blocks(m), 4)
    tall(U_SOUT, a["sc_w_out_2"][0])
    return out


def _vectors(a):
    def cols(v):
        return np.reshape(v, (-1, P)).T

    def padded(v):
        return np.concatenate([v, np.zeros(P - v.size, np.float32)])[:, None]

    mu = a["rwkv_shift_mix"][0]
    dc = a["dn_conv_w_2"][0].reshape(32, P, 4)
    dn = np.concatenate([dc[b] for i in range(8) for b in (i, 8 + i, 16 + 2 * i, 17 + 2 * i)], 1)
    sc = a["sc_conv_w_2"][0].reshape(24, P, 3).transpose(1, 0, 2).reshape(P, 72)
    got = {
        "g_mix": cols(a["g_mix"][0]), "g_ffn": cols(a["g_ffn"][0]), "norm2": cols(a["norm_w_2"]), "final": cols(a["final_norm_w_2"]),
        "mu": np.concatenate([cols(mu[0:1024]), cols(mu[1088:2112]), cols(mu[2112:3136])], 1),
        "mu_dwda": np.concatenate([mu[1024:1088], mu[3136:3200]])[:, None], "mu_dg1": mu[3200:3328][:, None],
        "mu_dg2": padded(mu[3328:3360]), "w0": cols(a["w0"][0]), "a0": cols(a["a0"][0]), "k_k": cols(a["k_k"][0]),
        "k_a": cols(a["k_a"][0]), "r_k": cols(a["r_k"][0]), "lnw": cols(a["ln_x_w"][0]), "lnb": cols(a["ln_x_b"][0]),
        "q_gain": cols(a["q_gain"][0]), "k_gain": cols(a["k_gain"][0]), "dn_norm": cols(a["dn_norm_w_2"][0]),
        "dn_conv": dn, "sc_conv": sc, "a_log": padded(a["dn_a_log_2"][0]), "dt_bias": padded(a["dn_dt_bias_2"][0]),
    }
    return np.ascontiguousarray(np.concatenate([got[n] for n, _ in _VEC], 1))


def _lora(a):
    g = a["w_gate_lora_up"][0]
    wa = np.concatenate([a["w_decay_up"][0], a["w_aicl_up"][0]], 0)
    g2 = np.concatenate([g[128:], np.zeros((96, g.shape[1]), np.float32)], 0)
    return np.ascontiguousarray(np.stack([np.concatenate([m[:, P * p:P * (p + 1)] for m in (wa, g[:128], g2)], 1)
                                          for p in range(RWKV_P)]))


def _arrays(a):
    c0, c1, c2 = _constants()
    route = np.concatenate([a["w_route_group"][0], a["w_route_expert"][0]], 1).reshape(KT, P, 20).transpose(1, 0, 2)
    rb = np.concatenate([a["b_route_group"][0], a["b_route_expert"][0]])
    return {
        "stream": _stream(a), "x": np.ascontiguousarray(a["x"][0].T.reshape(KT, P, S).transpose(1, 0, 2)),
        "vecs": _vectors(a), "c0": c0, "c1": c1, "c2": c2, "lora": _lora(a), "route": np.ascontiguousarray(route),
        "rbias": np.ascontiguousarray(np.broadcast_to(rb, (P, 20))),
    }


def kernel(**inputs):
    import concourse.bacc as bacc
    from concourse.bass_utils import run_bass_kernel_spmd

    nc = bacc.Bacc("TRN2", target_bir_lowering=False, num_devices=1)
    arrays, args = {}, []
    for name, v in _arrays({k: np.asarray(v) for k, v in inputs.items()}).items():
        arrays[f"in_{name}"] = v
        args.append(nc.dram_tensor(f"in_{name}", v.shape, mybir.dt.from_np(v.dtype), kind="ExternalInput").ap())
    out = nc.dram_tensor("out_0", (P, KT, S), F32, kind="ExternalOutput").ap()
    program(nc, *args, out)
    got = run_bass_kernel_spmd(nc, [arrays], core_ids=[0]).results[0]["out_0"]
    return np.ascontiguousarray(got.transpose(1, 0, 2).reshape(D, S).T)[None]
```
